# Optimizing a Trainium2 kernel written in Bass

```python
import math
import jax, jax.numpy as jnp
from jax import lax
import numpy as np

D_MODEL = 1024
BATCH = 1
SEQ = 256
DEPTH = 2

CHUNK = 64
Q_BLOCK = 128
N_MIXERS = 2
ATTN_HEADS = 8
ATTN_HEAD_DIM = 64
ATTN_WIDTH = ATTN_HEADS * 2 * ATTN_HEAD_DIM
ROPE_DIM = ATTN_HEAD_DIM // 4
ROPE_THETA = 500000.0
CONV_WIDTH = 3
CONV_CH = D_MODEL
D_FF = -(-8 * D_MODEL // (3 * 256)) * 256
ALPHA = (2 * DEPTH) ** 0.25
BETA = (8 * DEPTH) ** -0.25
N_ATTN_LAYERS = (DEPTH + 1) // 2
N_CONV_LAYERS = DEPTH // 2
LN_EPS = 1e-5
NEG_INF = -1e30


def layer_norm(x, g, b):
    xf = x.astype(jnp.float32)
    mu = jnp.mean(xf, axis=-1, keepdims=True)
    xc = xf - mu
    var = jnp.mean(xc * xc, axis=-1, keepdims=True)
    y = xc * lax.rsqrt(var + LN_EPS) * g.astype(jnp.float32) + b.astype(jnp.float32)
    return y.astype(x.dtype)

def rms_norm(x, g):
    xf = x.astype(jnp.float32)
    y = xf * lax.rsqrt(jnp.mean(xf * xf, axis=-1, keepdims=True) + LN_EPS) * g.astype(jnp.float32)
    return y.astype(x.dtype)

def rope_tables(seq):
    pos = jnp.arange(seq, dtype=jnp.float32)
    inv = ROPE_THETA ** (-jnp.arange(0, ROPE_DIM, 2, dtype=jnp.float32) / ROPE_DIM)
    ang = pos[:, None] * inv[None, :]
    return jnp.cos(ang), jnp.sin(ang)

def partial_rotary(x, cos, sin):
    half = ROPE_DIM // 2
    c = cos[None, :, None, None, :].astype(x.dtype)
    s = sin[None, :, None, None, :].astype(x.dtype)
    x1 = x[..., :half]
    x2 = x[..., half:ROPE_DIM]
    rot = jnp.concatenate([x1 * c - x2 * s, x2 * c + x1 * s], axis=-1)
    return jnp.concatenate([rot, x[..., ROPE_DIM:]], axis=-1)

def lambda_init_fn(layer_idx):
    return 0.8 - 0.6 * math.exp(-0.3 * layer_idx)

def diff_attention(x, w_qkv, w_o, lq1, lk1, lq2, lk2, g_sub, lam_init):
    B, S, _ = x.shape
    H, Dh = ATTN_HEADS, ATTN_HEAD_DIM
    qkv = jnp.einsum('bsd,de->bse', x, w_qkv)
    q = qkv[..., :ATTN_WIDTH].reshape(B, S, H, 2, Dh)
    k = qkv[..., ATTN_WIDTH:2 * ATTN_WIDTH].reshape(B, S, H, 2, Dh)
    v = qkv[..., 2 * ATTN_WIDTH:].reshape(B, S, H, 2 * Dh)
    cos, sin = rope_tables(S)
    q = partial_rotary(q, cos, sin) * (Dh ** -0.5)
    k = partial_rotary(k, cos, sin)
    f32 = jnp.float32
    lam = (jnp.exp(jnp.sum(lq1.astype(f32) * lk1.astype(f32)))
           - jnp.exp(jnp.sum(lq2.astype(f32) * lk2.astype(f32))) + lam_init)
    nb = S // Q_BLOCK
    q_blocks = jnp.moveaxis(q.reshape(B, nb, Q_BLOCK, H, 2, Dh), 1, 0)
    key_chunk = jnp.arange(S) // CHUNK

    def one_block(args):
        q_blk, bi = args
        s = jnp.einsum('bqhcd,bkhcd->bhcqk', q_blk, k).astype(f32)
        q_chunk = (bi * Q_BLOCK + jnp.arange(Q_BLOCK)) // CHUNK
        mask = key_chunk[None, :] <= q_chunk[:, None]
        s = jnp.where(mask, s, NEG_INF)
        p = jax.nn.softmax(s, axis=-1)
        a = p[:, :, 0] - lam * p[:, :, 1]
        return jnp.einsum('bhqk,bkhe->bqhe', a.astype(v.dtype), v)

    o = lax.map(one_block, (q_blocks, jnp.arange(nb)))
    o = jnp.moveaxis(o, 0, 1).reshape(B, S, H, 2 * Dh)
    o = rms_norm(o, g_sub) * (1.0 - lam_init)
    return jnp.einsum('bse,ed->bsd', o.reshape(B, S, ATTN_WIDTH), w_o)

def short_gated_conv(x, w_in, w_conv, w_out):
    bcx = jnp.einsum('bsd,de->bse', x, w_in)
    b_gate = bcx[..., :CONV_CH]
    c_gate = bcx[..., CONV_CH:2 * CONV_CH]
    xt = bcx[..., 2 * CONV_CH:]
    u = c_gate * xt
    y = lax.conv_general_dilated(
        u, w_conv[:, None, :], window_strides=(1,),
        padding=[(CONV_WIDTH - 1, 0)],
        dimension_numbers=('NWC', 'WIO', 'NWC'),
        feature_group_count=CONV_CH)
    return jnp.einsum('bsc,cd->bsd', b_gate * y, w_out)

def swiglu(x, w_gate, w_up, w_down):
    h = jax.nn.silu(jnp.einsum('bsd,df->bsf', x, w_gate)) * jnp.einsum('bsd,df->bsf', x, w_up)
    return jnp.einsum('bsf,fd->bsd', h, w_down)

def first_inputs(seed: int = 0) -> dict:
    key = jax.random.key(seed)
    ks = jax.random.split(key, 18)
    f32 = jnp.float32

    def nrm(k, shape, scale):
        return jax.random.normal(k, shape, f32) * scale

    NA, NC, Dh = N_ATTN_LAYERS, N_CONV_LAYERS, ATTN_HEAD_DIM
    return {
        'x': nrm(ks[0], (BATCH, SEQ, D_MODEL), 1.0),
        'attn_w_qkv': nrm(ks[1], (NA, D_MODEL, 3 * ATTN_WIDTH), D_MODEL ** -0.5),
        'attn_w_o': nrm(ks[2], (NA, ATTN_WIDTH, D_MODEL), ATTN_WIDTH ** -0.5 * BETA),
        'attn_lambda_q1': nrm(ks[3], (NA, Dh), 0.1),
        'attn_lambda_k1': nrm(ks[4], (NA, Dh), 0.1),
        'attn_lambda_q2': nrm(ks[5], (NA, Dh), 0.1),
        'attn_lambda_k2': nrm(ks[6], (NA, Dh), 0.1),
        'attn_subln_g': 1.0 + nrm(ks[7], (NA, 2 * Dh), 0.02),
        'conv_w_in': nrm(ks[8], (NC, D_MODEL, 3 * CONV_CH), D_MODEL ** -0.5),
        'conv_w': nrm(ks[9], (NC, CONV_WIDTH, CONV_CH), CONV_WIDTH ** -0.5),
        'conv_w_out': nrm(ks[10], (NC, CONV_CH, D_MODEL), CONV_CH ** -0.5 * BETA),
        'ffn_w_gate': nrm(ks[11], (DEPTH, D_MODEL, D_FF), D_MODEL ** -0.5),
        'ffn_w_up': nrm(ks[12], (DEPTH, D_MODEL, D_FF), D_MODEL ** -0.5),
        'ffn_w_down': nrm(ks[13], (DEPTH, D_FF, D_MODEL), D_FF ** -0.5 * BETA),
        'ln1_g': 1.0 + nrm(ks[14], (DEPTH, D_MODEL), 0.02),
        'ln1_b': nrm(ks[15], (DEPTH, D_MODEL), 0.02),
        'ln2_g': 1.0 + nrm(ks[16], (DEPTH, D_MODEL), 0.02),
        'ln2_b': nrm(ks[17], (DEPTH, D_MODEL), 0.02),
    }

def first_block(x, attn_w_qkv, attn_w_o, attn_lambda_q1, attn_lambda_k1, attn_lambda_q2,
              attn_lambda_k2, attn_subln_g, conv_w_in, conv_w, conv_w_out,
              ffn_w_gate, ffn_w_up, ffn_w_down, ln1_g, ln1_b, ln2_g, ln2_b):
    h = x
    for i in range(DEPTH):
        j = i // N_MIXERS
        if i % N_MIXERS == 0:
            m = diff_attention(h, attn_w_qkv[j], attn_w_o[j], attn_lambda_q1[j],
                               attn_lambda_k1[j], attn_lambda_q2[j], attn_lambda_k2[j],
                               attn_subln_g[j], lambda_init_fn(i))
        else:
            m = short_gated_conv(h, conv_w_in[j], conv_w[j], conv_w_out[j])
        h = layer_norm(ALPHA * h + m, ln1_g[i], ln1_b[i])
        h = layer_norm(ALPHA * h + swiglu(h, ffn_w_gate[i], ffn_w_up[i], ffn_w_down[i]),
                       ln2_g[i], ln2_b[i])
    return h


DEPTH_2 = 1

MIX_WIDTH = D_MODEL
N_MLSTM_HEADS = 4
MLSTM_HEAD_DIM = 128
MLSTM_WIDTH = N_MLSTM_HEADS * MLSTM_HEAD_DIM
N_SB_HEADS = 8
SB_HEAD_DIM = 64
SB_WIDTH = N_SB_HEADS * SB_HEAD_DIM
CONV_WIDTH_2 = 4
MLSTM_CHUNK = 128
SB_BLOCK = 128
PROJ_WIDTH = 4 * MLSTM_WIDTH + 2 * N_MLSTM_HEADS + 3 * SB_WIDTH
PROJ_SPLITS = (2 * MLSTM_WIDTH, 3 * MLSTM_WIDTH, 4 * MLSTM_WIDTH,
               4 * MLSTM_WIDTH + N_MLSTM_HEADS, 4 * MLSTM_WIDTH + 2 * N_MLSTM_HEADS)
MEM_TOKENS = 256
N_XATTN_HEADS = 4
XATTN_HEAD_DIM = D_MODEL // N_XATTN_HEADS
PEER_HEADS = 8
PEER_N_KEYS = 128
PEER_N_EXPERTS = PEER_N_KEYS * PEER_N_KEYS
PEER_TOPK = 16
PEER_QUERY_DIM = 256
PEER_HALF = PEER_QUERY_DIM // 2
PEER_CHUNK = 128
EPS = 1e-6


def rms_norm_2(x, g):
    xf = x.astype(jnp.float32)
    y = xf * lax.rsqrt(jnp.mean(xf * xf, axis=-1, keepdims=True) + EPS) * g.astype(jnp.float32)
    return y.astype(x.dtype)

def head_rms_norm(a, g):
    H, dh = a.shape[1], a.shape[3]
    y = a * lax.rsqrt(jnp.mean(a * a, axis=-1, keepdims=True) + EPS)
    return y * g.astype(jnp.float32).reshape(H, 1, dh)

def split_heads(a, n):
    B_, S, W = a.shape
    return a.reshape(B_, S, n, W // n).transpose(0, 2, 1, 3)

def merge_heads(a):
    B_, H, S, dh = a.shape
    return a.transpose(0, 2, 1, 3).reshape(B_, S, H * dh)

def causal_depthwise_conv(a, w, b):
    C = a.shape[-1]
    out = lax.conv_general_dilated(a, w[:, None, :].astype(a.dtype), window_strides=(1,),
                                   padding=[(CONV_WIDTH_2 - 1, 0)],
                                   dimension_numbers=('NWC', 'WIO', 'NWC'),
                                   feature_group_count=C)
    return out + b.astype(a.dtype)

def mlstm_chunkwise(q, k, v, log_i, log_f):
    B_, H, S, dh = q.shape
    L = MLSTM_CHUNK
    nc = S // L

    def to_chunks(a):
        return jnp.moveaxis(a.reshape(B_, H, nc, L, *a.shape[3:]), 2, 0)

    xs = (to_chunks(q), to_chunks(k), to_chunks(v), to_chunks(log_i), to_chunks(log_f))
    causal = jnp.tril(jnp.ones((L, L), dtype=bool))

    def step(carry, inp):
        C, n, m = carry
        qb, kb, vb, ib, fb = inp
        b = jnp.cumsum(fb, axis=-1)
        g = b + m[..., None]
        Dm = jnp.where(causal, b[..., :, None] - b[..., None, :] + ib[..., None, :], -jnp.inf)
        m_t = jnp.maximum(g, jnp.max(Dm, axis=-1))
        W = jnp.exp(Dm - m_t[..., None])
        inter = jnp.exp(g - m_t)
        qk = jnp.einsum('bhtd,bhsd->bhts', qb, kb) * W
        num = inter[..., None] * jnp.einsum('bhvk,bhtk->bhtv', C, qb) + jnp.einsum('bhts,bhsv->bhtv', qk, vb)
        den = inter * jnp.einsum('bhk,bhtk->bht', n, qb) + jnp.sum(qk, axis=-1)
        h = num / jnp.maximum(jnp.abs(den), jnp.exp(-m_t))[..., None]
        F = b[..., -1]
        a = F[..., None] - b + ib
        m_new = jnp.maximum(F + m, jnp.max(a, axis=-1))
        decay = jnp.exp(F + m - m_new)
        w_s = jnp.exp(a - m_new[..., None])
        C_new = decay[..., None, None] * C + jnp.einsum('bhsv,bhsk->bhvk', vb * w_s[..., None], kb)
        n_new = decay[..., None] * n + jnp.einsum('bhs,bhsk->bhk', w_s, kb)
        return (C_new, n_new, m_new), h

    init = (jnp.zeros((B_, H, dh, dh), jnp.float32), jnp.zeros((B_, H, dh), jnp.float32),
            jnp.zeros((B_, H), jnp.float32))
    _, hs = lax.scan(step, init, xs)
    return jnp.moveaxis(hs, 0, 2).reshape(B_, H, S, dh)

def stick_breaking_attention(q, k, v):
    B_, H, S, dh = q.shape
    L = SB_BLOCK
    scale = dh ** -0.5
    outs = []
    for blk in range(S // L):
        n_prefix = (blk + 1) * L
        q_blk = q[:, :, blk * L:(blk + 1) * L]
        k_pre = k[:, :, :n_prefix]
        v_pre = v[:, :, :n_prefix]
        z = jnp.einsum('bhtd,bhsd->bhts', q_blk, k_pre) * scale
        t_idx = blk * L + jnp.arange(L)[:, None]
        s_idx = jnp.arange(n_prefix)[None, :]
        strict = s_idx < t_idx
        log_1m_beta = jnp.where(strict, jax.nn.log_sigmoid(-z), 0.0)
        log_a = z + lax.cumsum(log_1m_beta, axis=3, reverse=True)
        A = jnp.exp(jnp.where(strict, log_a, -jnp.inf))
        outs.append(jnp.einsum('bhts,bhsd->bhtd', A, v_pre))
    return jnp.concatenate(outs, axis=2)

def parallel_mixer(h, w_in, conv_w, conv_b, igate_b, fgate_b, mlstm_norm_g, sb_norm_g, w_out):
    dtype = h.dtype
    f32 = jnp.float32
    proj = h @ w_in
    qk_m, v_m, o_m, i_pre, f_pre, qkv_s = jnp.split(proj, PROJ_SPLITS, axis=-1)
    qk_m = jax.nn.silu(causal_depthwise_conv(qk_m, conv_w, conv_b))
    q_m, k_m = jnp.split(qk_m, 2, axis=-1)
    q_m = split_heads(q_m, N_MLSTM_HEADS).astype(f32)
    k_m = split_heads(k_m, N_MLSTM_HEADS).astype(f32) * (MLSTM_HEAD_DIM ** -0.5)
    v_m = split_heads(v_m, N_MLSTM_HEADS).astype(f32)
    log_i = jnp.swapaxes((i_pre + igate_b).astype(f32), 1, 2)
    log_f = jax.nn.log_sigmoid(jnp.swapaxes((f_pre + fgate_b).astype(f32), 1, 2))
    h_m = mlstm_chunkwise(q_m, k_m, v_m, log_i, log_f)
    h_m = jax.nn.sigmoid(split_heads(o_m, N_MLSTM_HEADS).astype(f32)) * h_m
    h_m = head_rms_norm(h_m, mlstm_norm_g)
    q_s, k_s, v_s = jnp.split(qkv_s, 3, axis=-1)
    h_s = stick_breaking_attention(split_heads(q_s, N_SB_HEADS).astype(f32),
                                   split_heads(k_s, N_SB_HEADS).astype(f32),
                                   split_heads(v_s, N_SB_HEADS).astype(f32))
    h_s = head_rms_norm(h_s, sb_norm_g)
    mixed = jnp.concatenate([merge_heads(h_m), merge_heads(h_s)], axis=-1).astype(dtype)
    return mixed @ w_out

def memory_cross_attention(h, mem_n, wq, wkv, wo):
    B_, S, _ = h.shape
    M = mem_n.shape[1]
    q = (h @ wq).reshape(B_, S, N_XATTN_HEADS, XATTN_HEAD_DIM).astype(jnp.float32)
    k, v = jnp.split(mem_n @ wkv, 2, axis=-1)
    k = k.reshape(B_, M, N_XATTN_HEADS, XATTN_HEAD_DIM).astype(jnp.float32)
    v = v.reshape(B_, M, N_XATTN_HEADS, XATTN_HEAD_DIM).astype(jnp.float32)
    p = jax.nn.softmax(jnp.einsum('bshd,bmhd->bhsm', q, k) * (XATTN_HEAD_DIM ** -0.5), axis=-1)
    o = jnp.einsum('bhsm,bmhd->bshd', p, v).reshape(B_, S, N_XATTN_HEADS * XATTN_HEAD_DIM)
    return o.astype(h.dtype) @ wo

def peer_ffn(h, wq, subkeys, u, v):
    B_, S, D = h.shape
    T = B_ * S
    xt = h.reshape(T, D)
    q = (xt @ wq).reshape(T, PEER_HEADS, 2, PEER_HALF)
    s = jnp.einsum('thpc,hpnc->thpn', q, subkeys).astype(jnp.float32)
    s_top, i_top = lax.top_k(s, PEER_TOPK)
    cand = s_top[:, :, 0, :, None] + s_top[:, :, 1, None, :]
    cand_idx = i_top[:, :, 0, :, None] * PEER_N_KEYS + i_top[:, :, 1, None, :]
    best, pos = lax.top_k(cand.reshape(T, PEER_HEADS, PEER_TOPK * PEER_TOPK), PEER_TOPK)
    experts = jnp.take_along_axis(cand_idx.reshape(T, PEER_HEADS, PEER_TOPK * PEER_TOPK), pos, axis=-1)
    gates = jax.nn.softmax(best, axis=-1).astype(h.dtype)
    nb = T // PEER_CHUNK
    E = PEER_HEADS * PEER_TOPK

    def block(args):
        xb, eb, gb = args
        ub = u[eb]
        vb = v[eb]
        act = jax.nn.gelu(jnp.einsum('cd,ced->ce', xb, ub), approximate=False) * gb
        return jnp.einsum('ce,ced->cd', act, vb)

    y = lax.map(block, (xt.reshape(nb, PEER_CHUNK, D), experts.reshape(nb, PEER_CHUNK, E),
                        gates.reshape(nb, PEER_CHUNK, E)))
    return y.reshape(B_, S, D)

def second_inputs(seed: int = 0) -> dict:
    key = jax.random.key(seed)
    ks = jax.random.split(key, 24)
    f32 = jnp.float32

    def nrm(k, shape, scale):
        return jax.random.normal(k, shape, f32) * scale

    def gain(k, shape):
        return 1.0 + 0.02 * jax.random.normal(k, shape, f32)

    return {
        'x': nrm(ks[0], (BATCH, SEQ, D_MODEL), 1.0),
        'mem': nrm(ks[1], (BATCH, MEM_TOKENS, D_MODEL), 1.0),
        'mix_norm_g': gain(ks[2], (DEPTH_2, D_MODEL)),
        'w_in': nrm(ks[3], (DEPTH_2, D_MODEL, PROJ_WIDTH), D_MODEL ** -0.5),
        'conv_w': nrm(ks[4], (DEPTH_2, CONV_WIDTH_2, 2 * MLSTM_WIDTH), CONV_WIDTH_2 ** -0.5),
        'conv_b': nrm(ks[5], (DEPTH_2, 2 * MLSTM_WIDTH), 0.02),
        'igate_b': nrm(ks[6], (DEPTH_2, N_MLSTM_HEADS), 0.1),
        'fgate_b': jnp.linspace(3.0, 6.0, N_MLSTM_HEADS, dtype=f32)[None, :] + nrm(ks[7], (DEPTH_2, N_MLSTM_HEADS), 0.1),
        'mlstm_norm_g': gain(ks[8], (DEPTH_2, MLSTM_WIDTH)),
        'sb_norm_g': gain(ks[9], (DEPTH_2, SB_WIDTH)),
        'w_out': nrm(ks[10], (DEPTH_2, MIX_WIDTH, D_MODEL), MIX_WIDTH ** -0.5),
        'xattn_norm_g': gain(ks[11], (DEPTH_2, D_MODEL)),
        'mem_norm_g': gain(ks[12], (DEPTH_2, D_MODEL)),
        'xattn_wq': nrm(ks[13], (DEPTH_2, D_MODEL, D_MODEL), D_MODEL ** -0.5),
        'xattn_wkv': nrm(ks[14], (DEPTH_2, D_MODEL, 2 * D_MODEL), D_MODEL ** -0.5),
        'xattn_wo': nrm(ks[15], (DEPTH_2, D_MODEL, D_MODEL), D_MODEL ** -0.5),
        'ffn_norm_g': gain(ks[16], (DEPTH_2, D_MODEL)),
        'peer_wq': nrm(ks[17], (DEPTH_2, D_MODEL, PEER_HEADS * PEER_QUERY_DIM), D_MODEL ** -0.5),
        'peer_subkeys': nrm(ks[18], (DEPTH_2, PEER_HEADS, 2, PEER_N_KEYS, PEER_HALF), PEER_HALF ** -0.5),
        'peer_u': nrm(ks[19], (DEPTH_2, PEER_N_EXPERTS, D_MODEL), D_MODEL ** -0.5),
        'peer_v': nrm(ks[20], (DEPTH_2, PEER_N_EXPERTS, D_MODEL), (PEER_HEADS * PEER_TOPK) ** -0.5),
        'final_norm_g': gain(ks[21], (D_MODEL,)),
    }

def second_block(x, mem, mix_norm_g, w_in, conv_w, conv_b, igate_b, fgate_b, mlstm_norm_g, sb_norm_g,
              w_out, xattn_norm_g, mem_norm_g, xattn_wq, xattn_wkv, xattn_wo, ffn_norm_g, peer_wq,
              peer_subkeys, peer_u, peer_v, final_norm_g):
    for l in range(DEPTH_2):
        x = x + parallel_mixer(rms_norm_2(x, mix_norm_g[l]), w_in[l], conv_w[l], conv_b[l], igate_b[l],
                               fgate_b[l], mlstm_norm_g[l], sb_norm_g[l], w_out[l])
        x = x + memory_cross_attention(rms_norm_2(x, xattn_norm_g[l]), rms_norm_2(mem, mem_norm_g[l]),
                                       xattn_wq[l], xattn_wkv[l], xattn_wo[l])
        x = x + peer_ffn(rms_norm_2(x, ffn_norm_g[l]), peer_wq[l], peer_subkeys[l], peer_u[l], peer_v[l])
    return rms_norm_2(x, final_norm_g)


def setup_inputs(seed=0):
    out = dict(first_inputs(seed))
    for name, value in second_inputs(seed + 1).items():
        if name != "x":
            out[name + "_2"] = value
    return out


def reference(
    x, attn_w_qkv, attn_w_o, attn_lambda_q1, attn_lambda_k1, attn_lambda_q2, attn_lambda_k2,
    attn_subln_g, conv_w_in, conv_w, conv_w_out, ffn_w_gate, ffn_w_up, ffn_w_down, ln1_g, ln1_b,
    ln2_g, ln2_b, mem_2, mix_norm_g_2, w_in_2, conv_w_2, conv_b_2, igate_b_2, fgate_b_2,
    mlstm_norm_g_2, sb_norm_g_2, w_out_2, xattn_norm_g_2, mem_norm_g_2, xattn_wq_2, xattn_wkv_2,
    xattn_wo_2, ffn_norm_g_2, peer_wq_2, peer_subkeys_2, peer_u_2, peer_v_2, final_norm_g_2,
):
    x = first_block(
        x, attn_w_qkv, attn_w_o, attn_lambda_q1, attn_lambda_k1, attn_lambda_q2, attn_lambda_k2,
        attn_subln_g, conv_w_in, conv_w, conv_w_out, ffn_w_gate, ffn_w_up, ffn_w_down, ln1_g,
        ln1_b, ln2_g, ln2_b,
    )
    return second_block(
        x, mem_2, mix_norm_g_2, w_in_2, conv_w_2, conv_b_2, igate_b_2, fgate_b_2,
        mlstm_norm_g_2, sb_norm_g_2, w_out_2, xattn_norm_g_2, mem_norm_g_2, xattn_wq_2,
        xattn_wkv_2, xattn_wo_2, ffn_norm_g_2, peer_wq_2, peer_subkeys_2, peer_u_2, peer_v_2,
        final_norm_g_2,
    )


_drawn_inputs = setup_inputs


def setup_inputs(seed=0):
    import zlib

    import numpy as np

    out = dict(_drawn_inputs(seed))
    spreads = {}
    factors = {'attn_lambda_q1': 4.624,
     'attn_lambda_k1': 3.393,
     'attn_lambda_q2': 8.0,
     'attn_subln_g': 5.514,
     'mix_norm_g_2': 2.765,
     'conv_b_2': 6.991,
     'igate_b_2': 64.0,
     'mlstm_norm_g_2': 5.313,
     'sb_norm_g_2': 5.862,
     'xattn_norm_g_2': 8.0,
     'mem_norm_g_2': 8.0,
     'ffn_norm_g_2': 53.854,
     'final_norm_g_2': 8.069}
    for name, (base, spread) in spreads.items():
        noise = np.random.default_rng([zlib.crc32(name.encode()), seed]).standard_normal(out[name].shape)
        drawn = base * np.exp(spread * noise) if base else spread * noise
        out[name] = __import__('jax').numpy.asarray(drawn.astype(out[name].dtype))
    for name, factor in factors.items():
        out[name] = (out[name] * factor).astype(out[name].dtype)
    return out
```

```python
import numpy as np

import concourse.bass as bass
from concourse import mybir
from concourse.alu_op_type import AluOpType as ALU

F32 = mybir.dt.float32
F32R = mybir.dt.float32r
U32 = mybir.dt.uint32
ACT = mybir.ActivationFunctionType
AX = mybir.AxisListType.X

P = 128
D = 1024
KT = D // P
S = 256
FT = 22
CW = 2048
NR = 3
NS = 3
NG = 4
NQ = 32
ALPHA = 4.0 ** 0.25
LAM0 = 0.2
BASE = 16512

GAINS = ["ln1g0", "ln1b0", "ln2g0", "ln2b0", "ln1g1", "ln1b1", "ln2g1", "ln2b1",
         "mem", "mix", "heads", "xattn", "ffn", "final"]
STREAM = ([("qkv", i) for i in range(12)] + [("wo", i) for i in range(4)]
          + [("gu0", i) for i in range(FT)] + [("dn0", i) for i in range(FT // 2)]
          + [("cin", i) for i in range(12)] + [("cout", i) for i in range(4)]
          + [("gu1", i) for i in range(FT)] + [("dn1", i) for i in range(FT // 2)]
          + [("win", i) for i in range(14)] + [("wout", i) for i in range(4)]
          + [("xk", i) for i in range(4)] + [("xv", i) for i in range(4)]
          + [("xq", i) for i in range(4)] + [("xo", i) for i in range(4)]
          + [("pq", i) for i in range(8)] + [("sk", 0)]
          + [("ex", i) for i in range(P)])
CC = {"cos": (0, 256), "sin": (256, 256), "amask": (512, 512), "cmask": (1024, 512),
      "keep": (1536, 256), "sneg": (1792, 256), "tri": (2048, 128), "ones": (2176, 128)}
CWID = 2304


def flat(items):
    out = []
    for x in items:
        if x is None:
            continue
        if len(x) == 2 and isinstance(x[1], int):
            out.append(x)
        else:
            out += flat(x)
    return out


class Lane:

    def __init__(self, eng, sem, turn=False):
        self.eng, self.sem, self.count, self.seen, self.turn = eng, sem, 0, {}, turn

    def wait(self, *after):
        for sem, value in flat(after):
            if self.seen.get(sem.name, 0) < value:
                self.seen[sem.name] = value
                self.eng.wait_ge(sem, value)

    def __call__(self, fn, *after, sig=True):
        self.wait(after, [(self.sem, self.count)] if self.turn else None)
        r = fn(self.eng)
        if not sig:
            return None
        r.then_inc(self.sem, 1)
        self.count += 1
        return (self.sem, self.count)

    def dma(self, fn, sem, total, *after):
        self.wait(after)
        fn(self.eng).then_inc(sem, 16)
        return (sem, total)


def build(nc, a, out, ctx):
    def sem(name):
        return ctx.enter_context(nc.semaphore(name))

    at = [BASE]

    def sb(name, shape, dt=F32, off=None):
        size = int(np.prod(shape[1:])) * 4
        size = -(-size // 32) * 32
        if off is None:
            off = at[0]
            at[0] += size
        else:
            o = off[0]
            off[0] += size
            assert off[0] <= nc.sbuf_usable_end, (name, off[0], nc.sbuf_usable_end)
            off = o
        return nc.alloc_sbuf_tensor_at(name, list(shape), dt, offset=off)

    PE, AC, DV, GP, SP = (Lane(e, sem(n), t) for e, n, t in (
        (nc.tensor, "s_pe", False), (nc.scalar, "s_act", True), (nc.vector, "s_dve", True),
        (nc.gpsimd, "s_pool", False), (nc.sync, "s_sp", False)))

    banks = ctx.enter_context(nc.psum_tensor("banks", [P, 8, 512], F32))
    ps = [banks[:, i, :] for i in range(8)]
    free = [[] for _ in range(8)]

    raw = [sb(f"raw{i}", [P, CW]) for i in range(NR)]
    wH = [sb(f"wH{i}", [P, CW], F32R) for i in range(NS)]
    wL = [sb(f"wL{i}", [P, CW], F32R) for i in range(NS)]
    xH = sb("xH", [P, KT, S], F32R)
    xL = sb("xL", [P, KT, S], F32R)
    h = sb("h", [P, 2, D])
    gn = [sb(f"gn{i}", [P, D]) for i in range(NG)]
    ident = sb("ident", [P, P])
    iota = sb("iota", [P, P])
    stat = sb("stat", [P, 2, 2, 6])
    mv = sb("mv", [P, 2, 2])
    rs = sb("rs", [P, 2, 2])
    lamv = sb("lamv", [P, 8])
    OV = at[0]

    s_raw = [sem(f"s_raw{i}") for i in range(NR)]
    s_gn = [sem(f"s_gn{i}") for i in range(NG)]
    s_x, s_id, s_cst, s_lam, s_sub, s_mem, s_cw, s_c4, s_gw, s_gb = (
        sem(n) for n in ("s_x", "s_id", "s_cst", "s_lam", "s_sub", "s_mem", "s_cw", "s_c4", "s_gw", "s_gb"))
    s_out = sem("s_out")

    x_t = SP.dma(lambda e: e.dma_start(h[:, :, :], a["x"]), s_x, 16)
    SP.dma(lambda e: e.dma_start(ident[:, :], a["ident"]), s_id, 16)
    id_t = SP.dma(lambda e: e.dma_start(iota[:, :], a["iota"]), s_id, 32)

    split_a, split_v, done, raw_t = {}, {}, {}, {}

    def fetch(n):
        if n >= len(STREAM):
            return
        name, i = STREAM[n]
        r = n % NR
        raw_t[n] = SP.dma(lambda e: e.dma_start(raw[r][:, :], a[name][i]), s_raw[r], 16 * (n // NR + 1),
                          split_a.get(n - NR), split_v.get(n - NR))

    nsplit = [0]

    def split(upto):
        while nsplit[0] < min(upto, len(STREAM)):
            n = nsplit[0]
            r, s = n % NR, n % NS
            split_a[n] = AC(lambda e: e.activation(wH[s][:, :], raw[r][:, :], ACT.Copy), raw_t[n], done[n - NS] if n >= NS else None)
            split_v[n] = DV(lambda e: e.tensor_tensor(wL[s][:, :], raw[r][:, :], wH[s][:, :].bitcast(F32), ALU.subtract),
                            split_a[n], done[n - NS] if n >= NS else None)
            fetch(n + NR)
            nsplit[0] += 1

    nuse = [0]

    def take(name, i, ahead=NS):
        n = nuse[0]
        assert STREAM[n] == (name, i), (STREAM[n], name, i)
        nuse[0] += 1
        split(n + ahead)
        return n, wH[n % NS], wL[n % NS], [split_a[n], split_v[n]]

    gain_t, gain_use = {}, {}

    def load_gain(n):
        if n >= len(GAINS):
            return
        g = n % NG
        gain_t[n] = GP.dma(lambda e: e.dma_start(gn[g][:, :], a["gains"][n:n + 1, :].broadcast_to([P, D])),
                           s_gn[g], 16 * (n // NG + 1), gain_use.get(n - NG))

    def gain(name):
        n = GAINS.index(name)
        return gn[n % NG], gain_t[n]

    def gain_used(name, tok):
        n = GAINS.index(name)
        gain_use[n] = tok
        load_gain(n + NG)

    for n in range(NR):
        fetch(n)
    for n in range(NG):
        load_gain(n)

    def mm(o, l, r, start, stop, *after, sig=False):
        return PE(lambda e: e.matmul(o, l, r, start=start, stop=stop), *after, sig=sig)

    def transpose(o, i, *after, sig=False):
        k = i.shape[0]
        return PE(lambda e: e.transpose(o, i, ident[:k, :k]), *after, sig=sig)

    def cols(bank, off, H, L, wh, wl, wcol, after):
        for k in range(KT):
            w0 = k * 256 + wcol
            o = ps[bank][:, off:off + S]
            first = (after, free[bank]) if k == 0 else ()
            mm(o, wh[:, w0:w0 + P], H[:, k, :], k == 0, False, *first)
            mm(o, wh[:, w0:w0 + P], L[:, k, :], False, False)
            t = mm(o, wl[:, w0:w0 + P], H[:, k, :], False, k == KT - 1, sig=k == KT - 1)
        return t

    def rows(name, n, H, L, after):
        for c in range(n):
            idx, wh, wl, wt = take(name, c)
            for kk in range(2):
                k = 2 * c + kk
                for t in range(2):
                    ts = slice(t * P, t * P + P)
                    for part, (l, w) in enumerate(((H, wh), (H, wl), (L, wh))):
                        for e in range(2):
                            b = 2 * t + e
                            w0 = kk * D + e * 512
                            lastk = k == 2 * n - 1 and part == 2
                            first = (after, wt, free[b]) if c == 0 and kk == 0 else (wt,)
                            tok = mm(ps[b][:, :], l[:, k, ts], w[:, w0:w0 + 512], k == 0 and part == 0, lastk,
                                     *first, sig=(kk == 1 and t == 1 and part == 2 and e == 1) or lastk)
                            if lastk:
                                free[b] = [tok]
            done[idx] = tok
        return [free[b][0] for b in range(4)]

    def blocks(name, c0, H, L, bank, after):
        for c in range(2):
            idx, wh, wl, wt = take(name, c0 + c)
            for kk in range(4):
                k = 4 * c + kk
                for t in range(2):
                    ts = slice(t * P, t * P + P)
                    for part, (l, w) in enumerate(((H, wh), (H, wl), (L, wh))):
                        last = k == KT - 1 and part == 2
                        tok = mm(ps[bank + t][:, :], l[:, k, ts], w[:, kk * 512:kk * 512 + 512], k == 0 and part == 0,
                                 last, after, wt, free[bank + t] if k == 0 else None,
                                 sig=last or (kk == 3 and t == 1 and part == 2))
                        if last:
                            free[bank + t] = [tok]
            done[idx] = tok
        return [free[bank][0], free[bank + 1][0]]

    def part(dH, dL, src, after, scale=None):
        if scale is None:
            t1 = AC(lambda e: e.activation(dH, src, ACT.Copy), after)
        else:
            t1 = AC(lambda e: e.activation(dH, src, ACT.Copy, scale=scale), after)
        t2 = DV(lambda e: e.tensor_tensor(dL, src, dH.bitcast(F32), ALU.subtract), t1, after)
        return [t1, t2]

    def turn(nat, toks, H, L, after=None, banks=(4, 5, 6, 7)):
        out_t = []
        n = 0
        for j in range(2):
            for q in range(2):
                b = banks[n % len(banks)]
                n += 1
                for i in range(4):
                    k = 4 * q + i
                    t = transpose(ps[b][:, i * P:i * P + P], nat[:, j, k * P:k * P + P],
                                  toks[j], free[b], id_t, sig=i == 3)
                src = ps[b][:, :].rearrange("p (k t) -> p k t", k=4)
                r = part(H[:, 4 * q:4 * q + 4, j * P:j * P + P], L[:, 4 * q:4 * q + 4, j * P:j * P + P], src, [t, after])
                free[b] = [r[1]]
                out_t += r
        return out_t

    def root(j, src, mul, eps, after):
        t = DV(lambda e: e.tensor_scalar(rs[:, j, 0:1], src, mul, eps, ALU.mult, ALU.add), after)
        t = AC(lambda e: e.activation(rs[:, j, 0:1], rs[:, j, 0:1], ACT.Sqrt), t)
        return DV(lambda e: e.reciprocal(rs[:, j, 1:2], rs[:, j, 0:1]), t)

    def add_norm(banks_t, g, b):
        (gw, gt), (bw, bt) = gain(g), gain(b)
        res = []
        for j in range(2):
            for e2 in range(2):
                k = 2 * j + e2
                hv = h[:, j, e2 * 512:e2 * 512 + 512]
                t = DV(lambda e: e.scalar_tensor_tensor(hv, hv, ALPHA, ps[k][:, :], ALU.mult, ALU.add), banks_t[k])
                free[k] = [t]
                t = DV(lambda e: e.bn_stats(stat[:, j, e2, :], hv), t)
            t = DV(lambda e: e.bn_aggr(mv[:, j, :], stat[:, j, :, :].rearrange("p a b -> p (a b)")), t)
            t = root(j, mv[:, j, 1:2], 1.0, 1e-5, t)
            t0 = DV(lambda e: e.scalar_tensor_tensor(h[:, j, :], h[:, j, :], mv[:, j, 0:1], gw[:, :], ALU.subtract, ALU.mult), t, gt)
            res.append(DV(lambda e: e.scalar_tensor_tensor(h[:, j, :], h[:, j, :], rs[:, j, 1:2], bw[:, :], ALU.mult, ALU.add), t0, t, bt))
        gain_used(g, res[1])
        gain_used(b, res[1])
        return res

    def rms(src, toks, nat, g, after=None):
        gw, gt = gain(g)
        res = []
        for j in range(2):
            t = AC(lambda e: e.activation(nat[:, j, :], src[:, j, :], ACT.Square, accum_out=mv[:, j, 0:1]), toks[j], after)
            t = root(j, mv[:, j, 0:1], 1.0 / D, 1e-6, t)
            res.append(DV(lambda e: e.scalar_tensor_tensor(nat[:, j, :], src[:, j, :], rs[:, j, 1:2], gw[:, :], ALU.mult, ALU.mult), t, gt))
        gain_used(g, res[1])
        return res

    def add_rows(banks_t):
        res = []
        for j in range(2):
            for e2 in range(2):
                k = 2 * j + e2
                hv = h[:, j, e2 * 512:e2 * 512 + 512]
                t = DV(lambda e: e.tensor_tensor(hv, hv, ps[k][:, :], ALU.add), banks_t[k])
                free[k] = [t]
            res.append(t)
        return res

    o = [OV]
    cst = sb("cst", [P, CWID], off=o)
    OW = o[0]

    def const(name):
        c0, n = CC[name]
        return cst[:, c0:c0 + n]

    QK = sb("QK", [P, 2, 2048], off=o)
    V = sb("V", [P, 2, D], off=o)
    QT = sb("QT", [P, 8, S], off=o)
    KTt = sb("KT", [P, 8, S], off=o)
    O = sb("O", [P, 2, D], off=o)
    lq = sb("lq", [P, 4, 64], off=o)
    lpr = sb("lpr", [P, 2, 64], off=o)
    sub = sb("sub", [P, P], off=o)
    rot = sb("rot", [P, 4, P], off=o)
    Sm = [sb(f"Sm{i}", [P, 2, S], off=o) for i in range(2)]
    Am = [sb(f"Am{i}", [P, S], off=o) for i in range(2)]
    AT = [sb(f"AT{i}", [P, 2, P], off=o) for i in range(2)]
    sm = [sb(f"sm{i}", [P, 8], off=o) for i in range(2)]
    s8 = sb("s8", [P, 2, 3, 8], off=o)

    cst_t = SP.dma(lambda e: e.dma_start(cst[:, :], a["consts"]), s_cst, 16)
    lam_t = SP.dma(lambda e: e.dma_start(lq[:, :, :].rearrange("p a b -> p (a b)"), a["lam"].broadcast_to([P, 256])), s_lam, 16)
    sub_t = SP.dma(lambda e: e.dma_start(sub[:, :], a["subg"].broadcast_to([P, P])), s_sub, 16)

    xt = turn(h, [x_t, x_t], xH, xL)

    t = DV(lambda e: e.tensor_tensor(lpr[:, :, :], lq[:, 0:2, :], lq[:, 2:4, :], ALU.mult), lam_t)
    t = DV(lambda e: e.reduce_sum(lamv[:, 0:2], lpr[:, :, :], AX), t)
    t = AC(lambda e: e.activation(lamv[:, 2:4], lamv[:, 0:2], ACT.Exp), t)
    t = DV(lambda e: e.tensor_tensor(lamv[:, 4:5], lamv[:, 3:4], lamv[:, 2:3], ALU.subtract), t)
    nlam_t = DV(lambda e: e.tensor_scalar(lamv[:, 5:6], lamv[:, 4:5], LAM0, None, ALU.subtract), t)

    qk_t = {}
    for blk in range(6):
        bank = 2 * (blk % 2)
        bt = blocks("qkv", 2 * blk, xH, xL, bank, xt if blk == 0 else None)
        for j in range(2):
            if blk < 4:
                dst, sc = QK[:, j, blk * 512:blk * 512 + 512], (0.125 if blk < 2 else 1.0)
            else:
                dst, sc = V[:, j, (blk - 4) * 512:(blk - 4) * 512 + 512], 1.0
            t = AC(lambda e: e.activation(dst, ps[bank + j][:, :], ACT.Copy, scale=sc), bt[j])
            free[bank + j] = [t]
            qk_t[blk, j] = t

    T_t = {}
    for w in range(2):
        for j in range(2):
            z = QK[:, j, w * D:w * D + D].rearrange("p (g d) -> p g d", d=64)
            x1, x2 = z[:, :, 0:8], z[:, :, 8:16]
            c = const("cos")[:, j * P:j * P + P].rearrange("p (g d) -> p g d", d=8)
            s = const("sin")[:, j * P:j * P + P].rearrange("p (g d) -> p g d", d=8)
            r = [rot[:, i, :].rearrange("p (g d) -> p g d", d=8) for i in range(4)]
            dep = [qk_t[2 * w, j], qk_t[2 * w + 1, j], cst_t]
            m = [DV(lambda e, q=q, u=u, v=v: e.tensor_tensor(r[q], u, v, ALU.mult), dep)
                 for q, u, v in ((0, x1, c), (1, x2, s), (2, x2, c), (3, x1, s))]
            DV(lambda e: e.tensor_tensor(x1, r[0], r[1], ALU.subtract), m)
            t = DV(lambda e: e.tensor_tensor(x2, r[2], r[3], ALU.add), m)
            dst = QT if w == 0 else KTt
            for q in range(2):
                b = 4 + (4 * w + 2 * j + q) % 4
                for i in range(4):
                    hd = 4 * q + i
                    tt = transpose(ps[b][:, i * P:i * P + P], QK[:, j, w * D + hd * P:w * D + hd * P + P], t, dep, free[b], sig=i == 3)
                src = ps[b][:, :].rearrange("p (k t) -> p k t", k=4)
                T_t[w, j, q] = AC(lambda e: e.activation(dst[:, 4 * q:4 * q + 4, j * P:j * P + P], src, ACT.Copy), tt)
                free[b] = [T_t[w, j, q]]

    units = [(hd, j) for hd in range(8) for j in range(2)]
    at_p, use_p = {}, {}

    def att_scores(u):
        hd, j = units[u]
        b, i = u % 2, u % 2
        nk = P * (j + 1)
        q = hd // 4
        dep = [T_t[0, j, q]] + [T_t[1, jj, q] for jj in range(j + 1)]
        for c in range(2):
            cs = slice(64 * c, 64 * c + 64)
            t = mm(ps[2 * b + c][:, 0:nk], QT[cs, hd, j * P:j * P + P], KTt[cs, hd, 0:nk], True, True,
                   dep, free[2 * b + c], sig=c == 1)
        sv = Sm[i][:, :, 0:nk]
        mk = const("amask")[:, j * S:j * S + nk].unsqueeze(1).broadcast_to([P, 2, nk])
        t = DV(lambda e: e.tensor_tensor(sv, banks[:, 2 * b:2 * b + 2, 0:nk], mk, ALU.add), t, use_p.get(u - 2))
        free[2 * b] = free[2 * b + 1] = [t]
        m = sm[i]
        t = DV(lambda e: e.tensor_reduce(m[:, 0:2], sv, AX, ALU.max, negate=True), t)
        ex = [AC(lambda e, c=c: e.activation(Sm[i][:, c, 0:nk], Sm[i][:, c, 0:nk], ACT.Exp, bias=m[:, c:c + 1],
                                             accum_out=m[:, 2 + c:3 + c]), t) for c in range(2)]
        t = DV(lambda e: e.reciprocal(m[:, 4:6], m[:, 2:4]), ex)
        t2 = DV(lambda e: e.tensor_scalar(m[:, 6:7], m[:, 5:6], lamv[:, 5:6], None, ALU.mult), t, nlam_t)
        t = DV(lambda e: e.tensor_scalar(Sm[i][:, 0, 0:nk], Sm[i][:, 0, 0:nk], m[:, 4:5], None, ALU.mult), t)
        at_p[u] = DV(lambda e: e.scalar_tensor_tensor(Am[i][:, 0:nk], Sm[i][:, 1, 0:nk], m[:, 6:7], Sm[i][:, 0, 0:nk],
                                                      ALU.mult, ALU.add), t, t2, use_p.get(u - 2))

    O_t = {}

    def att_out(u):
        hd, j = units[u]
        b, bo, i = 4 + u % 2, 6 + u % 2, u % 2
        for k in range(j + 1):
            t = transpose(ps[b][:, k * P:k * P + P], Am[i][:, k * P:k * P + P], at_p[u], free[b], sig=k == j)
        use_p[u] = t
        t = AC(lambda e: e.activation(AT[i][:, 0:j + 1, :].rearrange("p a b -> p (a b)"), ps[b][:, 0:P * (j + 1)], ACT.Copy), t, O_t.get(u - 2))
        free[b] = [t]
        for k in range(j + 1):
            tt = mm(ps[bo][:, 0:P], AT[i][:, k, :], V[:, k, hd * P:hd * P + P], k == 0, k == j,
                    t, free[bo], qk_t[4 + hd // 4, k], sig=k == j)
        O_t[u] = AC(lambda e: e.activation(O[:, j, hd * P:hd * P + P], ps[bo][:, 0:P], ACT.Copy), tt)
        free[bo] = [O_t[u]]

    for u in range(17):
        if u < 16:
            att_scores(u)
        if u >= 1:
            att_out(u - 1)

    def head_norm(src, toks, sq, groups, eps, mul, scale_row, row_t):
        res = []
        for j in range(2):
            t = AC(lambda e: e.activation(sq[:, j, :], src[:, j, :], ACT.Square), toks[j])
            last = t
            for c0, nh, w in groups:
                v = sq[:, j, c0:c0 + nh * w].rearrange("p (a b) -> p a b", b=w)
                sv = src[:, j, c0:c0 + nh * w].rearrange("p (a b) -> p a b", b=w)
                a0, a1, a2 = s8[:, j, 0, 0:nh], s8[:, j, 1, 0:nh], s8[:, j, 2, 0:nh]
                t1 = DV(lambda e: e.reduce_sum(a0, v, AX), t)
                t1 = DV(lambda e: e.tensor_scalar(a1, a0, 1.0 / w, eps, ALU.mult, ALU.add), t1, last)
                t1 = AC(lambda e: e.activation(a1, a1, ACT.Sqrt), t1)
                t1 = DV(lambda e: e.reciprocal(a2, a1), t1)
                if mul != 1.0:
                    t1 = DV(lambda e: e.tensor_scalar(a2, a2, mul, None, ALU.mult), t1)
                last = DV(lambda e: e.tensor_tensor(sv, sv, a2.unsqueeze(2).broadcast_to([P, nh, w]), ALU.mult), t1)
            res.append(DV(lambda e: e.tensor_tensor(src[:, j, :], src[:, j, :], scale_row, ALU.mult)
                          if scale_row.shape[-1] == D else
                          e.tensor_tensor(src[:, j, :].rearrange("p (a b) -> p a b", b=P), src[:, j, :].rearrange("p (a b) -> p a b", b=P),
                                          scale_row.unsqueeze(1).broadcast_to([P, 8, P]), ALU.mult), last, row_t))
        return res

    o_t = head_norm(O, [[O_t[u] for u in range(16)]] * 2, V, [(0, 8, P)], 1e-5, 1.0 - LAM0, sub[:, :], sub_t)
    xt = turn(O, o_t, xH, xL)
    ln_t = add_norm(rows("wo", 4, xH, xL, xt), "ln1g0", "ln1b0")

    o = [OW]
    fH = sb("fH", [P, FT, S], F32R, off=o)
    fL = sb("fL", [P, FT, S], F32R, off=o)
    sg = [sb(f"sg{i}", [P, S], off=o) for i in range(2)]
    fv = [sb(f"fv{i}", [P, S], off=o) for i in range(2)]

    def swiglu(layer, xt):
        f_t = []
        for f in range(FT):
            idx, wh, wl, wt = take(f"gu{layer}", f)
            b, i = 4 + f % 4, f % 2
            tg = cols(b, 0, xH, xL, wh, wl, 0, [wt, xt])
            tu = cols(b, S, xH, xL, wh, wl, P, [])
            done[idx] = tu
            t1 = AC(lambda e: e.activation(sg[i][:, :], ps[b][:, 0:S], ACT.Silu), tu, f_t[2 * (f - 2)] if f >= 2 else None,
                    f_t[2 * (f - 2) + 1] if f >= 2 else None)
            t2 = DV(lambda e: e.tensor_tensor(fv[i][:, :], sg[i][:, :], ps[b][:, S:2 * S], ALU.mult), t1,
                    f_t[2 * (f - 2)] if f >= 2 else None)
            free[b] = [t2]
            t3 = AC(lambda e: e.activation(fH[:, f, :], fv[i][:, :], ACT.Copy), t2)
            t4 = DV(lambda e: e.tensor_tensor(fL[:, f, :], fv[i][:, :], fH[:, f, :].bitcast(F32), ALU.subtract), t3)
            f_t += [t3, t4]
        return rows(f"dn{layer}", FT // 2, fH, fL, f_t)

    xt = turn(h, ln_t, xH, xL)
    ln_t = add_norm(swiglu(0, xt), "ln2g0", "ln2b0")

    yc = sb("yc", [P, KT, S], off=o)
    up = [sb(f"up{i}", [P, S + 2], off=o) for i in range(2)]
    cw = sb("cw", [P, KT, 3], off=o)
    cw_t = GP.dma(lambda e: e.dma_start(cw[:, :, :], a["convw"]), s_cw, 16, ln_t)
    pad_t = [DV(lambda e, i=i: e.memset(up[i][:, 0:2], 0.0), ln_t) for i in range(2)]
    xt = turn(h, ln_t, xH, xL)
    y_t = []
    for c in range(8):
        idx, wh, wl, wt = take("cin", c)
        b, i = 4 + c % 4, c % 2
        cols(b, 0, xH, xL, wh, wl, 0, [wt, xt])
        tu = cols(b, S, xH, xL, wh, wl, P, [])
        done[idx] = tu
        prev = y_t[c - 2] if c >= 2 else None
        t1 = AC(lambda e: e.activation(sg[i][:, :], ps[b][:, 0:S], ACT.Copy), tu, prev)
        t2 = DV(lambda e: e.tensor_tensor(up[i][:, 2:S + 2], sg[i][:, :], ps[b][:, S:2 * S], ALU.mult), t1, prev, pad_t)
        free[b] = [t2]
        t = DV(lambda e: e.tensor_scalar(yc[:, c, :], up[i][:, 0:S], cw[:, c, 0:1], None, ALU.mult), t2, cw_t, pad_t)
        for q in (1, 2):
            t = DV(lambda e, q=q: e.scalar_tensor_tensor(yc[:, c, :], up[i][:, q:S + q], cw[:, c, q:q + 1], yc[:, c, :], ALU.mult, ALU.add), t)
        y_t.append(t)
    z_t = []
    for c in range(4):
        idx, wh, wl, wt = take("cin", 8 + c)
        for q in range(2):
            n = 2 * c + q
            b, i = 4 + n % 4, n % 2
            tb = cols(b, 0, xH, xL, wh, wl, q * P, [wt])
            t2 = DV(lambda e: e.tensor_tensor(fv[i][:, :], yc[:, n, :], ps[b][:, 0:S], ALU.mult), tb, y_t[n],
                    z_t[2 * (n - 2)] if n >= 2 else None)
            free[b] = [t2]
            t3 = AC(lambda e: e.activation(fH[:, n, :], fv[i][:, :], ACT.Copy), t2)
            t4 = DV(lambda e: e.tensor_tensor(fL[:, n, :], fv[i][:, :], fH[:, n, :].bitcast(F32), ALU.subtract), t3)
            z_t += [t3, t4]
        done[idx] = tb
    ln_t = add_norm(rows("cout", 4, fH, fL, z_t), "ln1g1", "ln1b1")
    xt = turn(h, ln_t, xH, xL)
    ln_t = add_norm(swiglu(1, xt), "ln2g1", "ln2b1")

    o = [OW]
    mH = sb("mH", [P, KT, S], F32R, off=o)
    mL = sb("mL", [P, KT, S], F32R, off=o)
    nat = sb("nat", [P, 2, D], off=o)
    OM = o[0]
    mem_t = GP.dma(lambda e: e.dma_start(nat[:, :, :], a["mem"]), s_mem, 16, ln_t)
    mt = rms(nat, [mem_t, mem_t], nat2 := sb("nat2", [P, 2, D], off=o), "mem")
    mt = turn(nat2, mt, mH, mL)

    o = [OM]
    ct = sb("ct", [P, 8, 5], off=o)
    gwt = sb("gwt", [P, KT, 8], off=o)
    gbt = sb("gbt", [4, 2], off=o)
    selt = sb("selt", [4, 4, P], off=o)
    qp = [sb(f"qp{i}", [P, 2, S + 3], off=o) for i in range(2)]
    qm = sb("qm", [P, 8, S], off=o)
    vm = sb("vm", [P, 2, 512], off=o)
    og = sb("og", [P, 2, 512], off=o)
    qs = sb("qs", [P, 4, S], off=o)
    ks = sb("ks", [P, 4, S], off=o)
    vs = sb("vs", [P, 2, 512], off=o)
    gi = [sb(f"gi{i}", [4, S], off=o) for i in range(7)]
    gc = sb("gc", [P, 2, 2, 4], off=o)
    s8m = sb("s8m", [P, 8], off=o)
    Wt = [sb(f"Wt{i}", [P, S], off=o) for i in range(2)]
    Pm = [sb(f"Pm{i}", [P, S], off=o) for i in range(2)]
    PT = [sb(f"PT{i}", [P, 2, P], off=o) for i in range(2)]
    dn = [sb(f"dn{i}", [P, 4], off=o) for i in range(2)]
    xm = nat
    mx = nat2
    after_mem = mt
    c4_t = GP.dma(lambda e: e.dma_start(ct[:, :, :], a["conv4"]), s_c4, 16, after_mem)
    GP.dma(lambda e: e.dma_start(gwt[:, :, :], a["gatew"]), s_gw, 16, after_mem)
    GP.dma(lambda e: e.dma_start(gbt[:, :], a["gateb"]), s_gw, 32, after_mem)
    gw_t = GP.dma(lambda e: e.dma_start(selt[:, :, :], a["sel"]), s_gw, 48, after_mem)
    n_t = rms(h, ln_t, xm, "mix", after=after_mem)
    xt = turn(xm, n_t, xH, xL)
    pad_t = [DV(lambda e, i=i: e.memset(qp[i][:, :, 0:3], 0.0), after_mem) for i in range(2)]

    for g in range(2):
        for k in range(KT):
            for part_, (H, sig_) in enumerate(((xH, False), (xL, k == KT - 1))):
                t = mm(ps[0][0:4, g * S:g * S + S], gwt[:, k, 4 * g:4 * g + 4], H[:, k, :].bitcast(F32),
                       k == 0 and part_ == 0, k == KT - 1 and part_ == 1, xt, gw_t, free[0], sig=sig_ and g == 1)
    gi_i, gi_f, g1, g2, gB, gmm, gng = gi
    t_i = DV(lambda e: e.tensor_scalar(gi_i[:, :], ps[0][0:4, 0:S], gbt[:, 0:1], None, ALU.add), t, gw_t)
    t_f = DV(lambda e: e.tensor_scalar(gi_f[:, :], ps[0][0:4, S:2 * S], gbt[:, 1:2], None, ALU.add), t, gw_t)
    free[0] = [t_f]
    t = DV(lambda e: e.scalar_tensor_tensor(g1[:, :], gi_f[:, :], -1.0, gi_f[:, :], ALU.mult, ALU.max), t_f)
    t = AC(lambda e: e.activation(g1[:, :], g1[:, :], ACT.Exp, scale=-1.0), t)
    t = AC(lambda e: e.activation(g2[:, :], g1[:, :], ACT.Ln, bias=1.0), t)
    t = DV(lambda e: e.scalar_tensor_tensor(g1[:, :], gi_f[:, :], 0.0, g2[:, :], ALU.min, ALU.subtract), t)
    z0 = DV(lambda e: e.memset(g2[:, :], 1.0), t)
    t_B = DV(lambda e: e.tensor_tensor_scan(gB[:, :], g2[:, :], g1[:, :], 0.0, ALU.mult, ALU.add), t, z0)
    t_c = DV(lambda e: e.tensor_tensor(gi_i[:, :], gi_i[:, :], gB[:, :], ALU.subtract), t_B, t_i)
    z0 = DV(lambda e: e.memset(g1[:, :], 0.0), t_B)
    t_mm = DV(lambda e: e.tensor_tensor_scan(gmm[:, :], g1[:, :], gi_i[:, :], 0.0, ALU.add, ALU.max), t_c, z0)
    t = DV(lambda e: e.tensor_tensor(gng[:, :], gB[:, :], gmm[:, :], ALU.add), t_mm)
    t_ng = AC(lambda e: e.activation(gng[:, :], gng[:, :], ACT.Exp, scale=-1.0), t)
    for j in range(2):
        transpose(ps[1][:, 8 * j:8 * j + 4], gmm[:, j * P:j * P + P], t_mm, free[1])
        t = transpose(ps[1][:, 8 * j + 4:8 * j + 8], gng[:, j * P:j * P + P], t_ng, sig=True)
    gcv = ps[1][:, 0:16].rearrange("p (j a b) -> p j a b", j=2, a=2)
    DV(lambda e: e.tensor_scalar(gc[:, :, 0, :], gcv[:, :, 0, :], -1.0, None, ALU.mult), t)
    gc_t = DV(lambda e: e.tensor_copy(gc[:, :, 1, :], gcv[:, :, 1, :]), t)
    free[1] = [gc_t]

    qm_t = []
    for c in range(4):
        idx, wh, wl, wt = take("win", c)
        b, i = 4 + c % 4, c % 2
        cols(b, 0, xH, xL, wh, wl, 0, [wt, xt])
        t = cols(b, S, xH, xL, wh, wl, P, [])
        done[idx] = t
        t = AC(lambda e: e.activation(qp[i][:, :, 3:S + 3], ps[b][:, :].rearrange("p (a t) -> p a t", a=2), ACT.Copy), t,
               qm_t[2 * (c - 2):2 * (c - 2) + 2] if c >= 2 else None, pad_t)
        free[b] = [t]
        for q in range(2):
            n = 2 * c + q
            m = DV(lambda e: e.tensor_scalar(qm[:, n, :], qp[i][:, q, 0:S], ct[:, n, 0:1], ct[:, n, 4:5], ALU.mult, ALU.add), t, c4_t, pad_t)
            for w in range(1, 4):
                m = DV(lambda e, w=w: e.scalar_tensor_tensor(qm[:, n, :], qp[i][:, q, w:S + w], ct[:, n, w:w + 1], qm[:, n, :], ALU.mult, ALU.add), m)
            qm_t.append(m)
    silu_t = [AC(lambda e, n=n: e.activation(qm[:, n, :], qm[:, n, :], ACT.Silu), qm_t[n]) for n in range(8)]
    vm_t, og_t, vs_t = [], [], []
    bt = blocks("win", 4, xH, xL, 0, xt)
    for j in range(2):
        vm_t.append(AC(lambda e: e.activation(vm[:, j, :], ps[j][:, :], ACT.Copy), bt[j]))
        free[j] = [vm_t[j]]
    bt = blocks("win", 6, xH, xL, 2, xt)
    for j in range(2):
        og_t.append(AC(lambda e: e.activation(og[:, j, :], ps[2 + j][:, :], ACT.Sigmoid), bt[j]))
        free[2 + j] = [og_t[j]]
    sq_t = {}
    for w in range(2):
        for c in range(2):
            idx, wh, wl, wt = take("win", 8 + 2 * w + c)
            b = 4 + (2 * w + c) % 4
            cols(b, 0, xH, xL, wh, wl, 0, [wt, xt])
            t = cols(b, S, xH, xL, wh, wl, P, [])
            done[idx] = t
            dst = (qs if w == 0 else ks)[:, 2 * c:2 * c + 2, :].rearrange("p a t -> p (a t)")
            sq_t[w, c] = AC(lambda e: e.activation(dst, ps[b][:, :], ACT.Copy, scale=0.125 if w == 0 else 1.0), t)
            free[b] = [sq_t[w, c]]
    bt = blocks("win", 12, xH, xL, 0, xt)
    for j in range(2):
        vs_t.append(AC(lambda e: e.activation(vs[:, j, :], ps[j][:, :], ACT.Copy), bt[j]))
        free[j] = [vs_t[j]]

    munits = [(hd, j) for hd in range(4) for j in range(2)]
    pm_t, mx_t, pt_t = {}, {}, {}

    def ml_scores(u):
        hd, j = munits[u]
        b, i, nk = u % 2, u % 2, P * (j + 1)
        mm(ps[b][:, 0:nk], qm[:, hd, j * P:j * P + P], qm[:, 4 + hd, 0:nk], True, True, silu_t[hd], silu_t[4 + hd], free[b])
        t = mm(ps[b][:, S:S + nk], selt[:, hd, :], gi_i[:, 0:nk], True, True, t_c, gw_t, sig=True)
        w_ = DV(lambda e: e.tensor_tensor(Wt[i][:, 0:nk], ps[b][:, S:S + nk], const("cmask")[:, j * S:j * S + nk], ALU.add), t, pm_t.get(u - 2))
        w_ = AC(lambda e: e.activation(Wt[i][:, 0:nk], Wt[i][:, 0:nk], ACT.Exp, bias=gc[:, j, 0, hd:hd + 1]), w_, gc_t)
        w_ = DV(lambda e: e.scalar_tensor_tensor(Pm[i][:, 0:nk], ps[b][:, 0:nk], float(P) ** -0.5, Wt[i][:, 0:nk], ALU.mult, ALU.mult,
                                                 accum_out=dn[i][:, 0:1]), w_, pt_t.get(u - 2), mx_t.get(u - 2))
        pm_t[u] = w_
        free[b] = [w_]
        t = DV(lambda e: e.scalar_tensor_tensor(dn[i][:, 3:4], dn[i][:, 0:1], -1.0, dn[i][:, 0:1], ALU.mult, ALU.max), w_)
        t = DV(lambda e: e.tensor_scalar(dn[i][:, 1:2], dn[i][:, 3:4], gc[:, j, 1, hd:hd + 1], None, ALU.max), t, gc_t)
        t = DV(lambda e: e.reciprocal(dn[i][:, 2:3], dn[i][:, 1:2]), t)
        return t

    def ml_out(u, rden):
        hd, j = munits[u]
        i, b, bo = u % 2, 2 + u % 2, 4 + u % 2
        for k in range(j + 1):
            t = transpose(ps[b][:, k * P:k * P + P], Pm[i][:, k * P:k * P + P], pm_t[u], free[b], sig=k == j)
        pt_t[u] = t
        t = AC(lambda e: e.activation(PT[i][:, 0:j + 1, :].rearrange("p a b -> p (a b)"), ps[b][:, 0:P * (j + 1)], ACT.Copy), t, mx_t.get(u - 2))
        free[b] = [t]
        for k in range(j + 1):
            t2 = mm(ps[bo][:, 0:P], PT[i][:, k, :], vm[:, k, hd * P:hd * P + P], k == 0, k == j, t, vm_t[k], free[bo], sig=k == j)
        mx_t[u] = DV(lambda e: e.scalar_tensor_tensor(mx[:, j, hd * P:hd * P + P], ps[bo][:, 0:P], dn[i][:, 2:3],
                                                      og[:, j, hd * P:hd * P + P], ALU.mult, ALU.mult), t2, rden, og_t[j])
        free[bo] = [mx_t[u]]

    rden = {}
    for u in range(9):
        if u < 8:
            rden[u] = ml_scores(u)
        if u >= 1:
            ml_out(u - 1, rden[u - 1])

    zs = [sb(f"zs{i}", [P, 384], off=o) for i in range(2)]
    ze = [sb(f"ze{i}", [P, 384], off=o) for i in range(2)]
    zl = [sb(f"zl{i}", [P, 384], off=o) for i in range(2)]
    l_t, sb_t, la_t = {}, {}, {}

    def st_logits(hd):
        i, b, tl = hd % 2, hd % 2, hd // 2
        rp = slice(64 * (hd % 2), 64 * (hd % 2) + 64)
        dep = [sq_t[0, tl // 2], sq_t[1, tl // 2]]
        for n, (s_, t_) in enumerate(((0, 0), (1, 1), (0, 1))):
            t = mm(ps[b][:, n * P:n * P + P], ks[rp, tl, s_ * P:s_ * P + P], qs[rp, tl, t_ * P:t_ * P + P], True, True,
                   dep, free[b], sig=n == 2)
        t1 = AC(lambda e: e.activation(zs[i][:, :], ps[b][:, 0:384], ACT.Copy), t, la_t.get(hd - 2))
        free[b] = [t1]
        t = DV(lambda e: e.scalar_tensor_tensor(ze[i][:, :], zs[i][:, :], -1.0, zs[i][:, :], ALU.mult, ALU.max), t1, la_t.get(hd - 2))
        t = AC(lambda e: e.activation(ze[i][:, :], ze[i][:, :], ACT.Exp, scale=-1.0), t)
        t = AC(lambda e: e.activation(ze[i][:, :], ze[i][:, :], ACT.Ln, bias=1.0), t)
        t = DV(lambda e: e.scalar_tensor_tensor(zl[i][:, :], zs[i][:, :], 0.0, ze[i][:, :], ALU.max, ALU.add), t, sb_t.get(hd - 2))
        t = DV(lambda e: e.tensor_tensor(zl[i][:, 0:S], zl[i][:, 0:S], const("keep"), ALU.mult), t)
        t2 = DV(lambda e: e.tensor_tensor(zs[i][:, 0:S], zs[i][:, 0:S], const("sneg"), ALU.add), t)
        l_t[hd] = [t, t2]

    def st_out(hd):
        i, b, bo = hd % 2, 2 + hd % 2, 6 + hd % 2
        mm(ps[b][:, 0:384], const("tri"), zl[i][:, :], True, True, l_t[hd], free[b])
        t = PE(lambda e: e.matmul(ps[b][:, S:384], const("ones"), zl[i][:, P:S], start=False, stop=True, skip_group_check=True), sig=True)
        t = DV(lambda e: e.scalar_tensor_tensor(ze[i][:, :], ps[b][:, 0:384], -1.0, zs[i][:, :], ALU.mult, ALU.add), t, l_t[hd])
        free[b] = [t]
        la_t[hd] = t
        t = AC(lambda e: e.activation(ze[i][:, :], ze[i][:, :], ACT.Exp), t)
        vc = slice(64 * hd, 64 * hd + 64)
        mm(ps[bo][:, 0:64], ze[i][:, 0:P], vs[:, 0, vc], True, True, t, free[bo], vs_t)
        mm(ps[bo][:, 64:P], ze[i][:, S:384], vs[:, 0, vc], True, False)
        t = mm(ps[bo][:, 64:P], ze[i][:, P:S], vs[:, 1, vc], False, True, sig=True)
        la_t[hd] = [la_t[hd], t]
        ov = ps[bo][:, 0:P].rearrange("p (j d) -> p j d", j=2)
        sb_t[hd] = AC(lambda e: e.activation(mx[:, :, 512 + 64 * hd:512 + 64 * hd + 64], ov, ACT.Copy), t)
        free[bo] = [sb_t[hd]]

    for hd in range(9):
        if hd < 8:
            st_logits(hd)
        if hd >= 1:
            st_out(hd - 1)

    s8 = sb("s8b", [P, 2, 3, 8], off=o)
    hg, hg_t = gain("heads")
    every = [mx_t[u] for u in range(8)] + [sb_t[u] for u in range(8)]
    m_t = head_norm(mx, [every, every], xm, [(0, 4, P), (512, 8, 64)], 1e-6, 1.0, hg[:, :], hg_t)
    gain_used("heads", m_t[1])
    xt = turn(mx, m_t, xH, xL)
    r_t = add_rows(rows("wout", 4, xH, xL, xt))

    o = [OM]
    xn = sb("xn", [P, 2, D], off=o)
    xq = sb("xq", [P, KT, S], off=o)
    xk = sb("xk", [P, KT, S], off=o)
    xv = sb("xv", [P, 2, D], off=o)
    pr = [sb(f"pr{i}", [P, S], off=o) for i in range(2)]
    pT = [sb(f"pT{i}", [P, 2, S], off=o) for i in range(2)]
    px = [sb(f"px{i}", [P, 4], off=o) for i in range(2)]
    k_t = {}

    def turned(name, dst, H, L, scale, dep, keep):
        for c in range(4):
            idx, wh, wl, wt = take(name, c)
            b = 4 + c % 4
            cols(b, 0, H, L, wh, wl, 0, [wt, dep])
            t = cols(b, S, H, L, wh, wl, P, [])
            done[idx] = t
            keep[c] = AC(lambda e: e.activation(dst[:, 2 * c:2 * c + 2, :].rearrange("p a t -> p (a t)"), ps[b][:, :], ACT.Copy, scale=scale), t, r_t)
            free[b] = [keep[c]]

    kx_t, qx_t = {}, {}
    n_t = rms(h, r_t, xn, "xattn")
    turned("xk", xk, mH, mL, 1.0, mt, kx_t)
    bt = rows("xv", 4, mH, mL, mt)
    v_t = []
    for j in range(2):
        for e2 in range(2):
            k = 2 * j + e2
            t = AC(lambda e: e.activation(xv[:, j, e2 * 512:e2 * 512 + 512], ps[k][:, :], ACT.Copy), bt[k], r_t)
            free[k] = [t]
            v_t.append(t)
    xt = turn(xn, n_t, xH, xL)
    turned("xq", xq, xH, xL, 1.0 / 16, xt, qx_t)
    xp_t, pT_t, ox_t = {}, {}, []

    def x_scores(hd, j):
        u = 2 * hd + j
        b, i = u % 2, u % 2
        for k in range(2):
            t = mm(ps[b][:, 0:S], xq[:, 2 * hd + k, j * P:j * P + P], xk[:, 2 * hd + k, :], k == 0, k == 1,
                   qx_t[hd], kx_t[hd], free[b], sig=k == 1)
        m = px[i]
        t = DV(lambda e: e.tensor_reduce(m[:, 0:1], ps[b][:, 0:S], AX, ALU.max, negate=True), t, xp_t.get(u - 2))
        t = AC(lambda e: e.activation(pr[i][:, :], ps[b][:, 0:S], ACT.Exp, bias=m[:, 0:1], accum_out=m[:, 1:2]), t, pT_t.get((u - 2, 0)))
        free[b] = [t]
        t = DV(lambda e: e.reciprocal(m[:, 2:3], m[:, 1:2]), t)
        xp_t[u] = DV(lambda e: e.tensor_scalar(pr[i][:, :], pr[i][:, :], m[:, 2:3], None, ALU.mult), t)

    def x_turn(hd, j):
        u = 2 * hd + j
        b, i = 2 + u % 2, u % 2
        for k in range(2):
            t = transpose(ps[b][:, k * P:k * P + P], pr[i][:, k * P:k * P + P], xp_t[u], free[b], sig=k == 1)
        pT_t[u, 0] = t
        pT_t[u, 1] = AC(lambda e: e.activation(pT[hd % 2][:, :, j * P:j * P + P], ps[b][:, 0:S].rearrange("p (k t) -> p k t", k=2), ACT.Copy),
                        t, ox_t[-2] if hd >= 2 else None)
        free[b] = [pT_t[u, 1]]

    def x_out(hd):
        dep = [pT_t[2 * hd, 1], pT_t[2 * hd + 1, 1]]
        for q in range(2):
            b = 4 + (2 * hd + q) % 4
            for k in range(2):
                t = mm(ps[b][:, 0:S], xv[:, k, (2 * hd + q) * P:(2 * hd + q) * P + P], pT[hd % 2][:, k, :], k == 0, k == 1,
                       dep, v_t, free[b], sig=k == 1)
            r = part(xH[:, 2 * hd + q, :], xL[:, 2 * hd + q, :], ps[b][:, 0:S], [t, [qx_t[c] for c in range(4)]])
            free[b] = [r[1]]
            o_parts.extend(r)
        ox_t.append(t)

    o_parts = []
    for hd in range(5):
        if hd < 4:
            x_scores(hd, 0)
            x_scores(hd, 1)
        if hd >= 1:
            x_out(hd - 1)
        if hd < 4:
            x_turn(hd, 0)
            x_turn(hd, 1)
    r_t = add_rows(rows("xo", 4, xH, xL, o_parts))

    o = [OW]
    pn = sb("pn", [P, 2, D], off=o)
    qH = sb("qH", [P, 16, S], F32R, off=o)
    qL = sb("qL", [P, 16, S], F32R, off=o)
    n_t = rms(h, r_t, pn, "ffn")
    xt = turn(pn, n_t, xH, xL)
    q_t = []
    for c in range(8):
        idx, wh, wl, wt = take("pq", c)
        b = 4 + c % 4
        cols(b, 0, xH, xL, wh, wl, 0, [wt, xt])
        t = cols(b, S, xH, xL, wh, wl, P, [])
        done[idx] = t
        r = part(qH[:, 2 * c:2 * c + 2, :].rearrange("p a t -> p (a t)"), qL[:, 2 * c:2 * c + 2, :].rearrange("p a t -> p (a t)"),
                 ps[b][:, :], t)
        free[b] = [r[1]]
        q_t += r

    o = [OW]
    G = [sb(f"G{i}", [P, NQ, S], off=o) for i in range(2)]
    AB = o[0]
    ga = [sb(f"ga{i}", [P, S], off=o) for i in range(2)]
    gH = [sb(f"gH{i}", [P, S], F32R, off=o) for i in range(2)]
    gL = [sb(f"gL{i}", [P, S], F32R, off=o) for i in range(2)]
    i1T = sb("i1T", [P, S], off=o)
    i2T = sb("i2T", [P, S], off=o)
    gT = sb("gT", [P, S], off=o)
    oB = sb("oB", [P, 8, P], off=o)
    oA = [sb(f"oA{i}", [P, 8, NQ], off=o) for i in range(2)]
    o = [OW + 8192 + 32768]
    sc = sb("sc", [P, 16, P], off=o)
    wk = [sb(f"wk{i}", [P, S], off=o) for i in range(2)]
    ti = sb("ti", [P, 16, 16], U32, off=o)
    tf = sb("tf", [P, 16, 16], off=o)
    tv = sb("tv", [P, 16, 16], off=o)
    cand = sb("cand", [P, 8, S], off=[OW])
    bv = sb("bv", [P, 8, 16], off=o)
    bp = sb("bp", [P, 8, 16], U32, off=o)
    bq = [sb(f"bq{i}", [P, 8, 16], U32, off=o) for i in range(2)]
    bf = [sb(f"bf{i}", [P, 8, 16], off=o) for i in range(2)]
    ei = [sb(f"ei{i}", [P, 8, 16], off=o) for i in range(2)]
    gs = sb("gs", [P, 8, 2], off=o)
    eq = sb("eq", [P, P, 16], off=o)
    assert o[0] <= AB + 6 * 1024

    idx, wh, wl, wt = take("sk", 0)
    prev = None
    sel_t = []
    NEG = -3.0e38
    for j in range(2):
        st = {}
        for q in range(4):
            b = 4 * (j % 2) + q
            for i in range(4):
                hp = 4 * q + i
                ov = ps[b][:, i * P:i * P + P]
                ts = slice(j * P, j * P + P)
                kc = slice(hp * P, hp * P + P)
                mm(ov, qH[:, hp, ts], wh[:, kc], True, False, wt, q_t, free[b])
                mm(ov, qH[:, hp, ts], wl[:, kc], False, False)
                t = mm(ov, qL[:, hp, ts], wh[:, kc], False, True, sig=i == 3)
            st[q] = AC(lambda e: e.activation(sc[:, 4 * q:4 * q + 4, :].rearrange("p a b -> p (a b)"), ps[b][:, :], ACT.Copy), t, prev)
            free[b] = [st[q]]
        if j == 1:
            done[idx] = t
            pe_q = t
        last = prev
        for hp in range(16):
            row = sc[:, hp, :]
            w_ = wk[hp % 2][:, 0:P]
            t = DV(lambda e: e.max(tv[:, hp, 0:8], row), st[hp // 4], prev)
            i1 = DV(lambda e: e.max_index(ti[:, hp, 0:8], tv[:, hp, 0:8], row), t)
            t = DV(lambda e: e.match_replace(w_, tv[:, hp, 0:8], row, NEG), t)
            t = DV(lambda e: e.max(tv[:, hp, 8:16], w_), t)
            last = DV(lambda e: e.max_index(ti[:, hp, 8:16], tv[:, hp, 8:16], w_), t)
        tf_t = DV(lambda e: e.tensor_copy(tf[:, :, :], ti[:, :, :]), last, i1)
        s1 = tv[:, :, :].rearrange("p (h c) k -> p h c k", c=2)
        cv = cand[:, :, :].rearrange("p h (a b) -> p h a b", a=16)
        c_t = []
        for hd in range(8):
            c_t.append(DV(lambda e: e.tensor_tensor(cv[:, hd, :, :], s1[:, hd, 0, :].unsqueeze(2).broadcast_to([P, 16, 16]),
                                                    s1[:, hd, 1, :].unsqueeze(1).broadcast_to([P, 16, 16]), ALU.add), last, q_t, prev))
        for hd in range(8):
            row = cand[:, hd, :]
            w_ = wk[hd % 2][:, :]
            t = DV(lambda e: e.max(bv[:, hd, 0:8], row), c_t[hd])
            DV(lambda e: e.max_index(bp[:, hd, 0:8], bv[:, hd, 0:8], row), t)
            t = DV(lambda e: e.match_replace(w_, bv[:, hd, 0:8], row, NEG), t)
            t = DV(lambda e: e.max(bv[:, hd, 8:16], w_), t)
            last = DV(lambda e: e.max_index(bp[:, hd, 8:16], bv[:, hd, 8:16], w_), t)
        t = DV(lambda e: e.tensor_tensor(ei[0][:, :, :], bv[:, :, :], bv[:, :, 0:1].broadcast_to([P, 8, 16]), ALU.subtract), last)
        t = AC(lambda e: e.activation(ei[0][:, :, :], ei[0][:, :, :], ACT.Exp), t)
        t = DV(lambda e: e.reduce_sum(gs[:, :, 0], ei[0][:, :, :], AX), t)
        t = DV(lambda e: e.reciprocal(gs[:, :, 1], gs[:, :, 0]), t)
        g_t = DV(lambda e: e.tensor_tensor(bv[:, :, :], ei[0][:, :, :], gs[:, :, 1:2].broadcast_to([P, 8, 16]), ALU.mult), t)
        u0 = DV(lambda e: e.tensor_scalar(bq[0][:, :, :], bp[:, :, :], 4, None, ALU.logical_shift_right), last)
        u1 = DV(lambda e: e.tensor_scalar(bq[1][:, :, :], bp[:, :, :], 15, None, ALU.bitwise_and), last)
        u_t = [DV(lambda e, i=i: e.tensor_copy(bf[i][:, :, :], bq[i][:, :, :]), u0, u1) for i in range(2)]
        e_t = []
        tfv = tf[:, :, :].rearrange("p (h c) k -> p h c k", c=2)
        for i in range(2):
            t = DV(lambda e: e.tensor_tensor(eq[:, :, :], bf[i][:, :, :].rearrange("p a b -> p (a b)").unsqueeze(2).broadcast_to([P, P, 16]),
                                             iota[:, 0:16].unsqueeze(1).broadcast_to([P, P, 16]), ALU.is_equal), u_t[i], e_t[-1:], id_t)
            t = DV(lambda e: e.tensor_tensor(eq[:, :, :].rearrange("p (h k) a -> p h k a", h=8), eq[:, :, :].rearrange("p (h k) a -> p h k a", h=8),
                                             tfv[:, :, i, :].unsqueeze(2).broadcast_to([P, 8, 16, 16]), ALU.mult), t, tf_t)
            e_t.append(DV(lambda e: e.reduce_sum(ei[i][:, :, :].rearrange("p a b -> p (a b)"), eq[:, :, :], AX), t, g_t))
        b = 0 if j == 0 else 4
        for i, (src, tk) in enumerate(((ei[0], e_t[0]), (ei[1], e_t[1]), (bv, g_t))):
            t = transpose(ps[b][:, i * P:i * P + P], src[:, :, :].rearrange("p a b -> p (a b)"), tk, free[b], sig=i == 2)
        prev = t
        for i, dst in enumerate((i1T, i2T, gT)):
            t = AC(lambda e: e.activation(dst[:, j * P:j * P + P], ps[b][:, i * P:i * P + P], ACT.Copy), t)
        free[b] = [t]
        sel_t.append(t)

    ab_t, G_t, G_use = {}, {}, {}
    nb = [0]

    def gates(q, bt):
        n = nb[0]
        nb[0] += 1
        b, i = 6 + n % 2, n % 2
        tk = sel_t[0] if bt < 16 else sel_t[1]
        for m in range(8):
            t = 8 * bt + m
            DV(lambda e: e.tensor_scalar(oB[:, m, :], iota[:, :], i2T[:, t:t + 1], None, ALU.is_equal), tk, ab_t.get(n - 1), prev)
            ts = DV(lambda e: e.tensor_scalar(oA[i][:, m, :], iota[:, q * NQ:q * NQ + NQ], i1T[:, t:t + 1], gT[:, t:t + 1],
                                              ALU.is_equal, ALU.mult), tk, ab_t.get(n - 2))
            tm = mm(ps[b][:, m * NQ:m * NQ + NQ], oB[:, m, :], oA[i][:, m, :], True, True, ts, free[b], sig=m == 7)
        ab_t[n] = tm
        G_t[q, bt] = AC(lambda e: e.activation(G[q % 2][:, :, 8 * bt:8 * bt + 8], ps[b][:, 0:8 * NQ].rearrange("p (t i) -> p i t", t=8), ACT.Copy),
                        tm, G_use.get(q - 2), sel_t)
        free[b] = [G_t[q, bt]]

    split(nuse[0] + NS - 1)
    for bt in range(32):
        gates(0, bt)

    taken, gel, act_t = {}, {}, {}
    y_last = {}

    def ex_in(i):
        taken[i] = take("ex", i, NS - 1)
        idx, wh, wl, wt = taken[i]
        b = 4 + i % 2
        ov = ps[b][:, 0:S]
        for k in range(KT):
            kc = slice(k * P, k * P + P)
            mm(ov, wh[:, kc], xH[:, k, :], k == 0, False, wt, free[b], xt)
            mm(ov, wh[:, kc], xL[:, k, :], False, False)
            t = mm(ov, wl[:, kc], xH[:, k, :], False, k == KT - 1, sig=k == KT - 1)
        t = AC(lambda e: e.activation(ga[i % 2][:, :], ov, ACT.Gelu), t, act_t.get(i - 2))
        free[b] = [t]
        q = i // NQ
        t = DV(lambda e: e.tensor_tensor(ga[i % 2][:, :], ga[i % 2][:, :], G[q % 2][:, i % NQ, :], ALU.mult), t, G_t[q, 31])
        if i % NQ == NQ - 1:
            G_use[q] = t
        t1 = AC(lambda e: e.activation(gH[i % 2][:, :], ga[i % 2][:, :], ACT.Copy), t, y_last.get(i - 2))
        t2 = DV(lambda e: e.tensor_tensor(gL[i % 2][:, :], ga[i % 2][:, :], gH[i % 2][:, :].bitcast(F32), ALU.subtract), t1, y_last.get(i - 2))
        act_t[i] = [t1, t2]

    def ex_out(i):
        idx, wh, wl, wt = taken[i]
        for t in range(2):
            ts = slice(t * P, t * P + P)
            for part_, (l, w) in enumerate(((gH, wh), (gH, wl), (gL, wh))):
                for e2 in range(2):
                    b = 2 * t + e2
                    w0 = D + e2 * 512
                    last = i == P - 1 and part_ == 2
                    tok = mm(ps[b][:, :], l[i % 2][:, ts], w[:, w0:w0 + 512], i == 0 and part_ == 0, last,
                             act_t[i], wt, free[b] if i == 0 else None,
                             sig=last or (t == 1 and part_ == 2 and e2 == 1))
                    if last:
                        free[b] = [tok]
        done[idx] = tok
        y_last[i] = tok

    for i in range(P + 1):
        if i < P:
            ex_in(i)
        if i >= 1:
            ex_out(i - 1)
            split(nuse[0] - 1 + NS)
        if i // NQ + 1 < P // NQ:
            gates(i // NQ + 1, i % NQ)
    r_t = add_rows([free[b][0] for b in range(4)])
    f_t = rms(h, r_t, pn, "final", after=r_t)
    for j in range(2):
        SP.dma(lambda e, j=j: e.dma_start(out[j], pn[:, j, :]), s_out, 16 * (j + 1), f_t[j])
    SP.wait((s_out, 32))
    assert nuse[0] == len(STREAM)


def constants():
    c = np.zeros((P, CWID), np.float32)
    pos = np.arange(S, dtype=np.float32)
    inv = (np.float32(500000.0) ** (-np.arange(0, 16, 2, dtype=np.float32) / np.float32(16))).astype(np.float32)
    ang = pos[:, None] * inv[None, :]
    p, f = np.arange(P)[:, None], np.arange(S)[None, :]
    for j in range(2):
        for name, fn in (("cos", np.cos), ("sin", np.sin)):
            c0 = CC[name][0] + j * P
            c[:, c0:c0 + P] = np.tile(fn(ang[j * P:j * P + P]).astype(np.float32), (1, 16))
        c0 = CC["amask"][0] + j * S
        c[:, c0:c0 + S] = np.where(f // 64 <= (j * P + p) // 64, 0.0, -1e30)
        c0 = CC["cmask"][0] + j * S
        c[:, c0:c0 + S] = np.where(f <= j * P + p, 0.0, -1e30)
        g = np.arange(P)[None, :]
        c0 = CC["keep"][0] + j * P
        c[:, c0:c0 + P] = np.where(p < g, 1.0, 0.0)
        c0 = CC["sneg"][0] + j * P
        c[:, c0:c0 + P] = np.where(p < g, 0.0, -1e30)
    c0 = CC["tri"][0]
    c[:, c0:c0 + P] = np.where(p >= np.arange(P)[None, :], 1.0, 0.0)
    c0 = CC["ones"][0]
    c[:, c0:c0 + P] = 1.0
    sel = np.zeros((4, 4, P), np.float32)
    for k in range(4):
        sel[k, k, :] = 1.0
    return {"consts": c, "ident": np.eye(P, dtype=np.float32),
            "iota": np.tile(np.arange(P, dtype=np.float32)[None, :], (P, 1)), "sel": sel}


def layout(v):
    def side(w, n):
        e = w.shape[1] // n
        return w.reshape(KT, P, e, n).transpose(2, 1, 0, 3).reshape(e, P, KT * n)

    def deep(w, kk):
        c = w.shape[0] // (P * kk)
        return w.reshape(c, kk, P, w.shape[1]).transpose(0, 2, 1, 3).reshape(c, P, kk * w.shape[1])

    def block(w):
        b = w.shape[1] // 512
        return w.reshape(2, 4, P, b, 512).transpose(3, 0, 2, 1, 4).reshape(2 * b, P, CW)

    def pair(x, y):
        return np.stack([x.reshape(D, -1, P), y.reshape(D, -1, P)], 2).reshape(D, -1)

    def rows2(x):
        return x.reshape(2, P, D).transpose(1, 0, 2)

    out = constants()
    out["x"] = rows2(v["x"][0])
    out["mem"] = rows2(v["mem_2"][0])
    out["qkv"] = block(v["attn_w_qkv"][0])
    out["wo"] = deep(v["attn_w_o"][0], 2)
    for i in range(2):
        out[f"gu{i}"] = side(pair(v["ffn_w_gate"][i], v["ffn_w_up"][i]), 256)
        out[f"dn{i}"] = deep(v["ffn_w_down"][i], 2)
    ci = v["conv_w_in"][0]
    out["cin"] = np.concatenate([side(pair(ci[:, D:2 * D], ci[:, 2 * D:]), 256), side(ci[:, :D], 256)])
    out["cout"] = deep(v["conv_w_out"][0], 2)
    wi = v["w_in_2"][0]
    out["win"] = np.concatenate([side(wi[:, 0:1024], 256), block(wi[:, 1024:1536]), block(wi[:, 1536:2048]),
                                 side(wi[:, 2056:2568], 256), side(wi[:, 2568:3080], 256), block(wi[:, 3080:3592])])
    out["gatew"] = wi[:, 2048:2056].reshape(KT, P, 8).transpose(1, 0, 2)
    out["gateb"] = np.stack([v["igate_b_2"][0], v["fgate_b_2"][0]], 1)
    out["wout"] = deep(v["w_out_2"][0], 2)
    out["xk"] = side(v["xattn_wkv_2"][0][:, :D], 256)
    out["xv"] = deep(v["xattn_wkv_2"][0][:, D:], 2)
    out["xq"] = side(v["xattn_wq_2"][0], 256)
    out["xo"] = deep(v["xattn_wo_2"][0], 2)
    out["pq"] = side(v["peer_wq_2"][0], 256)
    out["sk"] = v["peer_subkeys_2"][0].reshape(16, P, P).transpose(2, 0, 1).reshape(1, P, CW)
    u = v["peer_u_2"][0].reshape(P, P, KT, P).transpose(0, 3, 2, 1).reshape(P, P, D)
    out["ex"] = np.concatenate([u, v["peer_v_2"][0].reshape(P, P, D)], 2)
    out["convw"] = v["conv_w"][0].reshape(3, KT, P).transpose(2, 1, 0)
    c4 = np.concatenate([v["conv_w_2"][0], v["conv_b_2"]], 0)
    out["conv4"] = c4.reshape(5, 8, P).transpose(2, 1, 0)
    out["lam"] = np.concatenate([v["attn_lambda_q1"], v["attn_lambda_q2"], v["attn_lambda_k1"], v["attn_lambda_k2"]], 1)
    out["subg"] = v["attn_subln_g"]
    rows = {"ln1g0": v["ln1_g"][0], "ln1b0": v["ln1_b"][0], "ln2g0": v["ln2_g"][0], "ln2b0": v["ln2_b"][0],
            "ln1g1": v["ln1_g"][1], "ln1b1": v["ln1_b"][1], "ln2g1": v["ln2_g"][1], "ln2b1": v["ln2_b"][1],
            "mem": v["mem_norm_g_2"][0], "mix": v["mix_norm_g_2"][0],
            "heads": np.concatenate([v["mlstm_norm_g_2"][0], v["sb_norm_g_2"][0]]),
            "xattn": v["xattn_norm_g_2"][0], "ffn": v["ffn_norm_g_2"][0], "final": v["final_norm_g_2"]}
    out["gains"] = np.stack([rows[n] for n in GAINS])
    return {k: np.ascontiguousarray(x) for k, x in out.items()}


def kernel(**inputs):
    from contextlib import ExitStack

    import concourse.bacc as bacc
    from concourse.bass_utils import run_bass_kernel_spmd

    nc = bacc.Bacc("TRN2", target_bir_lowering=False, num_devices=1)
    arrays = layout({k: np.asarray(x) for k, x in inputs.items()})
    aps = {k: nc.dram_tensor("in_" + k, list(x.shape), F32, kind="ExternalInput").ap() for k, x in arrays.items()}
    out = nc.dram_tensor("out_0", [2, P, D], F32, kind="ExternalOutput").ap()
    with ExitStack() as ctx:
        build(nc, aps, out, ctx)
    r = run_bass_kernel_spmd(nc, [{"in_" + k: x for k, x in arrays.items()}], core_ids=[0])
    return np.asarray(r.results[0]["out_0"]).reshape(1, S, D)
```

```python
import numpy as np

import concourse.bass as bass
from concourse import mybir
from concourse.alu_op_type import AluOpType as ALU

F32 = mybir.dt.float32
BF16 = mybir.dt.bfloat16
F32R = mybir.dt.float32r
U32 = mybir.dt.uint32
ACT = mybir.ActivationFunctionType
AX = mybir.AxisListType.X

P = 128
D = 1024
KT = D // P
S = 256
FT = 22
CW = 2048
NR = 3
NS = 3
NG = 4
UW = 1024
UR = 4
US = 3
ALPHA = 4.0 ** 0.25
LAM0 = 0.2
BASE = 16512

GAINS = ["ln1g0", "ln1b0", "ln2g0", "ln2b0", "ln1g1", "ln1b1", "ln2g1", "ln2b1",
         "mem", "mix", "heads", "xattn", "ffn"]
STREAM = ([("qkv", i) for i in range(12)] + [("wo", i) for i in range(4)]
          + [("gu0", i) for i in range(FT)] + [("dn0", i) for i in range(FT // 2)]
          + [("cin", i) for i in range(12)] + [("cout", i) for i in range(4)]
          + [("gu1", i) for i in range(FT)] + [("dn1", i) for i in range(FT // 2)]
          + [("win", i) for i in range(14)] + [("wout", i) for i in range(4)]
          + [("xk", i) for i in range(4)] + [("xv", i) for i in range(4)]
          + [("xq", i) for i in range(4)] + [("xo", i) for i in range(4)]
          + [("pq", i) for i in range(8)] + [("sk", 0)])
CC = {"cos": (0, 256), "sin": (256, 256), "amask": (512, 512), "cmask": (1024, 512),
      "keep": (1536, 256), "sneg": (1792, 256), "tri": (2048, 128), "ones": (2176, 128)}
CWID = 2304


def flat(items):
    out = []
    for x in items:
        if x is None:
            continue
        if len(x) == 2 and isinstance(x[1], int):
            out.append(x)
        else:
            out += flat(x)
    return out


class Lane:

    def __init__(self, eng, sem, turn=False):
        self.eng, self.sem, self.count, self.seen, self.turn = eng, sem, 0, {}, turn

    def wait(self, *after):
        for sem, value in flat(after):
            if self.seen.get(sem.name, 0) < value:
                self.seen[sem.name] = value
                self.eng.wait_ge(sem, value)

    def __call__(self, fn, *after, sig=True):
        self.wait(after, [(self.sem, self.count - 1)] if self.turn else None)
        r = fn(self.eng)
        if not sig:
            return None
        r.then_inc(self.sem, 1)
        self.count += 1
        return (self.sem, self.count)

    def dma(self, fn, sem, total, *after):
        self.wait(after)
        fn(self.eng).then_inc(sem, 16)
        return (sem, total)


def build(nc, a, out, ctx):
    def sem(name):
        return ctx.enter_context(nc.semaphore(name))

    at = [BASE]

    def sb(name, shape, dt=F32, off=None):
        size = int(np.prod(shape[1:])) * (2 if dt == BF16 else 4)
        size = -(-size // 32) * 32
        if off is None:
            off = at[0]
            at[0] += size
        else:
            o = off[0]
            off[0] += size
            assert off[0] <= nc.sbuf_usable_end, (name, off[0], nc.sbuf_usable_end)
            off = o
        return nc.alloc_sbuf_tensor_at(name, list(shape), dt, offset=off)

    PE, AC, DV, GP, SP = (Lane(e, sem(n), t) for e, n, t in (
        (nc.tensor, "s_pe", False), (nc.scalar, "s_act", True), (nc.vector, "s_dve", True),
        (nc.gpsimd, "s_pool", False), (nc.sync, "s_sp", False)))

    banks = ctx.enter_context(nc.psum_tensor("banks", [P, 8, 512], F32))
    ps = [banks[:, i, :] for i in range(8)]
    free = [[] for _ in range(8)]

    raw = [sb(f"raw{i}", [P, CW]) for i in range(2)]
    xH = sb("xH", [P, KT, S], F32R)
    xL = sb("xL", [P, KT, S], F32R)
    ident = sb("ident", [P, P])
    iota = sb("iota", [P, P])
    stat = sb("stat", [P, 2, 2, 6])
    mv = sb("mv", [P, 2, 2])
    rs = sb("rs", [P, 2, 2])
    lamv = sb("lamv", [P, 8])
    OX = at[0]
    raw += [sb("raw2", [P, CW])]
    wH = [sb(f"wH{i}", [P, CW], F32R) for i in range(NS)]
    wL = [sb(f"wL{i}", [P, CW], F32R) for i in range(NS)]
    h = sb("h", [P, 2, D])
    gn = [sb(f"gn{i}", [P, D]) for i in range(NG)]
    OV = at[0]

    s_raw = [sem(f"s_raw{i}") for i in range(NR)]
    s_gn = [sem(f"s_gn{i}") for i in range(NG)]
    s_x, s_id, s_cst, s_lam, s_sub, s_mem, s_cw, s_c4, s_gw, s_gb = (
        sem(n) for n in ("s_x", "s_id", "s_cst", "s_lam", "s_sub", "s_mem", "s_cw", "s_c4", "s_gw", "s_gb"))
    s_out, s_hs, s_gl = sem("s_out"), sem("s_hs"), sem("s_gl")
    hs = nc.dram_tensor("h_scratch", [P, 2, D], F32).ap()
    gel = nc.dram_tensor("gelu_scratch", [P, P, S], F32).ap()

    x_t = SP.dma(lambda e: e.dma_start(h[:, :, :], a["x"]), s_x, 16)
    SP.dma(lambda e: e.dma_start(ident[:, :], a["ident"]), s_id, 16)
    id_t = SP.dma(lambda e: e.dma_start(iota[:, :], a["iota"]), s_id, 32)

    split_a, split_v, done, raw_t = {}, {}, {}, {}

    def fetch(n):
        if n >= len(STREAM):
            return
        name, i = STREAM[n]
        r = n % NR
        raw_t[n] = SP.dma(lambda e: e.dma_start(raw[r][:, :], a[name][i]), s_raw[r], 16 * (n // NR + 1),
                          split_a.get(n - NR), split_v.get(n - NR))

    nsplit = [0]

    def split(upto):
        while nsplit[0] < min(upto, len(STREAM)):
            n = nsplit[0]
            r, s = n % NR, n % NS
            split_a[n] = AC(lambda e: e.activation(wH[s][:, :], raw[r][:, :], ACT.Copy), raw_t[n], done[n - NS] if n >= NS else None)
            split_v[n] = DV(lambda e: e.tensor_tensor(wL[s][:, :], raw[r][:, :], wH[s][:, :].bitcast(F32), ALU.subtract),
                            split_a[n], done[n - NS] if n >= NS else None)
            fetch(n + NR)
            nsplit[0] += 1

    nuse = [0]

    def take(name, i, ahead=NS):
        n = nuse[0]
        assert STREAM[n] == (name, i), (STREAM[n], name, i)
        nuse[0] += 1
        split(n + ahead)
        return n, wH[n % NS], wL[n % NS], [split_a[n], split_v[n]]

    gain_t, gain_use = {}, {}

    def load_gain(n):
        if n >= len(GAINS):
            return
        g = n % NG
        gain_t[n] = GP.dma(lambda e: e.dma_start(gn[g][:, :], a["gains"][n:n + 1, :].broadcast_to([P, D])),
                           s_gn[g], 16 * (n // NG + 1), gain_use.get(n - NG))

    def gain(name):
        n = GAINS.index(name)
        return gn[n % NG], gain_t[n]

    def gain_used(name, tok):
        n = GAINS.index(name)
        gain_use[n] = tok
        load_gain(n + NG)

    for n in range(NR):
        fetch(n)
    for n in range(NG):
        load_gain(n)

    def mm(o, l, r, start, stop, *after, sig=False):
        return PE(lambda e: e.matmul(o, l, r, start=start, stop=stop), *after, sig=sig)

    def transpose(o, i, *after, sig=False):
        k = i.shape[0]
        return PE(lambda e: e.transpose(o, i, ident[:k, :k]), *after, sig=sig)

    def cols(bank, off, H, L, wh, wl, wcol, after):
        for k in range(KT):
            w0 = k * 256 + wcol
            o = ps[bank][:, off:off + S]
            first = (after, free[bank]) if k == 0 else ()
            mm(o, wh[:, w0:w0 + P], H[:, k, :], k == 0, False, *first)
            mm(o, wh[:, w0:w0 + P], L[:, k, :], False, False)
            t = mm(o, wl[:, w0:w0 + P], H[:, k, :], False, k == KT - 1, sig=k == KT - 1)
        return t

    def rows(name, n, H, L, after):
        for c in range(n):
            idx, wh, wl, wt = take(name, c)
            for kk in range(2):
                k = 2 * c + kk
                for t in range(2):
                    ts = slice(t * P, t * P + P)
                    for part, (l, w) in enumerate(((H, wh), (H, wl), (L, wh))):
                        for e in range(2):
                            b = 2 * t + e
                            w0 = kk * D + e * 512
                            lastk = k == 2 * n - 1 and part == 2
                            first = (after, wt, free[b]) if c == 0 and kk == 0 else (wt,)
                            tok = mm(ps[b][:, :], l[:, k, ts], w[:, w0:w0 + 512], k == 0 and part == 0, lastk,
                                     *first, sig=(kk == 1 and t == 1 and part == 2 and e == 1) or lastk)
                            if lastk:
                                free[b] = [tok]
            done[idx] = tok
        return [free[b][0] for b in range(4)]

    def blocks(name, c0, H, L, bank, after):
        for c in range(2):
            idx, wh, wl, wt = take(name, c0 + c)
            for kk in range(4):
                k = 4 * c + kk
                for t in range(2):
                    ts = slice(t * P, t * P + P)
                    for part, (l, w) in enumerate(((H, wh), (H, wl), (L, wh))):
                        last = k == KT - 1 and part == 2
                        tok = mm(ps[bank + t][:, :], l[:, k, ts], w[:, kk * 512:kk * 512 + 512], k == 0 and part == 0,
                                 last, after, wt, free[bank + t] if k == 0 else None,
                                 sig=last or (kk == 3 and t == 1 and part == 2))
                        if last:
                            free[bank + t] = [tok]
            done[idx] = tok
        return [free[bank][0], free[bank + 1][0]]

    def part(dH, dL, src, after, scale=None):
        if scale is None:
            t1 = AC(lambda e: e.activation(dH, src, ACT.Copy), after)
        else:
            t1 = AC(lambda e: e.activation(dH, src, ACT.Copy, scale=scale), after)
        t2 = DV(lambda e: e.tensor_tensor(dL, src, dH.bitcast(F32), ALU.subtract), t1, after)
        return [t1, t2]

    def turn(nat, toks, H, L, after=None, banks=(4, 5, 6, 7)):
        out_t = []
        n = 0
        for j in range(2):
            for q in range(2):
                b = banks[n % len(banks)]
                n += 1
                for i in range(4):
                    k = 4 * q + i
                    t = transpose(ps[b][:, i * P:i * P + P], nat[:, j, k * P:k * P + P],
                                  toks[j], free[b], id_t, sig=i == 3)
                src = ps[b][:, :].rearrange("p (k t) -> p k t", k=4)
                r = part(H[:, 4 * q:4 * q + 4, j * P:j * P + P], L[:, 4 * q:4 * q + 4, j * P:j * P + P], src, [t, after])
                free[b] = [r[1]]
                out_t += r
        return out_t

    def root(j, src, mul, eps, after):
        t = DV(lambda e: e.tensor_scalar(rs[:, j, 0:1], src, mul, eps, ALU.mult, ALU.add), after)
        t = AC(lambda e: e.activation(rs[:, j, 0:1], rs[:, j, 0:1], ACT.Sqrt), t)
        return DV(lambda e: e.reciprocal(rs[:, j, 1:2], rs[:, j, 0:1]), t)

    def add_norm(banks_t, g, b):
        (gw, gt), (bw, bt) = gain(g), gain(b)
        res = []
        for j in range(2):
            for e2 in range(2):
                k = 2 * j + e2
                hv = h[:, j, e2 * 512:e2 * 512 + 512]
                t = DV(lambda e: e.scalar_tensor_tensor(hv, hv, ALPHA, ps[k][:, :], ALU.mult, ALU.add), banks_t[k])
                free[k] = [t]
                t = DV(lambda e: e.bn_stats(stat[:, j, e2, :], hv), t)
            t = DV(lambda e: e.bn_aggr(mv[:, j, :], stat[:, j, :, :].rearrange("p a b -> p (a b)")), t)
            t = root(j, mv[:, j, 1:2], 1.0, 1e-5, t)
            t0 = DV(lambda e: e.scalar_tensor_tensor(h[:, j, :], h[:, j, :], mv[:, j, 0:1], gw[:, :], ALU.subtract, ALU.mult), t, gt)
            res.append(DV(lambda e: e.scalar_tensor_tensor(h[:, j, :], h[:, j, :], rs[:, j, 1:2], bw[:, :], ALU.mult, ALU.add), t0, t, bt))
        gain_used(g, res[1])
        gain_used(b, res[1])
        return res

    def rms(src, toks, nat, g, after=None):
        gw, gt = gain(g)
        res = []
        for j in range(2):
            t = AC(lambda e: e.activation(nat[:, j, :], src[:, j, :], ACT.Square, accum_out=mv[:, j, 0:1]), toks[j], after)
            t = root(j, mv[:, j, 0:1], 1.0 / D, 1e-6, t)
            res.append(DV(lambda e: e.scalar_tensor_tensor(nat[:, j, :], src[:, j, :], rs[:, j, 1:2], gw[:, :], ALU.mult, ALU.mult), t, gt))
        gain_used(g, res[1])
        return res

    def add_rows(banks_t):
        res = []
        for j in range(2):
            for e2 in range(2):
                k = 2 * j + e2
                hv = h[:, j, e2 * 512:e2 * 512 + 512]
                t = DV(lambda e: e.tensor_tensor(hv, hv, ps[k][:, :], ALU.add), banks_t[k])
                free[k] = [t]
            res.append(t)
        return res

    o = [OV]
    cst = sb("cst", [P, CWID], off=o)
    OW = o[0]

    def const(name):
        c0, n = CC[name]
        return cst[:, c0:c0 + n]

    QK = sb("QK", [P, 2, 2048], off=o)
    V = sb("V", [P, 2, D], off=o)
    QT = sb("QT", [P, 8, S], off=o)
    KTt = sb("KT", [P, 8, S], off=o)
    O = sb("O", [P, 2, D], off=o)
    lq = sb("lq", [P, 4, 64], off=o)
    lpr = sb("lpr", [P, 2, 64], off=o)
    sub = sb("sub", [P, P], off=o)
    rot = sb("rot", [P, 4, P], off=o)
    Sm = [sb(f"Sm{i}", [P, 2, S], off=o) for i in range(2)]
    Am = [sb(f"Am{i}", [P, S], off=o) for i in range(2)]
    AT = [sb(f"AT{i}", [P, 2, P], off=o) for i in range(2)]
    sm = [sb(f"sm{i}", [P, 8], off=o) for i in range(2)]
    s8 = sb("s8", [P, 2, 3, 8], off=o)

    cst_t = SP.dma(lambda e: e.dma_start(cst[:, :], a["consts"]), s_cst, 16)
    lam_t = SP.dma(lambda e: e.dma_start(lq[:, :, :].rearrange("p a b -> p (a b)"), a["lam"].broadcast_to([P, 256])), s_lam, 16)
    sub_t = SP.dma(lambda e: e.dma_start(sub[:, :], a["subg"].broadcast_to([P, P])), s_sub, 16)

    xt = turn(h, [x_t, x_t], xH, xL)

    t = DV(lambda e: e.tensor_tensor(lpr[:, :, :], lq[:, 0:2, :], lq[:, 2:4, :], ALU.mult), lam_t)
    t = DV(lambda e: e.reduce_sum(lamv[:, 0:2], lpr[:, :, :], AX), t)
    t = AC(lambda e: e.activation(lamv[:, 2:4], lamv[:, 0:2], ACT.Exp), t)
    t = DV(lambda e: e.tensor_tensor(lamv[:, 4:5], lamv[:, 3:4], lamv[:, 2:3], ALU.subtract), t)
    nlam_t = DV(lambda e: e.tensor_scalar(lamv[:, 5:6], lamv[:, 4:5], LAM0, None, ALU.subtract), t)

    qk_t = {}
    for blk in range(6):
        bank = 2 * (blk % 2)
        bt = blocks("qkv", 2 * blk, xH, xL, bank, xt if blk == 0 else None)
        for j in range(2):
            if blk < 4:
                dst, sc = QK[:, j, blk * 512:blk * 512 + 512], (0.125 if blk < 2 else 1.0)
            else:
                dst, sc = V[:, j, (blk - 4) * 512:(blk - 4) * 512 + 512], 1.0
            t = AC(lambda e: e.activation(dst, ps[bank + j][:, :], ACT.Copy, scale=sc), bt[j])
            free[bank + j] = [t]
            qk_t[blk, j] = t

    T_t = {}
    for w in range(2):
        for j in range(2):
            z = QK[:, j, w * D:w * D + D].rearrange("p (g d) -> p g d", d=64)
            x1, x2 = z[:, :, 0:8], z[:, :, 8:16]
            c = const("cos")[:, j * P:j * P + P].rearrange("p (g d) -> p g d", d=8)
            s = const("sin")[:, j * P:j * P + P].rearrange("p (g d) -> p g d", d=8)
            r = [rot[:, i, :].rearrange("p (g d) -> p g d", d=8) for i in range(4)]
            dep = [qk_t[2 * w, j], qk_t[2 * w + 1, j], cst_t]
            m = [DV(lambda e, q=q, u=u, v=v: e.tensor_tensor(r[q], u, v, ALU.mult), dep)
                 for q, u, v in ((0, x1, c), (1, x2, s), (2, x2, c), (3, x1, s))]
            DV(lambda e: e.tensor_tensor(x1, r[0], r[1], ALU.subtract), m)
            t = DV(lambda e: e.tensor_tensor(x2, r[2], r[3], ALU.add), m)
            dst = QT if w == 0 else KTt
            for q in range(2):
                b = 4 + (4 * w + 2 * j + q) % 4
                for i in range(4):
                    hd = 4 * q + i
                    tt = transpose(ps[b][:, i * P:i * P + P], QK[:, j, w * D + hd * P:w * D + hd * P + P], t, dep, free[b], sig=i == 3)
                src = ps[b][:, :].rearrange("p (k t) -> p k t", k=4)
                T_t[w, j, q] = AC(lambda e: e.activation(dst[:, 4 * q:4 * q + 4, j * P:j * P + P], src, ACT.Copy), tt)
                free[b] = [T_t[w, j, q]]

    units = [(hd, j) for hd in range(8) for j in range(2)]
    at_p, use_p = {}, {}

    def att_scores(u):
        hd, j = units[u]
        b, i = u % 2, u % 2
        nk = P * (j + 1)
        q = hd // 4
        dep = [T_t[0, j, q]] + [T_t[1, jj, q] for jj in range(j + 1)]
        for c in range(2):
            cs = slice(64 * c, 64 * c + 64)
            t = mm(ps[2 * b + c][:, 0:nk], QT[cs, hd, j * P:j * P + P], KTt[cs, hd, 0:nk], True, True,
                   dep, free[2 * b + c], sig=c == 1)
        sv = Sm[i][:, :, 0:nk]
        mk = const("amask")[:, j * S:j * S + nk].unsqueeze(1).broadcast_to([P, 2, nk])
        t = DV(lambda e: e.tensor_tensor(sv, banks[:, 2 * b:2 * b + 2, 0:nk], mk, ALU.add), t, use_p.get(u - 2))
        free[2 * b] = free[2 * b + 1] = [t]
        m = sm[i]
        t = DV(lambda e: e.tensor_reduce(m[:, 0:2], sv, AX, ALU.max, negate=True), t)
        ex = [AC(lambda e, c=c: e.activation(Sm[i][:, c, 0:nk], Sm[i][:, c, 0:nk], ACT.Exp, bias=m[:, c:c + 1],
                                             accum_out=m[:, 2 + c:3 + c]), t) for c in range(2)]
        t = DV(lambda e: e.reciprocal(m[:, 4:6], m[:, 2:4]), ex)
        t2 = DV(lambda e: e.tensor_scalar(m[:, 6:7], m[:, 5:6], lamv[:, 5:6], None, ALU.mult), t, nlam_t)
        t = DV(lambda e: e.tensor_scalar(Sm[i][:, 0, 0:nk], Sm[i][:, 0, 0:nk], m[:, 4:5], None, ALU.mult), t)
        at_p[u] = DV(lambda e: e.scalar_tensor_tensor(Am[i][:, 0:nk], Sm[i][:, 1, 0:nk], m[:, 6:7], Sm[i][:, 0, 0:nk],
                                                      ALU.mult, ALU.add), t, t2, use_p.get(u - 2))

    O_t = {}

    def att_out(u):
        hd, j = units[u]
        b, bo, i = 4 + u % 2, 6 + u % 2, u % 2
        for k in range(j + 1):
            t = transpose(ps[b][:, k * P:k * P + P], Am[i][:, k * P:k * P + P], at_p[u], free[b], sig=k == j)
        use_p[u] = t
        t = AC(lambda e: e.activation(AT[i][:, 0:j + 1, :].rearrange("p a b -> p (a b)"), ps[b][:, 0:P * (j + 1)], ACT.Copy), t, O_t.get(u - 2))
        free[b] = [t]
        for k in range(j + 1):
            tt = mm(ps[bo][:, 0:P], AT[i][:, k, :], V[:, k, hd * P:hd * P + P], k == 0, k == j,
                    t, free[bo], qk_t[4 + hd // 4, k], sig=k == j)
        O_t[u] = AC(lambda e: e.activation(O[:, j, hd * P:hd * P + P], ps[bo][:, 0:P], ACT.Copy), tt)
        free[bo] = [O_t[u]]

    for u in range(17):
        if u < 16:
            att_scores(u)
        if u >= 1:
            att_out(u - 1)

    def head_norm(src, toks, sq, groups, eps, mul, scale_row, row_t):
        res = []
        for j in range(2):
            t = AC(lambda e: e.activation(sq[:, j, :], src[:, j, :], ACT.Square), toks[j])
            last = t
            for c0, nh, w in groups:
                v = sq[:, j, c0:c0 + nh * w].rearrange("p (a b) -> p a b", b=w)
                sv = src[:, j, c0:c0 + nh * w].rearrange("p (a b) -> p a b", b=w)
                a0, a1, a2 = s8[:, j, 0, 0:nh], s8[:, j, 1, 0:nh], s8[:, j, 2, 0:nh]
                t1 = DV(lambda e: e.reduce_sum(a0, v, AX), t)
                t1 = DV(lambda e: e.tensor_scalar(a1, a0, 1.0 / w, eps, ALU.mult, ALU.add), t1, last)
                t1 = AC(lambda e: e.activation(a1, a1, ACT.Sqrt), t1)
                t1 = DV(lambda e: e.reciprocal(a2, a1), t1)
                if mul != 1.0:
                    t1 = DV(lambda e: e.tensor_scalar(a2, a2, mul, None, ALU.mult), t1)
                last = DV(lambda e: e.tensor_tensor(sv, sv, a2.unsqueeze(2).broadcast_to([P, nh, w]), ALU.mult), t1)
            res.append(DV(lambda e: e.tensor_tensor(src[:, j, :], src[:, j, :], scale_row, ALU.mult)
                          if scale_row.shape[-1] == D else
                          e.tensor_tensor(src[:, j, :].rearrange("p (a b) -> p a b", b=P), src[:, j, :].rearrange("p (a b) -> p a b", b=P),
                                          scale_row.unsqueeze(1).broadcast_to([P, 8, P]), ALU.mult), last, row_t))
        return res

    o_t = head_norm(O, [[O_t[u] for u in range(16)]] * 2, V, [(0, 8, P)], 1e-5, 1.0 - LAM0, sub[:, :], sub_t)
    xt = turn(O, o_t, xH, xL)
    ln_t = add_norm(rows("wo", 4, xH, xL, xt), "ln1g0", "ln1b0")

    o = [OW]
    fH = sb("fH", [P, FT, S], F32R, off=o)
    fL = sb("fL", [P, FT, S], F32R, off=o)
    sg = [sb(f"sg{i}", [P, S], off=o) for i in range(2)]
    fv = [sb(f"fv{i}", [P, S], off=o) for i in range(2)]

    def swiglu(layer, xt):
        f_t = []
        for f in range(FT):
            idx, wh, wl, wt = take(f"gu{layer}", f)
            b, i = 4 + f % 4, f % 2
            tg = cols(b, 0, xH, xL, wh, wl, 0, [wt, xt])
            tu = cols(b, S, xH, xL, wh, wl, P, [])
            done[idx] = tu
            t1 = AC(lambda e: e.activation(sg[i][:, :], ps[b][:, 0:S], ACT.Silu), tu, f_t[2 * (f - 2)] if f >= 2 else None,
                    f_t[2 * (f - 2) + 1] if f >= 2 else None)
            t2 = DV(lambda e: e.tensor_tensor(fv[i][:, :], sg[i][:, :], ps[b][:, S:2 * S], ALU.mult), t1,
                    f_t[2 * (f - 2)] if f >= 2 else None)
            free[b] = [t2]
            t3 = AC(lambda e: e.activation(fH[:, f, :], fv[i][:, :], ACT.Copy), t2)
            t4 = DV(lambda e: e.tensor_tensor(fL[:, f, :], fv[i][:, :], fH[:, f, :].bitcast(F32), ALU.subtract), t3)
            f_t += [t3, t4]
        return rows(f"dn{layer}", FT // 2, fH, fL, f_t)

    xt = turn(h, ln_t, xH, xL)
    ln_t = add_norm(swiglu(0, xt), "ln2g0", "ln2b0")

    yc = sb("yc", [P, KT, S], off=o)
    up = [sb(f"up{i}", [P, S + 2], off=o) for i in range(2)]
    cw = sb("cw", [P, KT, 3], off=o)
    cw_t = GP.dma(lambda e: e.dma_start(cw[:, :, :], a["convw"]), s_cw, 16, ln_t)
    pad_t = [DV(lambda e, i=i: e.memset(up[i][:, 0:2], 0.0), ln_t) for i in range(2)]
    xt = turn(h, ln_t, xH, xL)
    y_t = []
    for c in range(8):
        idx, wh, wl, wt = take("cin", c)
        b, i = 4 + c % 4, c % 2
        cols(b, 0, xH, xL, wh, wl, 0, [wt, xt])
        tu = cols(b, S, xH, xL, wh, wl, P, [])
        done[idx] = tu
        prev = y_t[c - 2] if c >= 2 else None
        t1 = AC(lambda e: e.activation(sg[i][:, :], ps[b][:, 0:S], ACT.Copy), tu, prev)
        t2 = DV(lambda e: e.tensor_tensor(up[i][:, 2:S + 2], sg[i][:, :], ps[b][:, S:2 * S], ALU.mult), t1, prev, pad_t)
        free[b] = [t2]
        t = DV(lambda e: e.tensor_scalar(yc[:, c, :], up[i][:, 0:S], cw[:, c, 0:1], None, ALU.mult), t2, cw_t, pad_t)
        for q in (1, 2):
            t = DV(lambda e, q=q: e.scalar_tensor_tensor(yc[:, c, :], up[i][:, q:S + q], cw[:, c, q:q + 1], yc[:, c, :], ALU.mult, ALU.add), t)
        y_t.append(t)
    z_t = []
    for c in range(4):
        idx, wh, wl, wt = take("cin", 8 + c)
        for q in range(2):
            n = 2 * c + q
            b, i = 4 + n % 4, n % 2
            tb = cols(b, 0, xH, xL, wh, wl, q * P, [wt])
            t2 = DV(lambda e: e.tensor_tensor(fv[i][:, :], yc[:, n, :], ps[b][:, 0:S], ALU.mult), tb, y_t[n],
                    z_t[2 * (n - 2)] if n >= 2 else None)
            free[b] = [t2]
            t3 = AC(lambda e: e.activation(fH[:, n, :], fv[i][:, :], ACT.Copy), t2)
            t4 = DV(lambda e: e.tensor_tensor(fL[:, n, :], fv[i][:, :], fH[:, n, :].bitcast(F32), ALU.subtract), t3)
            z_t += [t3, t4]
        done[idx] = tb
    ln_t = add_norm(rows("cout", 4, fH, fL, z_t), "ln1g1", "ln1b1")
    xt = turn(h, ln_t, xH, xL)
    ln_t = add_norm(swiglu(1, xt), "ln2g1", "ln2b1")

    o = [OW]
    mH = sb("mH", [P, KT, S], F32R, off=o)
    mL = sb("mL", [P, KT, S], F32R, off=o)
    nat = sb("nat", [P, 2, D], off=o)
    OM = o[0]
    mem_t = GP.dma(lambda e: e.dma_start(nat[:, :, :], a["mem"]), s_mem, 16, ln_t)
    mt = rms(nat, [mem_t, mem_t], nat2 := sb("nat2", [P, 2, D], off=o), "mem")
    mt = turn(nat2, mt, mH, mL)

    o = [OM]
    ct = sb("ct", [P, 8, 5], off=o)
    gwt = sb("gwt", [P, KT, 8], off=o)
    gbt = sb("gbt", [4, 2], off=o)
    selt = sb("selt", [4, 4, P], off=o)
    qp = [sb(f"qp{i}", [P, 2, S + 3], off=o) for i in range(2)]
    qm = sb("qm", [P, 8, S], off=o)
    vm = sb("vm", [P, 2, 512], off=o)
    og = sb("og", [P, 2, 512], off=o)
    qs = sb("qs", [P, 4, S], off=o)
    ks = sb("ks", [P, 4, S], off=o)
    vs = sb("vs", [P, 2, 512], off=o)
    gi = [sb(f"gi{i}", [4, S], off=o) for i in range(7)]
    gc = sb("gc", [P, 2, 2, 4], off=o)
    s8m = sb("s8m", [P, 8], off=o)
    Wt = [sb(f"Wt{i}", [P, S], off=o) for i in range(2)]
    Pm = [sb(f"Pm{i}", [P, S], off=o) for i in range(2)]
    PT = [sb(f"PT{i}", [P, 2, P], off=o) for i in range(2)]
    dn = [sb(f"dn{i}", [P, 4], off=o) for i in range(2)]
    xm = nat
    mx = nat2
    after_mem = mt
    c4_t = GP.dma(lambda e: e.dma_start(ct[:, :, :], a["conv4"]), s_c4, 16, after_mem)
    GP.dma(lambda e: e.dma_start(gwt[:, :, :], a["gatew"]), s_gw, 16, after_mem)
    GP.dma(lambda e: e.dma_start(gbt[:, :], a["gateb"]), s_gw, 32, after_mem)
    gw_t = GP.dma(lambda e: e.dma_start(selt[:, :, :], a["sel"]), s_gw, 48, after_mem)
    n_t = rms(h, ln_t, xm, "mix", after=after_mem)
    xt = turn(xm, n_t, xH, xL)
    pad_t = [DV(lambda e, i=i: e.memset(qp[i][:, :, 0:3], 0.0), after_mem) for i in range(2)]

    for g in range(2):
        for k in range(KT):
            for part_, (H, sig_) in enumerate(((xH, False), (xL, k == KT - 1))):
                t = mm(ps[0][0:4, g * S:g * S + S], gwt[:, k, 4 * g:4 * g + 4], H[:, k, :].bitcast(F32),
                       k == 0 and part_ == 0, k == KT - 1 and part_ == 1, xt, gw_t, free[0], sig=sig_ and g == 1)
    gi_i, gi_f, g1, g2, gB, gmm, gng = gi
    t_i = DV(lambda e: e.tensor_scalar(gi_i[:, :], ps[0][0:4, 0:S], gbt[:, 0:1], None, ALU.add), t, gw_t)
    t_f = DV(lambda e: e.tensor_scalar(gi_f[:, :], ps[0][0:4, S:2 * S], gbt[:, 1:2], None, ALU.add), t, gw_t)
    free[0] = [t_f]
    t = DV(lambda e: e.scalar_tensor_tensor(g1[:, :], gi_f[:, :], -1.0, gi_f[:, :], ALU.mult, ALU.max), t_f)
    t = AC(lambda e: e.activation(g1[:, :], g1[:, :], ACT.Exp, scale=-1.0), t)
    t = AC(lambda e: e.activation(g2[:, :], g1[:, :], ACT.Ln, bias=1.0), t)
    t = DV(lambda e: e.scalar_tensor_tensor(g1[:, :], gi_f[:, :], 0.0, g2[:, :], ALU.min, ALU.subtract), t)
    z0 = DV(lambda e: e.memset(g2[:, :], 1.0), t)
    t_B = DV(lambda e: e.tensor_tensor_scan(gB[:, :], g2[:, :], g1[:, :], 0.0, ALU.mult, ALU.add), t, z0)
    t_c = DV(lambda e: e.tensor_tensor(gi_i[:, :], gi_i[:, :], gB[:, :], ALU.subtract), t_B, t_i)
    z0 = DV(lambda e: e.memset(g1[:, :], 0.0), t_B)
    t_mm = DV(lambda e: e.tensor_tensor_scan(gmm[:, :], g1[:, :], gi_i[:, :], 0.0, ALU.add, ALU.max), t_c, z0)
    t = DV(lambda e: e.tensor_tensor(gng[:, :], gB[:, :], gmm[:, :], ALU.add), t_mm)
    t_ng = AC(lambda e: e.activation(gng[:, :], gng[:, :], ACT.Exp, scale=-1.0), t)
    for j in range(2):
        transpose(ps[1][:, 8 * j:8 * j + 4], gmm[:, j * P:j * P + P], t_mm, free[1])
        t = transpose(ps[1][:, 8 * j + 4:8 * j + 8], gng[:, j * P:j * P + P], t_ng, sig=True)
    gcv = ps[1][:, 0:16].rearrange("p (j a b) -> p j a b", j=2, a=2)
    DV(lambda e: e.tensor_scalar(gc[:, :, 0, :], gcv[:, :, 0, :], -1.0, None, ALU.mult), t)
    gc_t = DV(lambda e: e.tensor_copy(gc[:, :, 1, :], gcv[:, :, 1, :]), t)
    free[1] = [gc_t]

    qm_t = []
    for c in range(4):
        idx, wh, wl, wt = take("win", c)
        b, i = 4 + c % 4, c % 2
        cols(b, 0, xH, xL, wh, wl, 0, [wt, xt])
        t = cols(b, S, xH, xL, wh, wl, P, [])
        done[idx] = t
        t = AC(lambda e: e.activation(qp[i][:, :, 3:S + 3], ps[b][:, :].rearrange("p (a t) -> p a t", a=2), ACT.Copy), t,
               qm_t[2 * (c - 2):2 * (c - 2) + 2] if c >= 2 else None, pad_t)
        free[b] = [t]
        for q in range(2):
            n = 2 * c + q
            m = DV(lambda e: e.tensor_scalar(qm[:, n, :], qp[i][:, q, 0:S], ct[:, n, 0:1], ct[:, n, 4:5], ALU.mult, ALU.add), t, c4_t, pad_t)
            for w in range(1, 4):
                m = DV(lambda e, w=w: e.scalar_tensor_tensor(qm[:, n, :], qp[i][:, q, w:S + w], ct[:, n, w:w + 1], qm[:, n, :], ALU.mult, ALU.add), m)
            qm_t.append(m)
    silu_t = [AC(lambda e, n=n: e.activation(qm[:, n, :], qm[:, n, :], ACT.Silu), qm_t[n]) for n in range(8)]
    vm_t, og_t, vs_t = [], [], []
    bt = blocks("win", 4, xH, xL, 0, xt)
    for j in range(2):
        vm_t.append(AC(lambda e: e.activation(vm[:, j, :], ps[j][:, :], ACT.Copy), bt[j]))
        free[j] = [vm_t[j]]
    bt = blocks("win", 6, xH, xL, 2, xt)
    for j in range(2):
        og_t.append(AC(lambda e: e.activation(og[:, j, :], ps[2 + j][:, :], ACT.Sigmoid), bt[j]))
        free[2 + j] = [og_t[j]]
    sq_t = {}
    for w in range(2):
        for c in range(2):
            idx, wh, wl, wt = take("win", 8 + 2 * w + c)
            b = 4 + (2 * w + c) % 4
            cols(b, 0, xH, xL, wh, wl, 0, [wt, xt])
            t = cols(b, S, xH, xL, wh, wl, P, [])
            done[idx] = t
            dst = (qs if w == 0 else ks)[:, 2 * c:2 * c + 2, :].rearrange("p a t -> p (a t)")
            sq_t[w, c] = AC(lambda e: e.activation(dst, ps[b][:, :], ACT.Copy, scale=0.125 if w == 0 else 1.0), t)
            free[b] = [sq_t[w, c]]
    bt = blocks("win", 12, xH, xL, 0, xt)
    for j in range(2):
        vs_t.append(AC(lambda e: e.activation(vs[:, j, :], ps[j][:, :], ACT.Copy), bt[j]))
        free[j] = [vs_t[j]]

    munits = [(hd, j) for hd in range(4) for j in range(2)]
    pm_t, mx_t, pt_t = {}, {}, {}

    def ml_scores(u):
        hd, j = munits[u]
        b, i, nk = u % 2, u % 2, P * (j + 1)
        mm(ps[b][:, 0:nk], qm[:, hd, j * P:j * P + P], qm[:, 4 + hd, 0:nk], True, True, silu_t[hd], silu_t[4 + hd], free[b])
        t = mm(ps[b][:, S:S + nk], selt[:, hd, :], gi_i[:, 0:nk], True, True, t_c, gw_t, sig=True)
        w_ = DV(lambda e: e.tensor_tensor(Wt[i][:, 0:nk], ps[b][:, S:S + nk], const("cmask")[:, j * S:j * S + nk], ALU.add), t, pm_t.get(u - 2))
        w_ = AC(lambda e: e.activation(Wt[i][:, 0:nk], Wt[i][:, 0:nk], ACT.Exp, bias=gc[:, j, 0, hd:hd + 1]), w_, gc_t)
        w_ = DV(lambda e: e.scalar_tensor_tensor(Pm[i][:, 0:nk], ps[b][:, 0:nk], float(P) ** -0.5, Wt[i][:, 0:nk], ALU.mult, ALU.mult,
                                                 accum_out=dn[i][:, 0:1]), w_, pt_t.get(u - 2), mx_t.get(u - 2))
        pm_t[u] = w_
        free[b] = [w_]
        t = DV(lambda e: e.scalar_tensor_tensor(dn[i][:, 3:4], dn[i][:, 0:1], -1.0, dn[i][:, 0:1], ALU.mult, ALU.max), w_)
        t = DV(lambda e: e.tensor_scalar(dn[i][:, 1:2], dn[i][:, 3:4], gc[:, j, 1, hd:hd + 1], None, ALU.max), t, gc_t)
        t = DV(lambda e: e.reciprocal(dn[i][:, 2:3], dn[i][:, 1:2]), t)
        return t

    def ml_out(u, rden):
        hd, j = munits[u]
        i, b, bo = u % 2, 2 + u % 2, 4 + u % 2
        for k in range(j + 1):
            t = transpose(ps[b][:, k * P:k * P + P], Pm[i][:, k * P:k * P + P], pm_t[u], free[b], sig=k == j)
        pt_t[u] = t
        t = AC(lambda e: e.activation(PT[i][:, 0:j + 1, :].rearrange("p a b -> p (a b)"), ps[b][:, 0:P * (j + 1)], ACT.Copy), t, mx_t.get(u - 2))
        free[b] = [t]
        for k in range(j + 1):
            t2 = mm(ps[bo][:, 0:P], PT[i][:, k, :], vm[:, k, hd * P:hd * P + P], k == 0, k == j, t, vm_t[k], free[bo], sig=k == j)
        mx_t[u] = DV(lambda e: e.scalar_tensor_tensor(mx[:, j, hd * P:hd * P + P], ps[bo][:, 0:P], dn[i][:, 2:3],
                                                      og[:, j, hd * P:hd * P + P], ALU.mult, ALU.mult), t2, rden, og_t[j])
        free[bo] = [mx_t[u]]

    rden = {}
    for u in range(9):
        if u < 8:
            rden[u] = ml_scores(u)
        if u >= 1:
            ml_out(u - 1, rden[u - 1])

    zs = [sb(f"zs{i}", [P, 384], off=o) for i in range(2)]
    ze = [sb(f"ze{i}", [P, 384], off=o) for i in range(2)]
    zl = [sb(f"zl{i}", [P, 384], off=o) for i in range(2)]
    l_t, sb_t, la_t = {}, {}, {}

    def st_logits(hd):
        i, b, tl = hd % 2, hd % 2, hd // 2
        rp = slice(64 * (hd % 2), 64 * (hd % 2) + 64)
        dep = [sq_t[0, tl // 2], sq_t[1, tl // 2]]
        for n, (s_, t_) in enumerate(((0, 0), (1, 1), (0, 1))):
            t = mm(ps[b][:, n * P:n * P + P], ks[rp, tl, s_ * P:s_ * P + P], qs[rp, tl, t_ * P:t_ * P + P], True, True,
                   dep, free[b], sig=n == 2)
        t1 = AC(lambda e: e.activation(zs[i][:, :], ps[b][:, 0:384], ACT.Copy), t, la_t.get(hd - 2))
        free[b] = [t1]
        t = DV(lambda e: e.scalar_tensor_tensor(ze[i][:, :], zs[i][:, :], -1.0, zs[i][:, :], ALU.mult, ALU.max), t1, la_t.get(hd - 2))
        t = AC(lambda e: e.activation(ze[i][:, :], ze[i][:, :], ACT.Exp, scale=-1.0), t)
        t = AC(lambda e: e.activation(ze[i][:, :], ze[i][:, :], ACT.Ln, bias=1.0), t)
        t = DV(lambda e: e.scalar_tensor_tensor(zl[i][:, :], zs[i][:, :], 0.0, ze[i][:, :], ALU.max, ALU.add), t, sb_t.get(hd - 2))
        t = DV(lambda e: e.tensor_tensor(zl[i][:, 0:S], zl[i][:, 0:S], const("keep"), ALU.mult), t)
        t2 = DV(lambda e: e.tensor_tensor(zs[i][:, 0:S], zs[i][:, 0:S], const("sneg"), ALU.add), t)
        l_t[hd] = [t, t2]

    def st_out(hd):
        i, b, bo = hd % 2, 2 + hd % 2, 6 + hd % 2
        mm(ps[b][:, 0:384], const("tri"), zl[i][:, :], True, True, l_t[hd], free[b])
        t = PE(lambda e: e.matmul(ps[b][:, S:384], const("ones"), zl[i][:, P:S], start=False, stop=True, skip_group_check=True), sig=True)
        t = DV(lambda e: e.scalar_tensor_tensor(ze[i][:, :], ps[b][:, 0:384], -1.0, zs[i][:, :], ALU.mult, ALU.add), t, l_t[hd])
        free[b] = [t]
        la_t[hd] = t
        t = AC(lambda e: e.activation(ze[i][:, :], ze[i][:, :], ACT.Exp), t)
        vc = slice(64 * hd, 64 * hd + 64)
        mm(ps[bo][:, 0:64], ze[i][:, 0:P], vs[:, 0, vc], True, True, t, free[bo], vs_t)
        mm(ps[bo][:, 64:P], ze[i][:, S:384], vs[:, 0, vc], True, False)
        t = mm(ps[bo][:, 64:P], ze[i][:, P:S], vs[:, 1, vc], False, True, sig=True)
        la_t[hd] = [la_t[hd], t]
        ov = ps[bo][:, 0:P].rearrange("p (j d) -> p j d", j=2)
        sb_t[hd] = AC(lambda e: e.activation(mx[:, :, 512 + 64 * hd:512 + 64 * hd + 64], ov, ACT.Copy), t)
        free[bo] = [sb_t[hd]]

    for hd in range(9):
        if hd < 8:
            st_logits(hd)
        if hd >= 1:
            st_out(hd - 1)

    s8 = sb("s8b", [P, 2, 3, 8], off=o)
    hg, hg_t = gain("heads")
    every = [mx_t[u] for u in range(8)] + [sb_t[u] for u in range(8)]
    m_t = head_norm(mx, [every, every], xm, [(0, 4, P), (512, 8, 64)], 1e-6, 1.0, hg[:, :], hg_t)
    gain_used("heads", m_t[1])
    xt = turn(mx, m_t, xH, xL)
    r_t = add_rows(rows("wout", 4, xH, xL, xt))

    o = [OM]
    xn = sb("xn", [P, 2, D], off=o)
    xq = sb("xq", [P, KT, S], off=o)
    xk = sb("xk", [P, KT, S], off=o)
    xv = sb("xv", [P, 2, D], off=o)
    pr = [sb(f"pr{i}", [P, S], off=o) for i in range(2)]
    pT = [sb(f"pT{i}", [P, 2, S], off=o) for i in range(2)]
    px = [sb(f"px{i}", [P, 4], off=o) for i in range(2)]
    k_t = {}

    def turned(name, dst, H, L, scale, dep, keep):
        for c in range(4):
            idx, wh, wl, wt = take(name, c)
            b = 4 + c % 4
            cols(b, 0, H, L, wh, wl, 0, [wt, dep])
            t = cols(b, S, H, L, wh, wl, P, [])
            done[idx] = t
            keep[c] = AC(lambda e: e.activation(dst[:, 2 * c:2 * c + 2, :].rearrange("p a t -> p (a t)"), ps[b][:, :], ACT.Copy, scale=scale), t, r_t)
            free[b] = [keep[c]]

    kx_t, qx_t = {}, {}
    n_t = rms(h, r_t, xn, "xattn")
    turned("xk", xk, mH, mL, 1.0, mt, kx_t)
    bt = rows("xv", 4, mH, mL, mt)
    v_t = []
    for j in range(2):
        for e2 in range(2):
            k = 2 * j + e2
            t = AC(lambda e: e.activation(xv[:, j, e2 * 512:e2 * 512 + 512], ps[k][:, :], ACT.Copy), bt[k], r_t)
            free[k] = [t]
            v_t.append(t)
    xt = turn(xn, n_t, xH, xL)
    turned("xq", xq, xH, xL, 1.0 / 16, xt, qx_t)
    xp_t, pT_t, ox_t = {}, {}, []

    def x_scores(hd, j):
        u = 2 * hd + j
        b, i = u % 2, u % 2
        for k in range(2):
            t = mm(ps[b][:, 0:S], xq[:, 2 * hd + k, j * P:j * P + P], xk[:, 2 * hd + k, :], k == 0, k == 1,
                   qx_t[hd], kx_t[hd], free[b], sig=k == 1)
        m = px[i]
        t = DV(lambda e: e.tensor_reduce(m[:, 0:1], ps[b][:, 0:S], AX, ALU.max, negate=True), t, xp_t.get(u - 2))
        t = AC(lambda e: e.activation(pr[i][:, :], ps[b][:, 0:S], ACT.Exp, bias=m[:, 0:1], accum_out=m[:, 1:2]), t, pT_t.get((u - 2, 0)))
        free[b] = [t]
        t = DV(lambda e: e.reciprocal(m[:, 2:3], m[:, 1:2]), t)
        xp_t[u] = DV(lambda e: e.tensor_scalar(pr[i][:, :], pr[i][:, :], m[:, 2:3], None, ALU.mult), t)

    def x_turn(hd, j):
        u = 2 * hd + j
        b, i = 2 + u % 2, u % 2
        for k in range(2):
            t = transpose(ps[b][:, k * P:k * P + P], pr[i][:, k * P:k * P + P], xp_t[u], free[b], sig=k == 1)
        pT_t[u, 0] = t
        pT_t[u, 1] = AC(lambda e: e.activation(pT[hd % 2][:, :, j * P:j * P + P], ps[b][:, 0:S].rearrange("p (k t) -> p k t", k=2), ACT.Copy),
                        t, ox_t[-2] if hd >= 2 else None)
        free[b] = [pT_t[u, 1]]

    def x_out(hd):
        dep = [pT_t[2 * hd, 1], pT_t[2 * hd + 1, 1]]
        for q in range(2):
            b = 4 + (2 * hd + q) % 4
            for k in range(2):
                t = mm(ps[b][:, 0:S], xv[:, k, (2 * hd + q) * P:(2 * hd + q) * P + P], pT[hd % 2][:, k, :], k == 0, k == 1,
                       dep, v_t, free[b], sig=k == 1)
            r = part(xH[:, 2 * hd + q, :], xL[:, 2 * hd + q, :], ps[b][:, 0:S], [t, [qx_t[c] for c in range(4)]])
            free[b] = [r[1]]
            o_parts.extend(r)
        ox_t.append(t)

    o_parts = []
    for hd in range(5):
        if hd < 4:
            x_scores(hd, 0)
            x_scores(hd, 1)
        if hd >= 1:
            x_out(hd - 1)
        if hd < 4:
            x_turn(hd, 0)
            x_turn(hd, 1)
    r_t = add_rows(rows("xo", 4, xH, xL, o_parts))

    o = [OW]
    pn = sb("pn", [P, 2, D], off=o)
    qH = sb("qH", [P, 16, S], F32R, off=o)
    qL = sb("qL", [P, 16, S], F32R, off=o)
    n_t = rms(h, r_t, pn, "ffn")
    xt = turn(pn, n_t, xH, xL)
    q_t = []
    for c in range(8):
        idx, wh, wl, wt = take("pq", c)
        b = 4 + c % 4
        cols(b, 0, xH, xL, wh, wl, 0, [wt, xt])
        t = cols(b, S, xH, xL, wh, wl, P, [])
        done[idx] = t
        r = part(qH[:, 2 * c:2 * c + 2, :].rearrange("p a t -> p (a t)"), qL[:, 2 * c:2 * c + 2, :].rearrange("p a t -> p (a t)"),
                 ps[b][:, :], t)
        free[b] = [r[1]]
        q_t += r

    o = [OX]
    uH = [sb(f"uH{i}", [P, UW], F32R, off=o) for i in range(US)]
    uL = [sb(f"uL{i}", [P, UW], F32R, off=o) for i in range(US)]
    st = [sb(f"st{i}", [P, S], off=o) for i in range(4)]
    iob = sb("iob", [P, P, 8], BF16, off=o)
    i1T = sb("i1T", [P, S], BF16, off=o)
    i2T = sb("i2T", [P, S], BF16, off=o)
    gT = sb("gT", [P, S], off=o)
    gp = [sb(f"gp{i}", [P, S], BF16, off=o) for i in range(3)]
    oB = sb("oB", [P, P, 8], BF16, off=o)
    oE = sb("oE", [P, P, 8], BF16, off=o)
    oA = [sb(f"oA{i}", [P, P, 8], BF16, off=o) for i in range(3)]
    GO = o[0]
    G = sb("G", [P, P, S], off=o)
    o = [OW + 8192 + 32768]
    sc = sb("sc", [P, 2, 16, P], off=o)
    wk = [sb(f"wk{i}", [P, S], off=o) for i in range(4)]
    ti = sb("ti", [P, 16, 16], U32, off=o)
    tf = sb("tf", [P, 16, 16], off=o)
    tv = sb("tv", [P, 16, 16], off=o)
    bv = sb("bv", [P, 8, 16], off=o)
    bp = sb("bp", [P, 8, 16], U32, off=o)
    bq = [sb(f"bq{i}", [P, 8, 16], U32, off=o) for i in range(2)]
    bf = [sb(f"bf{i}", [P, 8, 16], off=o) for i in range(2)]
    ei = [sb(f"ei{i}", [P, 8, 16], off=o) for i in range(2)]
    gs = sb("gs", [P, 8, 2], off=o)
    eq = sb("eq", [P, P, 16], off=o)
    cand = sb("cand", [P, 8, S], off=[OW])
    assert OW >= GO

    idx, wh, wl, wt = take("sk", 0)
    last_chunk = len(STREAM) - 1
    u_raw = [sem(f"s_u{i}") for i in range(UR)]
    ua, ub, udone, u_t = {}, {}, {}, {}

    def ufetch(n):
        if n >= 2 * P:
            return
        k = n % UR
        if n < UR:
            c = max(m for m in range(len(STREAM)) if m % NR == k // 2)
            dep = [split_a[c], split_v[c]]
        else:
            dep = [ua[n - UR], ub[n - UR]]
        src = a["eu"][n] if n < P else a["ev"][n - P]
        u_t[n] = SP.dma(lambda e: e.dma_start(raw[k // 2][:, (k % 2) * UW:(k % 2) * UW + UW], src), u_raw[k], 16 * (n // UR + 1), dep)

    def usplit(n):
        if n >= 2 * P:
            return
        k, s_ = n % UR, n % US
        src = raw[k // 2][:, (k % 2) * UW:(k % 2) * UW + UW]
        dep = udone[n - US] if n >= US else [done[last_chunk], done[last_chunk - 1], done[last_chunk - 2], n_t]
        ua[n] = AC(lambda e: e.activation(uH[s_][:, :], src, ACT.Copy), u_t[n], dep)
        lane = GP if n < P and n % 2 == 0 else DV
        ub[n] = lane(lambda e: e.tensor_tensor(uL[s_][:, :], src, uH[s_][:, :].bitcast(F32), ALU.subtract), ua[n], u_t[n], dep)
        ufetch(n + UR)

    for n in range(UR):
        ufetch(n)

    sc_t = {}
    for j in range(2):
        for q in range(4):
            b = 4 * j + q
            for i in range(4):
                hp = 4 * q + i
                ov = ps[b][:, i * P:i * P + P]
                ts = slice(j * P, j * P + P)
                kc = slice(hp * P, hp * P + P)
                mm(ov, qH[:, hp, ts], wh[:, kc], True, False, wt, q_t, free[b])
                mm(ov, qH[:, hp, ts], wl[:, kc], False, False)
                t = mm(ov, qL[:, hp, ts], wh[:, kc], False, True, sig=i == 3)
            sc_t[j, q] = AC(lambda e: e.activation(sc[:, j, 4 * q:4 * q + 4, :].rearrange("p a b -> p (a b)"), ps[b][:, :], ACT.Copy), t)
            free[b] = [sc_t[j, q]]
    done[idx] = t
    h_t = SP.dma(lambda e: e.dma_start(hs, h[:, :, :]), s_hs, 16, r_t)
    iob_t = GP(lambda e: e.iota(iob[:, :, :].rearrange("p i t -> p (i t)"), [[1, P], [0, 8]], base=0, channel_multiplier=0,
                                allow_small_or_imprecise_dtypes=True), t, n_t)

    sel_t, ev_t = [], []
    NEG = -3.0e38

    def top16(row, w_, vals, inds, dep):
        n = len(row)
        t = [DV(lambda e: e.max(vals[k][:, 0:8], row[k]), dep[k]) for k in range(n)]
        yield
        for k in range(n):
            DV(lambda e: e.max_index(inds[k][:, 0:8], vals[k][:, 0:8], row[k]), t[k])
        yield
        t = [DV(lambda e: e.match_replace(w_[k], vals[k][:, 0:8], row[k], NEG), t[k]) for k in range(n)]
        yield
        t = [DV(lambda e: e.max(vals[k][:, 8:16], w_[k]), t[k]) for k in range(n)]
        yield
        top_t[:] = [DV(lambda e: e.max_index(inds[k][:, 8:16], vals[k][:, 8:16], w_[k]), t[k]) for k in range(n)]
        yield

    top_t = []

    def route():
        prev = None
        for j in range(2):
            tops = []
            for q in range(4):
                r = range(4 * q, 4 * q + 4)
                yield from top16([sc[:, j, x, :] for x in r], [wk[x % 4][:, 0:P] for x in r], [tv[:, x, :] for x in r],
                                 [ti[:, x, :] for x in r], [[sc_t[j, q], prev, ev_t]] * 4)
                tops += top_t
            tf_t = DV(lambda e: e.tensor_copy(tf[:, :, :], ti[:, :, :]), tops)
            s1 = tv[:, :, :].rearrange("p (h c) k -> p h c k", c=2)
            cv = cand[:, :, :].rearrange("p h (a b) -> p h a b", a=16)
            c_t = []
            for hd in range(8):
                c_t.append(DV(lambda e: e.tensor_tensor(cv[:, hd, :, :], s1[:, hd, 0, :].unsqueeze(2).broadcast_to([P, 16, 16]),
                                                        s1[:, hd, 1, :].unsqueeze(1).broadcast_to([P, 16, 16]), ALU.add), tops, q_t))
                if hd % 2:
                    yield
            tops = []
            for q in range(2):
                r = range(4 * q, 4 * q + 4)
                yield from top16([cand[:, x, :] for x in r], [wk[x % 4][:, :] for x in r], [bv[:, x, :] for x in r],
                                 [bp[:, x, :] for x in r], [[c_t[x], prev] for x in r])
                tops += top_t
            t = DV(lambda e: e.tensor_tensor(ei[0][:, :, :], bv[:, :, :], bv[:, :, 0:1].broadcast_to([P, 8, 16]), ALU.subtract), tops)
            t = AC(lambda e: e.activation(ei[0][:, :, :], ei[0][:, :, :], ACT.Exp), t)
            t = DV(lambda e: e.reduce_sum(gs[:, :, 0], ei[0][:, :, :], AX), t)
            t = DV(lambda e: e.reciprocal(gs[:, :, 1], gs[:, :, 0]), t)
            g_t = DV(lambda e: e.tensor_tensor(bv[:, :, :], ei[0][:, :, :], gs[:, :, 1:2].broadcast_to([P, 8, 16]), ALU.mult), t)
            yield
            u0 = DV(lambda e: e.tensor_scalar(bq[0][:, :, :], bp[:, :, :], 4, None, ALU.logical_shift_right), tops)
            u1 = DV(lambda e: e.tensor_scalar(bq[1][:, :, :], bp[:, :, :], 15, None, ALU.bitwise_and), tops)
            f_t = [DV(lambda e: e.tensor_copy(bf[i][:, :, :], bq[i][:, :, :]), u0, u1) for i in range(2)]
            yield
            e_t = []
            tfv = tf[:, :, :].rearrange("p (h c) k -> p h c k", c=2)
            for i in range(2):
                t = DV(lambda e: e.tensor_tensor(eq[:, :, :], bf[i][:, :, :].rearrange("p a b -> p (a b)").unsqueeze(2).broadcast_to([P, P, 16]),
                                                 iota[:, 0:16].unsqueeze(1).broadcast_to([P, P, 16]), ALU.is_equal), f_t[i], e_t[-1:], id_t)
                yield
                ev = eq[:, :, :].rearrange("p (h k) a -> p h k a", h=8)
                t = DV(lambda e: e.tensor_tensor(ev, ev, tfv[:, :, i, :].unsqueeze(2).broadcast_to([P, 8, 16, 16]), ALU.mult), t, tf_t)
                yield
                e_t.append(DV(lambda e: e.reduce_sum(ei[i][:, :, :].rearrange("p a b -> p (a b)"), eq[:, :, :], AX), t, g_t))
                yield
            prev = (yield (e_t[0], e_t[1], g_t))

    def turn_picks(j, toks):
        b = 6 + j
        for i, src in enumerate((ei[0], ei[1], bv)):
            t = transpose(ps[b][:, i * P:i * P + P], src[:, :, :].rearrange("p a b -> p (a b)"), toks[i], free[b], sig=i == 2)
        tj = slice(j * P, j * P + P)
        c1 = DV(lambda e: e.tensor_copy(i1T[:, tj], ps[b][:, 0:P]), t, n_t)
        c2 = DV(lambda e: e.tensor_copy(i2T[:, tj], ps[b][:, P:2 * P]), t)
        g0 = DV(lambda e: e.tensor_copy(gT[:, tj], ps[b][:, 2 * P:3 * P]), t)
        free[b] = [g0]
        c = g0
        for i in range(3):
            c = DV(lambda e: e.tensor_copy(gp[i][:, tj], gT[:, tj]), c)
            if i < 2:
                c = DV(lambda e: e.tensor_tensor(gT[:, tj], gT[:, tj], gp[i][:, tj], ALU.subtract), c)
        sel_t.append([c1, c2, c])
        ev_t.append(t)
        return t

    G_t = []
    ab_t = [None]

    def gates(bt):
        sel_ = sel_t[bt // 16]
        tt = slice(8 * bt, 8 * bt + 8)

        def wide(x):
            return x[:, tt].unsqueeze(1).broadcast_to([P, P, 8])

        tb = DV(lambda e: e.tensor_tensor(oB[:, :, :], iob[:, :, :], wide(i2T), ALU.is_equal), sel_, iob_t, ab_t[0])
        te = DV(lambda e: e.tensor_tensor(oE[:, :, :], iob[:, :, :], wide(i1T), ALU.is_equal), sel_)
        ta = [DV(lambda e: e.tensor_tensor(oA[i][:, :, :], oE[:, :, :], wide(gp[i]), ALU.mult), te, ab_t[0]) for i in range(3)]
        for q in range(2):
            b = 6 + q
            for m in range(4):
                n = 4 * q + m
                for i in range(3):
                    t = mm(ps[b][:, m * P:m * P + P], oB[:, :, n], oA[i][:, :, n], i == 0, i == 2, tb, ta, free[b], sig=i == 2 and m == 3)
            t0 = 8 * bt + 4 * q
            G_t.append(AC(lambda e: e.activation(G[:, :, t0:t0 + 4], ps[b][:, :].rearrange("p (t i) -> p i t", t=4), ACT.Copy),
                          t, sel_t, h_t, n_t))
            free[b] = [G_t[-1]]
        ab_t[0] = t

    s_st = [sem(f"s_st{i}") for i in range(4)]
    st_t = {}

    def ex_in(i):
        b = 4 + i % 2
        ov = ps[b][:, 0:S]
        w_h, w_l, wt = uH[i % US], uL[i % US], [ua[i], ub[i]]
        for k in range(KT):
            kc = slice(k * P, k * P + P)
            mm(ov, w_h[:, kc], xH[:, k, :], k == 0, False, wt, free[b], xt)
            mm(ov, w_h[:, kc], xL[:, k, :], False, False)
            t = mm(ov, w_l[:, kc], xH[:, k, :], False, k == KT - 1, sig=k == KT - 1)
        udone[i] = t
        t = AC(lambda e: e.activation(st[i % 4][:, :], ov, ACT.Gelu), t, st_t.get(i - 4), n_t)
        free[b] = [t]
        st_t[i] = SP.dma(lambda e: e.dma_start(gel[i], st[i % 4][:, :]), s_st[i % 4], 16 * (i // 4 + 1), t)

    work = route()
    pend = None
    bt = 0
    for n in range(US - 1):
        usplit(n)
    for i in range(P):
        ex_in(i)
        usplit(i + US - 1)
        if work is not None:
            for _ in range(2):
                r = work.send(pend)
                pend = None
                if r is not None:
                    pend = turn_picks(len(sel_t), r)
                    if len(sel_t) == 2:
                        work = None
                        break
        elif i % 2 and bt < 32:
            gates(bt)
            bt += 1
    while bt < 32:
        gates(bt)
        bt += 1

    o = [GO - 5 * 2048]
    ga = [sb(f"ga{i}", [P, S], off=o) for i in range(2)]
    gH = [sb(f"gH{i}", [P, S], F32R, off=o) for i in range(2)]
    gL = [sb(f"gL{i}", [P, S], F32R, off=o) for i in range(2)]
    assert o[0] <= GO
    s_rb = [sem(f"s_rb{i}") for i in range(4)]
    rb_t, m_t, act_t = {}, {}, {}

    def ex_load(i):
        if i < P:
            rb_t[i] = SP.dma(lambda e: e.dma_start(st[i % 4][:, :], gel[i]), s_rb[i % 4], 16 * (i // 4 + 1),
                             st_t[i], st_t[P - 4 + i % 4], m_t.get(i - 4))

    def ex_act(i):
        if i >= P:
            return
        y2 = udone.get(P + i - 2) if i >= 2 else [G_t, ab_t[0]]
        t = DV(lambda e: e.tensor_tensor(ga[i % 2][:, :], st[i % 4][:, :], G[:, i, :], ALU.mult), rb_t[i], G_t, act_t.get(i - 2), y2)
        m_t[i] = t
        t1 = AC(lambda e: e.activation(gH[i % 2][:, :], ga[i % 2][:, :], ACT.Copy), t, y2)
        t2 = DV(lambda e: e.tensor_tensor(gL[i % 2][:, :], ga[i % 2][:, :], gH[i % 2][:, :].bitcast(F32), ALU.subtract), t1, y2)
        act_t[i] = [t1, t2]
        ex_load(i + 4)

    def ex_out(i):
        n = P + i
        w_h, w_l, wt = uH[n % US], uL[n % US], [ua[n], ub[n]]
        for t in range(2):
            ts = slice(t * P, t * P + P)
            for part_, (l, w) in enumerate(((gH, w_h), (gH, w_l), (gL, w_h))):
                for e2 in range(2):
                    b = 2 * t + e2
                    last = i == P - 1 and part_ == 2
                    tok = mm(ps[b][:, :], l[i % 2][:, ts], w[:, e2 * 512:e2 * 512 + 512], i == 0 and part_ == 0, last,
                             act_t[i], wt, free[b] if i == 0 else None, sig=last or (t == 1 and part_ == 2 and e2 == 1))
                    if last:
                        free[b] = [tok]
        udone[n] = tok

    for i in range(4):
        ex_load(i)
    ex_act(0)
    for i in range(P):
        ex_act(i + 1)
        ex_out(i)
        usplit(P + i + US - 1)

    o = [GO]
    hb = sb("hb", [P, 2, D], off=o)
    pn = sb("pnl", [P, 2, D], off=o)
    gl = sb("gl", [P, D], off=o)
    b_t = SP.dma(lambda e: e.dma_start(hb[:, :, :], hs), s_hs, 32, h_t, m_t[P - 1])
    gl_t = SP.dma(lambda e: e.dma_start(gl[:, :], a["gains"][len(GAINS):len(GAINS) + 1, :].broadcast_to([P, D])), s_gl, 16, m_t[P - 1])
    for j in range(2):
        for e2 in range(2):
            k = 2 * j + e2
            hv = hb[:, j, e2 * 512:e2 * 512 + 512]
            t = DV(lambda e: e.tensor_tensor(hv, hv, ps[k][:, :], ALU.add), free[k], b_t)
        t = AC(lambda e: e.activation(pn[:, j, :], hb[:, j, :], ACT.Square, accum_out=mv[:, j, 0:1]), t, (DV.sem, DV.count - 1), m_t[P - 1])
        t = root(j, mv[:, j, 0:1], 1.0 / D, 1e-6, t)
        t = DV(lambda e: e.scalar_tensor_tensor(pn[:, j, :], hb[:, j, :], rs[:, j, 1:2], gl[:, :], ALU.mult, ALU.mult), t, gl_t)
        SP.dma(lambda e: e.dma_start(out[j], pn[:, j, :]), s_out, 16 * (j + 1), t)
    SP.wait((s_out, 32))
    assert nuse[0] == len(STREAM)


def constants():
    c = np.zeros((P, CWID), np.float32)
    pos = np.arange(S, dtype=np.float32)
    inv = (np.float32(500000.0) ** (-np.arange(0, 16, 2, dtype=np.float32) / np.float32(16))).astype(np.float32)
    ang = pos[:, None] * inv[None, :]
    p, f = np.arange(P)[:, None], np.arange(S)[None, :]
    for j in range(2):
        for name, fn in (("cos", np.cos), ("sin", np.sin)):
            c0 = CC[name][0] + j * P
            c[:, c0:c0 + P] = np.tile(fn(ang[j * P:j * P + P]).astype(np.float32), (1, 16))
        c0 = CC["amask"][0] + j * S
        c[:, c0:c0 + S] = np.where(f // 64 <= (j * P + p) // 64, 0.0, -1e30)
        c0 = CC["cmask"][0] + j * S
        c[:, c0:c0 + S] = np.where(f <= j * P + p, 0.0, -1e30)
        g = np.arange(P)[None, :]
        c0 = CC["keep"][0] + j * P
        c[:, c0:c0 + P] = np.where(p < g, 1.0, 0.0)
        c0 = CC["sneg"][0] + j * P
        c[:, c0:c0 + P] = np.where(p < g, 0.0, -1e30)
    c0 = CC["tri"][0]
    c[:, c0:c0 + P] = np.where(p >= np.arange(P)[None, :], 1.0, 0.0)
    c0 = CC["ones"][0]
    c[:, c0:c0 + P] = 1.0
    sel = np.zeros((4, 4, P), np.float32)
    for k in range(4):
        sel[k, k, :] = 1.0
    return {"consts": c, "ident": np.eye(P, dtype=np.float32),
            "iota": np.tile(np.arange(P, dtype=np.float32)[None, :], (P, 1)), "sel": sel}


def layout(v):
    def side(w, n):
        e = w.shape[1] // n
        return w.reshape(KT, P, e, n).transpose(2, 1, 0, 3).reshape(e, P, KT * n)

    def deep(w, kk):
        c = w.shape[0] // (P * kk)
        return w.reshape(c, kk, P, w.shape[1]).transpose(0, 2, 1, 3).reshape(c, P, kk * w.shape[1])

    def block(w):
        b = w.shape[1] // 512
        return w.reshape(2, 4, P, b, 512).transpose(3, 0, 2, 1, 4).reshape(2 * b, P, CW)

    def pair(x, y):
        return np.stack([x.reshape(D, -1, P), y.reshape(D, -1, P)], 2).reshape(D, -1)

    def rows2(x):
        return x.reshape(2, P, D).transpose(1, 0, 2)

    out = constants()
    out["x"] = rows2(v["x"][0])
    out["mem"] = rows2(v["mem_2"][0])
    out["qkv"] = block(v["attn_w_qkv"][0])
    out["wo"] = deep(v["attn_w_o"][0], 2)
    for i in range(2):
        out[f"gu{i}"] = side(pair(v["ffn_w_gate"][i], v["ffn_w_up"][i]), 256)
        out[f"dn{i}"] = deep(v["ffn_w_down"][i], 2)
    ci = v["conv_w_in"][0]
    out["cin"] = np.concatenate([side(pair(ci[:, D:2 * D], ci[:, 2 * D:]), 256), side(ci[:, :D], 256)])
    out["cout"] = deep(v["conv_w_out"][0], 2)
    wi = v["w_in_2"][0]
    out["win"] = np.concatenate([side(wi[:, 0:1024], 256), block(wi[:, 1024:1536]), block(wi[:, 1536:2048]),
                                 side(wi[:, 2056:2568], 256), side(wi[:, 2568:3080], 256), block(wi[:, 3080:3592])])
    out["gatew"] = wi[:, 2048:2056].reshape(KT, P, 8).transpose(1, 0, 2)
    out["gateb"] = np.stack([v["igate_b_2"][0], v["fgate_b_2"][0]], 1)
    out["wout"] = deep(v["w_out_2"][0], 2)
    out["xk"] = side(v["xattn_wkv_2"][0][:, :D], 256)
    out["xv"] = deep(v["xattn_wkv_2"][0][:, D:], 2)
    out["xq"] = side(v["xattn_wq_2"][0], 256)
    out["xo"] = deep(v["xattn_wo_2"][0], 2)
    out["pq"] = side(v["peer_wq_2"][0], 256)
    out["sk"] = v["peer_subkeys_2"][0].reshape(16, P, P).transpose(2, 0, 1).reshape(1, P, CW)
    u = v["peer_u_2"][0].reshape(P, P, KT, P).transpose(0, 3, 2, 1).reshape(P, P, D)
    out["eu"] = u
    out["ev"] = v["peer_v_2"][0].reshape(P, P, D)
    out["convw"] = v["conv_w"][0].reshape(3, KT, P).transpose(2, 1, 0)
    c4 = np.concatenate([v["conv_w_2"][0], v["conv_b_2"]], 0)
    out["conv4"] = c4.reshape(5, 8, P).transpose(2, 1, 0)
    out["lam"] = np.concatenate([v["attn_lambda_q1"], v["attn_lambda_q2"], v["attn_lambda_k1"], v["attn_lambda_k2"]], 1)
    out["subg"] = v["attn_subln_g"]
    rows = {"ln1g0": v["ln1_g"][0], "ln1b0": v["ln1_b"][0], "ln2g0": v["ln2_g"][0], "ln2b0": v["ln2_b"][0],
            "ln1g1": v["ln1_g"][1], "ln1b1": v["ln1_b"][1], "ln2g1": v["ln2_g"][1], "ln2b1": v["ln2_b"][1],
            "mem": v["mem_norm_g_2"][0], "mix": v["mix_norm_g_2"][0],
            "heads": np.concatenate([v["mlstm_norm_g_2"][0], v["sb_norm_g_2"][0]]),
            "xattn": v["xattn_norm_g_2"][0], "ffn": v["ffn_norm_g_2"][0], "final": v["final_norm_g_2"]}
    out["gains"] = np.stack([rows[n] for n in GAINS + ["final"]])
    return {k: np.ascontiguousarray(x) for k, x in out.items()}


def kernel(**inputs):
    from contextlib import ExitStack

    import concourse.bacc as bacc
    from concourse.bass_utils import run_bass_kernel_spmd

    nc = bacc.Bacc("TRN2", target_bir_lowering=False, num_devices=1)
    arrays = layout({k: np.asarray(x) for k, x in inputs.items()})
    aps = {k: nc.dram_tensor("in_" + k, list(x.shape), F32, kind="ExternalInput").ap() for k, x in arrays.items()}
    out = nc.dram_tensor("out_0", [2, P, D], F32, kind="ExternalOutput").ap()
    with ExitStack() as ctx:
        build(nc, aps, out, ctx)
    r = run_bass_kernel_spmd(nc, [{"in_" + k: x for k, x in arrays.items()}], core_ids=[0])
    return np.asarray(r.results[0]["out_0"]).reshape(1, S, D)
```

```python
import numpy as np

import concourse.bass as bass
from concourse import mybir
from concourse.alu_op_type import AluOpType as ALU

F32 = mybir.dt.float32
BF16 = mybir.dt.bfloat16
F32R = mybir.dt.float32r
U32 = mybir.dt.uint32
ACT = mybir.ActivationFunctionType
AX = mybir.AxisListType.X

P = 128
D = 1024
KT = D // P
S = 256
FT = 22
CW = 2048
NR = 3
NS = 3
NG = 3
UW = 1024
UR = 4
US = 3
GB = 4
NA = 3
ALPHA = 4.0 ** 0.25
LAM0 = 0.2
PAUSE = (2, 2)
BASE = 16512

GAINS = ["mem", "ln1g0", "ln1b0", "ln2g0", "ln2b0", "ln1g1", "ln1b1", "ln2g1", "ln2b1",
         "mix", "heads", "xattn", "ffn"]
FEED = (2, 2, 2, 2, 2, 2, 1, 1, 1, 1, 1, 1, 1, 1, 1, 1, 1, 1, 1, 1)
TAILS = (2, 2, 2)
MEMORY = [("xk", i) for i in range(4)] + [("xv", i) for i in range(4)]
M = (3, 4, 5, 6)
STREAM = ([("qkv", 2 * b + i) for b in (0, 2, 4, 1, 3, 5) for i in range(2)] + MEMORY[:M[0]]
          + [("wo", i) for i in range(4)] + MEMORY[M[0]:M[1]]
          + [("gu0", i) for i in range(FT)] + [("dn0", i) for i in range(FT // 2)] + MEMORY[M[1]:M[2]]
          + [("cin", i) for i in range(12)] + [("cout", i) for i in range(4)] + MEMORY[M[2]:M[3]]
          + [("gu1", i) for i in range(FT)] + [("dn1", i) for i in range(FT // 2)] + MEMORY[M[3]:]
          + [("win", i) for i in range(14)] + [("wout", i) for i in (2, 3, 0, 1)]
          + [("xq", i) for i in range(4)] + [("xo", i) for i in range(4)]
          + [("pq", i) for i in range(8)] + [("sk", 0)])
POOLED = ("xk", "xv", "wo", "xq", "xo")
SHARED = ("win", "wout")
HALVES = ("xk", "xv")
STEADY = ("gu0", "cin", "gu1", "pq")
CC = {"cos": (0, 256), "sin": (256, 256), "amask": (512, 512), "cmask": (1024, 512),
      "keep": (1536, 256), "sneg": (1792, 256), "tri": (2048, 128), "ones": (2176, 128)}
CWID = 2304


def flat(items):
    out = []
    for x in items:
        if x is None:
            continue
        if len(x) == 2 and isinstance(x[1], int):
            out.append(x)
        else:
            out += flat(x)
    return out


class Lane:

    def __init__(self, eng, sem, turn=False):
        self.eng, self.sem, self.count, self.seen, self.turn = eng, sem, 0, {}, turn

    def wait(self, *after):
        for sem, value in flat(after):
            if self.seen.get(sem.name, 0) < value:
                self.seen[sem.name] = value
                self.eng.wait_ge(sem, value)

    def __call__(self, fn, *after, sig=True):
        self.wait(after, [(self.sem, self.count - 1)] if self.turn else None)
        r = fn(self.eng)
        if not sig:
            return None
        r.then_inc(self.sem, 1)
        self.count += 1
        return (self.sem, self.count)

    def dma(self, fn, sem, total, *after):
        self.wait(after)
        fn(self.eng).then_inc(sem, 16)
        return (sem, total)


def build(nc, a, out, ctx):
    def sem(name):
        return ctx.enter_context(nc.semaphore(name))

    at = [BASE]

    def sb(name, shape, dt=F32, off=None):
        size = int(np.prod(shape[1:])) * (2 if dt == BF16 else 4)
        size = -(-size // 32) * 32
        if off is None:
            off = at[0]
            at[0] += size
        else:
            o = off[0]
            off[0] += size
            assert off[0] <= nc.sbuf_usable_end, (name, off[0], nc.sbuf_usable_end)
            off = o
        return nc.alloc_sbuf_tensor_at(name, list(shape), dt, offset=off)

    PE, AC, DV, GP, SP = (Lane(e, sem(n), t) for e, n, t in (
        (nc.tensor, "s_pe", False), (nc.scalar, "s_act", True), (nc.vector, "s_dve", True),
        (nc.gpsimd, "s_pool", False), (nc.sync, "s_sp", False)))

    banks = ctx.enter_context(nc.psum_tensor("banks", [P, 8, 512], F32))
    ps = [banks[:, i, :] for i in range(8)]
    free = [[] for _ in range(8)]

    raw = [sb(f"raw{i}", [P, CW]) for i in range(2)]
    xH = sb("xH", [P, KT, S], F32R)
    xL = sb("xL", [P, KT, S], F32R)
    ident = sb("ident", [P, P])
    iota = sb("iota", [P, P])
    mv = sb("mv", [P, 2, 4])
    rs = sb("rs", [P, 2, 4])
    eps = sb("eps", [P, 2])
    lamv = sb("lamv", [P, 8])
    OX = at[0]
    raw += [sb("raw2", [P, CW])]
    wH = [sb(f"wH{i}", [P, CW], F32R) for i in range(NS)]
    wL = [sb(f"wL{i}", [P, CW], F32R) for i in range(NS)]
    h = sb("h", [P, 2, D])
    gn = [sb(f"gn{i}", [P, D]) for i in range(NG)]
    junk = sb("junk", [P, D], BF16)
    OV = at[0]

    s_raw = [sem(f"s_raw{i}") for i in range(NR)]
    s_gn = [sem(f"s_gn{i}") for i in range(NG)]
    s_x, s_id, s_cst, s_lam, s_sub, s_mem, s_cw, s_c4, s_gw, s_gb = (
        sem(n) for n in ("s_x0", "s_id", "s_cst", "s_lam", "s_sub", "s_mem", "s_cw", "s_c4", "s_gw", "s_gb"))
    s_out, s_hs, s_gl, s_x1, s_iota = sem("s_out"), sem("s_hs"), sem("s_gl"), sem("s_x1"), sem("s_iota")
    hs = nc.dram_tensor("h_scratch", [P, 2, D], F32).ap()
    gel = nc.dram_tensor("gelu_scratch", [P, P, S], F32).ap()

    id_t = SP.dma(lambda e: e.dma_start(ident[:, :], a["ident"]), s_id, 16)

    split_a, split_v, done, raw_t = {}, {}, {}, {}

    def fetch(n):
        if n >= len(STREAM):
            return
        name, i = STREAM[n]
        r = n % NR
        raw_t[n] = SP.dma(lambda e: e.dma_start(raw[r][:, :], a[name][i]), s_raw[r], 16 * (n // NR + 1),
                          split_a.get(n - NR), split_v.get(n - NR))

    nsplit = [0]

    def split(upto):
        while nsplit[0] < min(upto, len(STREAM)):
            n = nsplit[0]
            r, s = n % NR, n % NS
            name, i = STREAM[n]
            lane = GP if name in POOLED or (name == "qkv" and n >= 6) or (name in SHARED and n % 2) or (name in STEADY and i < NS) else DV
            split_a[n], split_v[n] = [], []
            parts = [slice(0, CW // 2), slice(CW // 2, CW)] if n == 0 or name in HALVES or (name in STEADY and i < 1) else [slice(0, CW)]
            for c in parts:
                split_a[n].append(AC(lambda e: e.activation(wH[s][:, c], raw[r][:, c], ACT.Copy), raw_t[n], done[n - NS] if n >= NS else None))
                split_v[n].append(lane(lambda e: e.tensor_tensor(wL[s][:, c], raw[r][:, c], wH[s][:, c].bitcast(F32), ALU.subtract),
                                       split_a[n], done[n - NS] if n >= NS else None))
            fetch(n + NR)
            nsplit[0] += 1

    nuse = [0]

    def take(name, i, ahead=NS):
        n = nuse[0]
        assert STREAM[n] == (name, i), (STREAM[n], name, i)
        nuse[0] += 1
        split(n + ahead)
        return n, wH[n % NS], wL[n % NS], [[split_a[n][i], split_v[n][i]] for i in (0, -1)]

    def ahead():
        split(nuse[0] + NS)

    gain_t, gain_use = {}, {}

    def load_gain(n):
        if n >= len(GAINS):
            return
        g = n % NG
        gain_t[n] = GP.dma(lambda e: e.dma_start(gn[g][:, :], a["gains"][n:n + 1, :].broadcast_to([P, D])),
                           s_gn[g], 16 * (n // NG + 1), gain_use.get(n - NG))

    def gain(name):
        n = GAINS.index(name)
        return gn[n % NG], gain_t[n]

    def gain_used(name, tok):
        n = GAINS.index(name)
        gain_use[n] = tok
        load_gain(n + NG)

    x_t = [SP.dma(lambda e, j=j: e.dma_start(h[:, j, :], a["x"][:, j, :]), (s_x, s_x1)[j], 16) for j in range(2)]
    for n in range(NR):
        fetch(n)
    GP.wait(raw_t[NR - 1])
    for n in range(NG):
        load_gain(n)

    def mm(o, l, r, start, stop, *after, sig=False):
        return PE(lambda e: e.matmul(o, l, r, start=start, stop=stop), *after, sig=sig)

    def transpose(o, i, *after, sig=False):
        k = i.shape[0]
        return PE(lambda e: e.transpose(o, i, ident[:k, :k]), *after, sig=sig)

    def whole(g):
        while True:
            try:
                next(g)
            except StopIteration as end:
                return end.value

    def cols(bank, off, H, L, wh, wl, wcol, after, xt):
        for k in range(KT):
            w0 = k * 256 + wcol
            o = ps[bank][:, off:off + S]
            mm(o, wh[:, w0:w0 + P], H[:, k, :], k == 0, False, xt[k // 4], after[k // 4], free[bank] if k == 0 else None)
            mm(o, wh[:, w0:w0 + P], L[:, k, :], False, False)
            t = mm(o, wl[:, w0:w0 + P], H[:, k, :], False, k == KT - 1, sig=k == KT - 1)
        return t

    def pair_cols(name, c, bank, H, L, xt):
        idx, wh, wl, wt = take(name, c)
        cols(bank, 0, H, L, wh, wl, 0, wt, xt)
        yield
        t = cols(bank, S, H, L, wh, wl, P, wt, xt)
        done[idx] = t
        return t

    def rows(name, order, H, L, after, tail=1):
        order = list(order)
        n = len(order) - tail

        def piece(c, w_, t, kk, begin, end, sig):
            idx, wh, wl, wt = w_
            k = 2 * c + kk
            ts = slice(t * P, t * P + P)
            for part_, (l, w) in enumerate(((H, wh), (H, wl), (L, wh))):
                for e in range(2):
                    b = 2 * t + e
                    w0 = kk * D + e * 512
                    first, last = begin and part_ == 0, end and part_ == 2
                    tok = mm(ps[b][:, :], l[:, k, ts], w[:, w0:w0 + 512], first, last, after[c], wt[kk], free[b] if first else None,
                             sig=last or (sig and part_ == 2 and e == 1))
                    if last:
                        free[b] = [tok]
            return tok

        for i, c in enumerate(order[:n]):
            w_ = take(name, c)
            for kk in range(2):
                for t in range(2):
                    tok = piece(c, w_, t, kk, i == 0 and kk == 0, False, kk == 1 and t == 1)
                if kk == 0:
                    yield
            done[w_[0]] = tok
            yield
        ws = [take(name, c, NS - i) for i, c in enumerate(order[n:])]
        for t in range(2):
            for i, (c, w_) in enumerate(zip(order[n:], ws)):
                for kk in range(2):
                    end = i == tail - 1 and kk == 1
                    tok = piece(c, w_, t, kk, n == 0 and i == 0 and kk == 0, end, t == 1 and kk == 1)
                if t == 1:
                    done[w_[0]] = tok
            if t == 0:
                yield
        return [free[b][0] for b in range(4)]

    def blocks(name, c0, H, L, bank, xt):
        for c in range(2):
            idx, wh, wl, wt = take(name, c0 + c)
            for kk in range(4):
                k = 4 * c + kk
                for t in range(2):
                    ts = slice(t * P, t * P + P)
                    for part_, (l, w) in enumerate(((H, wh), (H, wl), (L, wh))):
                        last = k == KT - 1 and part_ == 2
                        tok = mm(ps[bank + t][:, :], l[:, k, ts], w[:, kk * 512:kk * 512 + 512], k == 0 and part_ == 0,
                                 last, xt[c], wt[kk // 2], free[bank + t] if k == 0 else None,
                                 sig=last or (kk == 3 and t == 1 and part_ == 2))
                        if last:
                            free[bank + t] = [tok]
                if kk == 1:
                    yield
            done[idx] = tok
            if c == 0:
                yield
        return [free[bank][0], free[bank + 1][0]]

    def part(dH, dL, src, *after):
        t1 = AC(lambda e: e.activation(dH, src, ACT.Copy), after)
        t2 = DV(lambda e: e.tensor_tensor(dL, src, dH.bitcast(F32), ALU.subtract), t1, after)
        return [t1, t2]

    def turn_half(nat, j, toks, H, L, after=None, banks_=(4, 5, 6, 7)):
        out_t = []
        for q in range(2):
            b = banks_[2 * j + q]
            for i in range(4):
                k = 4 * q + i
                t = transpose(ps[b][:, i * P:i * P + P], nat[:, j, k * P:k * P + P], toks[q], free[b], id_t, sig=i == 3)
            src = ps[b][:, :].rearrange("p (k t) -> p k t", k=4)
            r = part(H[:, 4 * q:4 * q + 4, j * P:j * P + P], L[:, 4 * q:4 * q + 4, j * P:j * P + P], src, t, after)
            free[b] = [r[1]]
            out_t.append(r)
        return out_t

    def turn(nat, toks, H, L):
        return [list(x) for x in zip(*(turn_half(nat, j, toks[j], H, L) for j in range(2)))]

    def turn_cols(name, bank, nat, toks, H, L, more=0):
        keep = [whole(mem_chunk(i)) for i in range(more)]
        xt = turn(nat, toks, H, L)
        t = whole(pair_cols(name, 0, bank, H, L, xt))
        for f in keep:
            f()
        return t, xt

    def warm(fn):
        AC(lambda e: e.activation(lamv[:, 7:8], ident[:, 0:1], fn), id_t, (AC.sem, AC.count))

    def root(dst, src, mul, e, after):
        t = AC(lambda eng: eng.activation(src, src, ACT.Sqrt, scale=mul, bias=eps[:, e:e + 1]), after, eps_t)
        return lambda: DV(lambda eng: eng.reciprocal(dst, src), t)

    junk_t = [None]

    def square(src, bias, total, *after):
        if bias is None:
            junk_t[0] = AC(lambda e: e.activation(junk[:, :], src, ACT.Square, accum_out=total), after, junk_t[0])
        else:
            junk_t[0] = AC(lambda e: e.activation(junk[:, :], src, ACT.Square, bias=bias, accum_out=total), after, junk_t[0])
        return junk_t[0]

    def add_norm(banks_t, g, b, tmp, early=True, then=None):
        (gw, gt), (bw, bt) = gain(g), gain(b)
        half = [slice(0, 512), slice(512, D)]

        def add(j):
            t = []
            for e2 in range(2):
                hv = h[:, j, half[e2]]
                t.append(DV(lambda e: e.scalar_tensor_tensor(hv, hv, ALPHA, ps[2 * j + e2][:, :], ALU.mult, ALU.add,
                                                             accum_out=mv[:, j, e2:e2 + 1]), banks_t[2 * j + e2]))
                free[2 * j + e2] = [t[-1]]
            m = DV(lambda e: e.tensor_scalar(mv[:, j, 2:3], mv[:, j, 0:1], mv[:, j, 1:2], -1.0 / D, ALU.add, ALU.mult), t)
            return [t, m, square(h[:, j, :], mv[:, j, 2:3], rs[:, j, 0:1], m, t)]

        def scale(dst, j, after):
            return DV(lambda e: e.scalar_tensor_tensor(dst, h[:, j, :], mv[:, j, 2:3], gw[:, :], ALU.add, ALU.mult), after, gt)

        def shift(src, j, t, after):
            return [DV(lambda e, q=q: e.scalar_tensor_tensor(h[:, j, half[q]], src[:, half[q]], rs[:, j, 1:2], bw[:, half[q]], ALU.mult, ALU.add),
                       after, t, bt) for q in range(2)]

        s0 = add(0)
        a0 = scale(tmp[0], 0, s0[:2])
        r0 = root(rs[:, 0, 1:2], rs[:, 0, 0:1], 1.0 / D, 0, s0[2])
        if not early:
            s1 = add(1)
        res = [shift(tmp[0], 0, r0(), [a0, s0])]
        if then is not None:
            f0 = then(0, res[0])
        split(nuse[0] + 2)
        if early:
            s1 = add(1)
        r1 = root(rs[:, 1, 1:2], rs[:, 1, 0:1], 1.0 / D, 0, s1[2])
        a1 = scale(tmp[1], 1, s1[:2])
        n_t = [f0()] if then is not None else []
        res.append(shift(tmp[1], 1, r1(), [a1, s1]))
        if then is not None:
            n_t.append(then(1, res[1])())
        gain_used(g, res[1])
        gain_used(b, res[1])
        return (res, n_t) if then is not None else res

    def rms(src, j, toks, nat, g, after=None):
        gw, gt = gain(g)
        r = root(rs[:, j, 3:4], rs[:, j, 2:3], 1.0 / D, 1, square(src[:, j, :], None, rs[:, j, 2:3], toks))

        def rest():
            t = r()
            res = []
            for q in range(2):
                cs = slice(512 * q, 512 * q + 512)
                res.append(DV(lambda e: e.scalar_tensor_tensor(nat[:, j, cs], src[:, j, cs], rs[:, j, 3:4], gw[:, cs], ALU.mult, ALU.mult),
                              t, gt, toks, after))
            if j:
                gain_used(g, res)
            return res

        return rest

    def add_rms(banks_t, nat, g, after=None):
        sums, res = [], []
        for j in range(2):
            sums.append([])
            for e2 in range(2):
                k = 2 * j + e2
                hv = h[:, j, e2 * 512:e2 * 512 + 512]
                sums[j].append(DV(lambda e: e.tensor_tensor(hv, hv, ps[k][:, :], ALU.add), banks_t[k]))
                free[k] = [sums[j][-1]]
            res.append(rms(h, j, sums[j], nat, g, after))
        return sums, [f() for f in res]

    o = [OV]
    cst = sb("cst", [P, CWID], off=o)
    xk = sb("xk", [P, KT, S], off=o)
    xv = sb("xv", [P, 2, D], off=o)
    OW = o[0]

    def const(name):
        c0, n = CC[name]
        return cst[:, c0:c0 + n]

    QK = sb("QK", [P, 2, 2048], off=o)
    oH = sb("oH", [P, KT, S], F32R, off=[OW])
    oL = sb("oL", [P, KT, S], F32R, off=[OW + 8192])
    nat = sb("nat", [P, 2, D], off=[o[0]])
    QT = sb("QT", [P, 8, S], off=o)
    nat2 = sb("nat2", [P, 2, D], off=[o[0]])
    KTt = sb("KT", [P, 8, S], off=o)
    V = sb("V", [P, 2, D], off=o)
    lq = sb("lq", [P, 4, 64], off=o)
    lpr = sb("lpr", [P, 2, 64], off=o)
    sub = sb("sub", [P, P], off=o)
    Sm = [sb(f"Sm{i}", [P, 2, S], off=o) for i in range(2)]
    AT = [sb(f"AT{i}", [P, 2, P], off=o) for i in range(2)]
    Og = [sb(f"Og{i}", [P, 4, P], off=o) for i in range(2)]
    mH = sb("mH", [P, KT, S], F32R, off=o)
    mL = sb("mL", [P, KT, S], F32R, off=o)
    Am = [sb(f"Am{i}", [P, S], off=o) for i in range(2)]
    sm = [sb(f"sm{i}", [P, 8], off=o) for i in range(2)]
    ss = [sb(f"ss{i}", [P, 2, 4], off=o) for i in range(2)]
    rot = sb("rot", [P, 4, 64], off=o)

    cst_t = SP.dma(lambda e: e.dma_start(cst[:, :], a["consts"]), s_cst, 16)
    lam_t = SP.dma(lambda e: e.dma_start(lq[:, :, :].rearrange("p a b -> p (a b)"), a["lam"].broadcast_to([P, 256])), s_lam, 16)
    sub_t = SP.dma(lambda e: e.dma_start(sub[:, :], a["subg"].broadcast_to([P, P])), s_sub, 16)
    mem_t = SP.dma(lambda e: e.dma_start(nat[:, :, :], a["mem"]), s_mem, 16)
    iota_t = SP.dma(lambda e: e.dma_start(iota[:, :], a["iota"]), s_iota, 16)

    eps_t = [DV(lambda e, i=i, v=v: e.memset(eps[:, i:i + 1], v)) for i, v in enumerate((1e-5, 1e-6))]
    xt = turn(h, [[x_t[0]] * 2, [x_t[1]] * 2], xH, xL)

    qk_t, T_t = {}, {}

    def qkv_keep(blk, bank, bt):
        for j in range(2):
            if blk < 4:
                dst, sc = QK[:, j, blk * 512:blk * 512 + 512], (0.125 if blk < 2 else 1.0)
            else:
                dst, sc = V[:, j, (blk - 4) * 512:(blk - 4) * 512 + 512], 1.0
            t = AC(lambda e: e.activation(dst, ps[bank + j][:, :], ACT.Copy, scale=sc), bt[j])
            free[bank + j] = [t]
            qk_t[blk, j] = t

    def rope(w, q):
        res = []
        for j in range(2):
            z = QK[:, j, w * D + q * 512:w * D + q * 512 + 512].rearrange("p (g d) -> p g d", d=64)
            x1, x2 = z[:, :, 0:8], z[:, :, 8:16]
            c = const("cos")[:, j * P:j * P + 64].rearrange("p (g d) -> p g d", d=8)
            s = const("sin")[:, j * P:j * P + 64].rearrange("p (g d) -> p g d", d=8)
            r = [rot[:, i, :].rearrange("p (g d) -> p g d", d=8) for i in range(4)]
            dep = [qk_t[2 * w + q, j], cst_t, list(rope_t)]
            m = [DV(lambda e, n=n, u=u, v=v: e.tensor_tensor(r[n], u, v, ALU.mult), dep)
                 for n, u, v in ((0, x1, c), (1, x2, s), (2, x2, c), (3, x1, s))]
            t = DV(lambda e: e.tensor_tensor(x1, r[0], r[1], ALU.subtract), m)
            res.append([dep, t, DV(lambda e: e.tensor_tensor(x2, r[2], r[3], ALU.add), m)])
            rope_t[:] = res[-1][1:]
        return res

    rope_t = []
    mt = []

    def qk_turn(w, q, toks, bank):
        dst = QT if w == 0 else KTt
        for j in range(2):
            b = bank + j
            for i in range(4):
                hd = 4 * q + i
                tt = transpose(ps[b][:, i * P:i * P + P], QK[:, j, w * D + hd * P:w * D + hd * P + P], toks[j], free[b], sig=i == 3)
            src = ps[b][:, :].rearrange("p (k t) -> p k t", k=4)
            T_t[w, j, q] = AC(lambda e: e.activation(dst[:, 4 * q:4 * q + 4, j * P:j * P + P], src, ACT.Copy), tt, mn_t, mt)
            free[b] = [T_t[w, j, q]]

    mem_n, kx_t, v_t = [0], {}, []

    def mem_chunk(bank):
        name, c = MEMORY[mem_n[0]]
        mem_n[0] += 1
        if name == "xk":
            t = yield from pair_cols(name, c, bank, mH, mL, mt)
            dst, src = xk[:, 2 * c:2 * c + 2, :].rearrange("p a t -> p (a t)"), ps[bank][:, :]
        else:
            idx, wh, wl, wt = take(name, c)
            for j in range(2):
                ov, ts = ps[bank][:, j * S:j * S + S], slice(j * P, j * P + P)
                for k in range(KT):
                    kc = slice(k * S, k * S + S)
                    mm(ov, mH[:, k, ts], wh[:, kc], k == 0, False, mt[k // 4], wt[k // 4], free[bank] if k == 0 else None)
                    mm(ov, mH[:, k, ts], wl[:, kc], False, False)
                    t = mm(ov, mL[:, k, ts], wh[:, kc], False, k == KT - 1, sig=k == KT - 1)
                if j == 0:
                    yield
            done[idx] = t
            dst, src = xv[:, :, c * S:c * S + S], ps[bank][:, :].rearrange("p (j n) -> p j n", j=2)

        def keep():
            k_t = AC(lambda e: e.activation(dst, src, ACT.Copy), t)
            free[bank] = [k_t]
            if name == "xk":
                kx_t[c] = k_t
            else:
                v_t.append(k_t)

        return keep

    qkv_keep(0, 0, whole(blocks("qkv", 0, xH, xL, 0, xt)))
    t = DV(lambda e: e.tensor_tensor(lpr[:, :, :], lq[:, 0:2, :], lq[:, 2:4, :], ALU.mult), lam_t)
    t = DV(lambda e: e.reduce_sum(lamv[:, 0:2], lpr[:, :, :], AX), t)
    t = AC(lambda e: e.activation(lamv[:, 2:4], lamv[:, 0:2], ACT.Exp), t)
    t = DV(lambda e: e.tensor_tensor(lamv[:, 4:5], lamv[:, 3:4], lamv[:, 2:3], ALU.subtract), t)
    nlam_t = DV(lambda e: e.tensor_scalar(lamv[:, 5:6], lamv[:, 4:5], LAM0, None, ALU.subtract), t)
    sub_t = DV(lambda e: e.tensor_scalar(sub[:, :], sub[:, :], 1.0 - LAM0, None, ALU.mult), sub_t)
    mn_t = [f() for f in [rms(nat, j, mem_t, nat2, "mem") for j in range(2)]]
    qkv_keep(2, 2, whole(blocks("qkv", 4, xH, xL, 2, xt)))
    rope_q = rope(0, 0)
    mt += turn(nat2, mn_t, mH, mL)
    v0 = blocks("qkv", 8, xH, xL, 0, xt)
    next(v0)
    rope_k = rope(1, 0)
    qk_turn(0, 0, rope_q, 4)
    next(v0)
    qk_turn(1, 0, rope_k, 6)

    units = [(hd, j) for hd in range(8) for j in range(2)]
    at_p, use_p, AT_t, O_t, on_t, o_t = {}, {}, {}, {}, {}, {}

    def att_scores(u):
        hd, j = units[u]
        i, nk, q = u % 2, P * (j + 1), hd // 4
        dep = [T_t[0, j, q]] + [T_t[1, jj, q] for jj in range(j + 1)]
        for c in range(2):
            cs = slice(64 * c, 64 * c + 64)
            t = mm(ps[4 + c][:, 0:nk], QT[cs, hd, j * P:j * P + P], KTt[cs, hd, 0:nk], True, True,
                   dep, free[4 + c], sig=c == 1)
        sv = Sm[i][:, :, 0:nk]
        mk = const("amask")[:, j * S:j * S + nk].unsqueeze(1).broadcast_to([P, 2, nk])
        t = DV(lambda e: e.tensor_tensor(sv, banks[:, 4:6, 0:nk], mk, ALU.add), t, use_p.get(u - 2))
        free[4] = free[5] = [t]
        m = sm[i]
        t = DV(lambda e: e.tensor_reduce(m[:, 0:2], sv, AX, ALU.max, negate=True), t)
        ex = [AC(lambda e, c=c: e.activation(Sm[i][:, c, 0:nk], Sm[i][:, c, 0:nk], ACT.Exp, bias=m[:, c:c + 1],
                                             accum_out=m[:, 2 + c:3 + c]), t) for c in range(2)]
        t = DV(lambda e: e.reciprocal(m[:, 4:6], m[:, 2:4]), ex)
        t2 = DV(lambda e: e.tensor_scalar(m[:, 6:7], m[:, 5:6], lamv[:, 5:6], None, ALU.mult), t, nlam_t)
        t = DV(lambda e: e.tensor_scalar(Sm[i][:, 0, 0:nk], Sm[i][:, 0, 0:nk], m[:, 4:5], None, ALU.mult), t)
        at_p[u] = DV(lambda e: e.scalar_tensor_tensor(Am[i][:, 0:nk], Sm[i][:, 1, 0:nk], m[:, 6:7], Sm[i][:, 0, 0:nk],
                                                      ALU.mult, ALU.add), t, t2, use_p.get(u - 2))

    def att_turn(u):
        hd, j = units[u]
        b, i = 6 + u % 2, u % 2
        for k in range(j + 1):
            t = transpose(ps[b][:, k * P:k * P + P], Am[i][:, k * P:k * P + P], at_p[u], free[b], sig=k == j)
        use_p[u] = t
        AT_t[u] = AC(lambda e: e.activation(AT[i][:, 0:j + 1, :].rearrange("p a b -> p (a b)"), ps[b][:, 0:P * (j + 1)], ACT.Copy), t, O_t.get(u - 2))

    def att_out(u):
        hd, j = units[u]
        b, i, g, n = 6 + u % 2, u % 2, u // 4 % 2, u % 4
        ov = ps[b][:, S:S + P]
        for k in range(j + 1):
            t = mm(ov, AT[i][:, k, :], V[:, k, hd * P:hd * P + P], k == 0, k == j, AT_t[u], qk_t[4 + hd // 4, k], sig=k == j)
        t1 = AC(lambda e: e.activation(Og[g][:, n, :], ov, ACT.Copy), t, o_t.get(u // 4 - 2))
        t2 = AC(lambda e: e.activation(junk[:, 0:P], ov, ACT.Square, accum_out=ss[g][:, 0, n:n + 1]), t, junk_t[0], on_t.get(u // 4 - 2))
        junk_t[0] = t2
        O_t[u] = [t1, t2]
        free[b] = [t1, t2]

    def att_norm(g):
        s = ss[g % 2]
        t = root(s[:, 1, :], s[:, 0, :], 1.0 / P, 0, [O_t[u] for u in range(4 * g, 4 * g + 4)])()
        on_t[g] = [DV(lambda e, n=n: e.scalar_tensor_tensor(Og[g % 2][:, n, :], Og[g % 2][:, n, :], s[:, 1, n:n + 1], sub[:, :], ALU.mult, ALU.mult),
                      t, sub_t) for n in range(4)]

    def att_join(g, b):
        for n in range(4):
            t = transpose(ps[b][:, n * P:n * P + P], Og[g % 2][:, n, :], on_t[g], free[b], sig=n == 3)
        src = ps[b][:, :].rearrange("p (k t) -> p k t", k=2)
        o_t[g] = part(oH[:, 2 * g:2 * g + 2, :], oL[:, 2 * g:2 * g + 2, :], src, t, [T_t[x] for x in T_t])
        assert len(T_t) == 8
        free[b] = [o_t[g][1]]

    wo_t = []

    def att_fill():
        qkv_keep(4, 0, (yield from v0))
        yield
        qkv_keep(1, 2, (yield from blocks("qkv", 2, xH, xL, 2, xt)))
        rq = rope(0, 1)
        yield
        k1 = blocks("qkv", 6, xH, xL, 0, xt)
        yield next(k1)
        yield next(k1)
        qk_turn(0, 1, rq, 2)
        qkv_keep(3, 0, (yield from k1))
        rk = rope(1, 1)
        yield
        v1 = blocks("qkv", 10, xH, xL, 2, xt)
        yield next(v1)
        yield next(v1)
        qk_turn(1, 1, rk, 0)
        qkv_keep(5, 2, (yield from v1))
        yield
        for i in range(M[0]):
            (yield from mem_chunk(i % 2))()
            yield
        wo_t.extend((yield from rows("wo", range(4), oH, oL, o_t)))

    fill = att_fill()
    for u in range(20):
        if 2 <= u < 18:
            att_turn(u - 2)
        if u < 16:
            att_scores(u)
        if u >= 6 and u % 4 == 2:
            att_norm(u // 4 - 1)
        if u >= 7 and u % 4 == 3:
            att_join(u // 4 - 1, 6 + (u + 1) % 2)
        for _ in range(FEED[u]):
            next(fill)
        if 2 <= u < 18:
            att_out(u - 2)
    warm(ACT.Sqrt)
    for _ in fill:
        pass
    ln_t = add_norm(wo_t, "ln1g0", "ln1b0", [nat[:, 0, :], nat[:, 1, :]], False)

    o = [OW]
    fH = sb("fH", [P, FT, S], F32R, off=o)
    fL = sb("fL", [P, FT, S], F32R, off=o)
    tmp = [sb(f"tmp{i}", [P, D], off=[o[0] + 4096 * i]) for i in range(2)]
    tmp = [x[:, :] for x in tmp]
    sg = [sb(f"sg{i}", [P, S], off=o) for i in range(2)]
    fv = [sb(f"fv{i}", [P, S], off=o) for i in range(2)]
    o = [o[0] + 4096]

    def swiglu(layer, toks):
        f_t = []
        for f in range(FT):
            b, i = 4 + f % 4, f % 2
            if f == 0:
                tu, xt = turn_cols(f"gu{layer}", b, h, toks, xH, xL, M[1 + 2 * layer] - M[2 * layer])
            else:
                tu = whole(pair_cols(f"gu{layer}", f, b, xH, xL, xt))
            old = f_t[f - 2] if f >= 2 else None
            t1 = AC(lambda e: e.activation(sg[i][:, :], ps[b][:, 0:S], ACT.Silu), tu, old)
            t2 = DV(lambda e: e.tensor_tensor(fv[i][:, :], sg[i][:, :], ps[b][:, S:2 * S], ALU.mult), t1, old)
            free[b] = [t2]
            t3 = AC(lambda e: e.activation(fH[:, f, :], fv[i][:, :], ACT.Copy), t2)
            f_t.append([t3, DV(lambda e: e.tensor_tensor(fL[:, f, :], fv[i][:, :], fH[:, f, :].bitcast(F32), ALU.subtract), t3)])
        warm(ACT.Sqrt)
        return whole(rows(f"dn{layer}", range(FT // 2), fH, fL, [f_t[2 * c:2 * c + 2] for c in range(FT // 2)], TAILS[2 * layer]))

    ln_t = add_norm(swiglu(0, ln_t), "ln2g0", "ln2b0", tmp)

    o = [OW + 8192]
    yc = sb("yc", [P, KT, S], off=o)
    up = [sb(f"up{i}", [P, S + 2], off=o) for i in range(2)]
    cw = sb("cw", [P, KT, 3], off=o)
    cw_t = GP.dma(lambda e: e.dma_start(cw[:, :, :], a["convw"]), s_cw, 16, wo_t)
    pad_t = [DV(lambda e, i=i: e.memset(up[i][:, 0:2], 0.0)) for i in range(2)]
    y_t = []
    for c in range(8):
        b, i = 4 + c % 4, c % 2
        if c == 0:
            tu, xt = turn_cols("cin", b, h, ln_t, xH, xL, M[2] - M[1])
        else:
            tu = whole(pair_cols("cin", c, b, xH, xL, xt))
        prev = y_t[c - 2] if c >= 2 else None
        t1 = AC(lambda e: e.activation(sg[i][:, :], ps[b][:, 0:S], ACT.Copy), tu, prev)
        t2 = DV(lambda e: e.tensor_tensor(up[i][:, 2:S + 2], sg[i][:, :], ps[b][:, S:2 * S], ALU.mult), t1, prev, pad_t)
        free[b] = [t2]
        t = DV(lambda e: e.tensor_scalar(yc[:, c, :], up[i][:, 0:S], cw[:, c, 0:1], None, ALU.mult), t2, cw_t, pad_t)
        for q in (1, 2):
            t = DV(lambda e, q=q: e.scalar_tensor_tensor(yc[:, c, :], up[i][:, q:S + q], cw[:, c, q:q + 1], yc[:, c, :], ALU.mult, ALU.add), t)
        y_t.append(t)
    z_t = []
    for c in range(4):
        idx, wh, wl, wt = take("cin", 8 + c)
        for q in range(2):
            n = 2 * c + q
            b, i = 4 + n % 4, n % 2
            tb = cols(b, 0, xH, xL, wh, wl, q * P, wt, xt)
            t2 = DV(lambda e: e.tensor_tensor(fv[i][:, :], yc[:, n, :], ps[b][:, 0:S], ALU.mult), tb, y_t[n], z_t[n - 2] if n >= 2 else None)
            free[b] = [t2]
            t3 = AC(lambda e: e.activation(fH[:, n, :], fv[i][:, :], ACT.Copy), t2)
            z_t.append([t3, DV(lambda e: e.tensor_tensor(fL[:, n, :], fv[i][:, :], fH[:, n, :].bitcast(F32), ALU.subtract), t3)])
        done[idx] = tb
    warm(ACT.Sqrt)
    ln_t = add_norm(whole(rows("cout", range(4), fH, fL, [z_t[2 * c:2 * c + 2] for c in range(4)], TAILS[1])), "ln1g1", "ln1b1", tmp)
    dn_t = swiglu(1, ln_t)

    o = [OW]
    ct = sb("ct", [P, 8, 5], off=o)
    gwt = sb("gwt", [P, KT, 8], off=o)
    gbt = sb("gbt", [4, 2], off=o)
    selt = sb("selt", [4, 4, P], off=o)
    qp = [sb(f"qp{i}", [P, 2, S + 3], off=o) for i in range(2)]
    xm = sb("xm", [P, 2, D], off=[o[0]])
    qm = sb("qm", [P, 8, S], off=[o[0]])
    qs = sb("qs", [P, 4, S], off=o)
    ks = sb("ks", [P, 4, S], off=o)
    vm = sb("vm", [P, 2, 512], off=o)
    og = sb("og", [P, 2, 512], off=o)
    vs = sb("vs", [P, 2, 512], off=o)
    gi_i = sb("gi", [4, S], off=o)
    og2 = [o[0]]
    g_f, g1, g2, gB, gmm, gng = (sb(f"gi{i}", [4, S], off=og2) for i in range(6))
    Wt = [sb(f"Wt{i}", [P, S], off=o) for i in range(2)]
    Pm = [sb(f"Pm{i}", [P, S], off=o) for i in range(2)]
    PT = [sb(f"PT{i}", [P, 2, P], off=o) for i in range(2)]
    gc = sb("gc", [P, 2, 2, 4], off=o)
    dn = [sb(f"dn{i}", [P, 4], off=o) for i in range(4)]
    zs = sb("zs", [P, 4, 384], off=o)
    ze = sb("ze", [P, 4, 384], off=o)
    sO = sb("sO", [P, 2, 256], off=o)
    sq = sb("sq", [P, 2, 256], off=o)
    mO = [sb(f"mO{i}", [P, 4, P], off=o) for i in range(2)]
    s8 = [sb(f"s8{i}", [P, 2, 8], off=o) for i in range(4)]
    eH = sb("eH", [P, KT, S], F32R, off=o)
    eL = sb("eL", [P, KT, S], F32R, off=o)
    c4_t = GP.dma(lambda e: e.dma_start(ct[:, :, :], a["conv4"]), s_c4, 16, dn_t)
    GP.dma(lambda e: e.dma_start(gwt[:, :, :], a["gatew"]), s_gw, 16, dn_t)
    GP.dma(lambda e: e.dma_start(gbt[:, :], a["gateb"]), s_gw, 32, dn_t)
    gw_t = GP.dma(lambda e: e.dma_start(selt[:, :, :], a["sel"]), s_gw, 48, dn_t)
    ln_t, n_t = add_norm(dn_t, "ln2g1", "ln2b1", tmp, then=lambda j, t: rms(h, j, t, xm, "mix", dn_t))
    pad_t = [DV(lambda e, i=i: e.memset(qp[i][:, :, 0:3], 0.0), dn_t) for i in range(2)]
    def gates_turn():
        for j in range(2):
            transpose(ps[7][:, 8 * j:8 * j + 4], gmm[:, j * P:j * P + P], t_mm, free[7])
            t = transpose(ps[7][:, 8 * j + 4:8 * j + 8], gng[:, j * P:j * P + P], t_ng, sig=True)
        gcv = ps[7][:, 0:16].rearrange("p (j a b) -> p j a b", j=2, a=2)
        t1 = DV(lambda e: e.tensor_scalar(gc[:, :, 0, :], gcv[:, :, 0, :], -1.0, None, ALU.mult), t)
        t2 = DV(lambda e: e.tensor_copy(gc[:, :, 1, :], gcv[:, :, 1, :]), t)
        free[7] = [t2]
        return [t1, t2]

    hg, hg_t = gain("heads")
    sq_t = {}

    def st_heads(w, c, t=None):
        b = 4 + 2 * w + c
        t = t or whole(pair_cols("win", 2 * w + c, b, xH, xL, xt))
        dst = (qs if w == 0 else ks)[:, 2 * c:2 * c + 2, :].rearrange("p a t -> p (a t)")
        sq_t[w, c] = AC(lambda e: e.activation(dst, ps[b][:, :], ACT.Copy, scale=0.125 if w == 0 else 1.0), t, n_t, xt)
        free[b] = [sq_t[w, c]]

    t, xt = turn_cols("win", 4, xm, n_t, xH, xL, 8 - M[3])
    st_heads(0, 0, t)
    for g in range(2):
        for k in range(KT):
            for part_, (H, sig_) in enumerate(((xH, False), (xL, k == KT - 1))):
                t = mm(ps[0][0:4, g * S:g * S + S], gwt[:, k, 4 * g:4 * g + 4], H[:, k, :].bitcast(F32),
                       k == 0 and part_ == 0, k == KT - 1 and part_ == 1, xt, gw_t, free[0], sig=sig_ and g == 1)
    t_i = DV(lambda e: e.tensor_scalar(gi_i[:, :], ps[0][0:4, 0:S], gbt[:, 0:1], None, ALU.add), t, gw_t)
    t_f = DV(lambda e: e.tensor_scalar(g_f[:, :], ps[0][0:4, S:2 * S], gbt[:, 1:2], None, ALU.add), t, gw_t)
    free[0] = [t_f]
    t = DV(lambda e: e.scalar_tensor_tensor(g1[:, :], g_f[:, :], -1.0, g_f[:, :], ALU.mult, ALU.max), t_f)
    st_heads(0, 1)
    ahead()
    t = AC(lambda e: e.activation(g1[:, :], g1[:, :], ACT.Exp, scale=-1.0), t)
    t = AC(lambda e: e.activation(g2[:, :], g1[:, :], ACT.Ln, bias=1.0), t)
    t = DV(lambda e: e.scalar_tensor_tensor(g1[:, :], g_f[:, :], 0.0, g2[:, :], ALU.min, ALU.subtract), t)
    z0 = DV(lambda e: e.memset(g2[:, :], 1.0), t)
    t_B = DV(lambda e: e.tensor_tensor_scan(gB[:, :], g2[:, :], g1[:, :], 0.0, ALU.mult, ALU.add), t, z0)
    t_c = DV(lambda e: e.tensor_tensor(gi_i[:, :], gi_i[:, :], gB[:, :], ALU.subtract), t_B, t_i)
    z0 = DV(lambda e: e.memset(g1[:, :], 0.0), t_B)
    t_mm = DV(lambda e: e.tensor_tensor_scan(gmm[:, :], g1[:, :], gi_i[:, :], 0.0, ALU.add, ALU.max), t_c, z0)
    t = DV(lambda e: e.tensor_tensor(gng[:, :], gB[:, :], gmm[:, :], ALU.add), t_mm)
    st_heads(1, 0)
    ahead()
    t_ng = AC(lambda e: e.activation(gng[:, :], gng[:, :], ACT.Exp, scale=-1.0), t)
    st_heads(1, 1)
    ahead()

    def keep_block(dst, bank, bt, fn):
        res = []
        for j in range(2):
            res.append(AC(lambda e: e.activation(dst[:, j, :], ps[bank + j][:, :], fn), bt[j]))
            free[bank + j] = [res[j]]
        return res

    lg_t, l_t, a_t, sb_t, sn_t, e_t = {}, {}, {}, {}, {}, {}

    def st_logits(g):
        for n in range(4):
            hd = 4 * g + n
            tl, rp = hd // 2, slice(64 * (hd % 2), 64 * (hd % 2) + 64)
            for m, (s_, t_) in enumerate(((0, 0), (1, 1), (0, 1))):
                t = mm(ps[n][:, m * P:m * P + P], ks[rp, tl, s_ * P:s_ * P + P], qs[rp, tl, t_ * P:t_ * P + P], True, True,
                       sq_t[0, tl // 2], sq_t[1, tl // 2], free[n], sig=n == 3 and m == 2)
        lg_t[g] = t
        old = [a_t.get(g - 1), sb_t.get(g - 1)]
        z_ = AC(lambda e: e.activation(zs[:, :, :], banks[:, 0:4, 0:384], ACT.Copy), t, old)
        for n in range(4):
            free[n] = [z_]
        t = DV(lambda e: e.scalar_tensor_tensor(ze[:, :, :], zs[:, :, :], -1.0, zs[:, :, :], ALU.mult, ALU.max), z_, old)
        t = AC(lambda e: e.activation(ze[:, :, :], ze[:, :, :], ACT.Exp, scale=-1.0), t)
        t = AC(lambda e: e.activation(ze[:, :, :], ze[:, :, :], ACT.Ln, bias=1.0), t)
        t = DV(lambda e: e.scalar_tensor_tensor(ze[:, :, :], zs[:, :, :], 0.0, ze[:, :, :], ALU.max, ALU.add), t)
        keep, sneg = (const(n).unsqueeze(1).broadcast_to([P, 4, S]) for n in ("keep", "sneg"))
        t2 = DV(lambda e: e.tensor_tensor(ze[:, :, 0:S], ze[:, :, 0:S], keep, ALU.mult), t)
        l_t[g] = [t2, DV(lambda e: e.tensor_tensor(zs[:, :, 0:S], zs[:, :, 0:S], sneg, ALU.add), t)]

    def st_sums(g):
        for n in range(4):
            mm(ps[n][:, 0:384], const("tri"), ze[:, n, :], True, True, l_t[g], free[n])
            t = PE(lambda e: e.matmul(ps[n][:, S:384], const("ones"), ze[:, n, P:S], start=False, stop=True, skip_group_check=True), sig=n == 3)
        t2 = DV(lambda e: e.scalar_tensor_tensor(zs[:, :, :], banks[:, 0:4, 0:384], -1.0, zs[:, :, :], ALU.mult, ALU.add), t, l_t[g])
        for n in range(4):
            free[n] = [t2]
        a_t[g] = [t2, AC(lambda e: e.activation(ze[:, :, :], zs[:, :, :], ACT.Exp), t2, t)]

    def st_out(g):
        b = 6 + g
        for n in range(4):
            vc = slice(256 * g + 64 * n, 256 * g + 64 * n + 64)
            o0, o1 = ps[b][:, 64 * n:64 * n + 64], ps[b][:, 256 + 64 * n:256 + 64 * n + 64]
            mm(o0, ze[:, n, 0:P], vs[:, 0, vc], True, True, a_t[g], free[b], vs_t)
            mm(o1, ze[:, n, S:384], vs[:, 0, vc], True, False)
            t = mm(o1, ze[:, n, P:S], vs[:, 1, vc], False, True, sig=n == 3)
        sb_t[g] = t
        t1 = AC(lambda e: e.activation(sO[:, :, :], ps[b][:, :].rearrange("p (j d) -> p j d", j=2), ACT.Copy), t, e_t.get(2 + g - 1))
        free[b] = [t1]
        t = AC(lambda e: e.activation(sq[:, :, :], sO[:, :, :], ACT.Square), t1, sn_t.get(g - 1))
        s = s8[g]
        t = DV(lambda e: e.reduce_sum(s[:, 0, :], sq[:, :, :].rearrange("p j (n d) -> p (j n) d", d=64), AX), t)
        t = root(s[:, 1, :], s[:, 0, :], 1.0 / 64, 1, t)()
        sv = sO[:, :, :].rearrange("p j (n d) -> p (j n) d", d=64)
        t = DV(lambda e: e.tensor_tensor(sv, sv, s[:, 1, :].unsqueeze(2).broadcast_to([P, 8, 64]), ALU.mult), t)
        gr = hg[:, 512 + 256 * g:512 + 256 * g + 256].unsqueeze(1).broadcast_to([P, 2, 256])
        sn_t[g] = DV(lambda e: e.tensor_tensor(sO[:, :, :], sO[:, :, :], gr, ALU.mult), t, hg_t)

    def st_join(g):
        b, c = 6 + g, 2 + g
        for kk in range(2):
            for j in range(2):
                n = 2 * kk + j
                t = transpose(ps[b][:, n * P:n * P + P], sO[:, j, kk * P:kk * P + P], sn_t[g], free[b], sig=n == 3)
        e_t[c] = part(eH[:, 2 * c:2 * c + 2, :], eL[:, 2 * c:2 * c + 2, :], ps[b][:, :].rearrange("p (k t) -> p k t", k=2), t)
        free[b] = [e_t[c][1]]

    silu_t, qp_t = {}, {}

    def ml_conv(c, b, t):
        i = c % 2
        t0 = AC(lambda e: e.activation(qp[i][:, :, 3:S + 3], ps[b][:, :].rearrange("p (a t) -> p a t", a=2), ACT.Copy), t, qp_t.get(c - 2), pad_t)
        m = [AC(lambda e, q=q: e.activation(qm[:, 2 * c + q, :], ps[b][:, q * S:q * S + S], ACT.Identity,
                                            scale=ct[:, 4 * q + c, 3:4], bias=ct[:, 4 * q + c, 4:5]), t, c4_t, lg_t[1]) for q in range(2)]
        free[b] = m
        for w in (2, 1, 0):
            m = [DV(lambda e, q=q: e.scalar_tensor_tensor(qm[:, 2 * c + q, :], qp[i][:, q, w:S + w], ct[:, 4 * q + c, w:w + 1], qm[:, 2 * c + q, :],
                                                          ALU.mult, ALU.add), t0, m[q], c4_t, pad_t) for q in range(2)]
        qp_t[c] = m

    def ml_silu(c):
        silu_t[c] = AC(lambda e: e.activation(qm[:, 2 * c:2 * c + 2, :], qm[:, 2 * c:2 * c + 2, :], ACT.Silu), qp_t[c])

    munits = [(hd, j) for hd in range(4) for j in range(2)]
    pm_t, mx_t, pt_t, PT_t, rden, mn_t = {}, {}, {}, {}, {}, {}

    def ml_scores(u):
        hd, j = munits[u]
        b, i, nk = 4 + u % 2, u % 2, P * (j + 1)
        mm(ps[b][:, 0:nk], qm[:, 2 * hd, j * P:j * P + P], qm[:, 2 * hd + 1, 0:nk], True, True, silu_t[hd], free[b])
        t = mm(ps[b][:, S:S + nk], selt[:, hd, :], gi_i[:, 0:nk], True, True, t_c, gw_t, sig=True)
        w_ = DV(lambda e: e.tensor_tensor(Wt[i][:, 0:nk], ps[b][:, S:S + nk], const("cmask")[:, j * S:j * S + nk], ALU.add), t, pm_t.get(u - 2), gc_t, t_ng)
        w_ = AC(lambda e: e.activation(Wt[i][:, 0:nk], Wt[i][:, 0:nk], ACT.Exp, bias=gc[:, j, 0, hd:hd + 1]), w_, gc_t)
        w_ = DV(lambda e: e.scalar_tensor_tensor(Pm[i][:, 0:nk], ps[b][:, 0:nk], float(P) ** -0.5, Wt[i][:, 0:nk], ALU.mult, ALU.mult,
                                                 accum_out=dn[u % 4][:, 0:1]), w_, pt_t.get(u - 2), mx_t.get(u - 4))
        pm_t[u] = w_
        free[b] = [w_]
        t = DV(lambda e: e.scalar_tensor_tensor(dn[u % 4][:, 3:4], dn[u % 4][:, 0:1], -1.0, dn[u % 4][:, 0:1], ALU.mult, ALU.max), w_)
        t = DV(lambda e: e.tensor_scalar(dn[u % 4][:, 1:2], dn[u % 4][:, 3:4], gc[:, j, 1, hd:hd + 1], None, ALU.max), t, gc_t)
        rden[u] = DV(lambda e: e.reciprocal(dn[u % 4][:, 2:3], dn[u % 4][:, 1:2]), t)

    def ml_turn(u):
        j, i, b = u % 2, u % 2, 6 + u % 2
        for k in range(j + 1):
            t = transpose(ps[b][:, k * P:k * P + P], Pm[i][:, k * P:k * P + P], pm_t[u], free[b], sig=k == j)
        pt_t[u] = t
        PT_t[u] = AC(lambda e: e.activation(PT[i][:, 0:j + 1, :].rearrange("p a b -> p (a b)"), ps[b][:, 0:P * (j + 1)], ACT.Copy), t, mx_t.get(u - 2))

    def ml_out(u):
        hd, j = munits[u]
        i, b, g, n = u % 2, 6 + u % 2, u // 4, u % 4
        ov = ps[b][:, S:S + P]
        for k in range(j + 1):
            t = mm(ov, PT[i][:, k, :], vm[:, k, hd * P:hd * P + P], k == 0, k == j, PT_t[u], vm_t[k], sig=k == j)
        mx_t[u] = DV(lambda e: e.scalar_tensor_tensor(mO[g][:, n, :], ov, dn[u % 4][:, 2:3], og[:, j, hd * P:hd * P + P], ALU.mult, ALU.mult),
                     t, rden[u], og_t[j])
        free[b] = [mx_t[u]]
        junk_t[0] = AC(lambda e: e.activation(junk[:, 0:P], mO[g][:, n, :], ACT.Square, accum_out=s8[2 + g][:, 0, n:n + 1]), mx_t[u], junk_t[0])
        mn_t[u] = junk_t[0]

    def ml_norm(g):
        s = s8[2 + g]
        t = root(s[:, 1, 0:4], s[:, 0, 0:4], 1.0 / P, 1, [mn_t[u] for u in range(4 * g, 4 * g + 4)])()
        mn_t["on", g] = [DV(lambda e, n=n: e.scalar_tensor_tensor(mO[g][:, n, :], mO[g][:, n, :], s[:, 1, n:n + 1],
                                                                   hg[:, (2 * g + n // 2) * P:(2 * g + n // 2) * P + P], ALU.mult, ALU.mult),
                            t, hg_t) for n in range(4)]

    def ml_join(g, b):
        for n in range(4):
            t = transpose(ps[b][:, n * P:n * P + P], mO[g][:, n, :], mn_t["on", g], free[b], sig=n == 3)
        e_t[g] = part(eH[:, 2 * g:2 * g + 2, :], eL[:, 2 * g:2 * g + 2, :], ps[b][:, :].rearrange("p (k t) -> p k t", k=2), t)
        free[b] = [e_t[g][1]]

    st_logits(0)
    vs_t = keep_block(vs, 4, whole(blocks("win", 4, xH, xL, 4, xt)), ACT.Copy)
    ahead()
    gc_t = gates_turn()
    vmg = blocks("win", 6, xH, xL, 4, xt)
    next(vmg)
    st_sums(0)
    vm_t = keep_block(vm, 4, whole(vmg), ACT.Copy)
    ahead()
    st_out(0)
    st_logits(1)
    ml_conv(0, 4, whole(pair_cols("win", 8, 4, xH, xL, xt)))
    st_join(0)
    ml_conv(1, 5, whole(pair_cols("win", 9, 5, xH, xL, xt)))
    qm2 = pair_cols("win", 10, 4, xH, xL, xt)
    next(qm2)
    st_sums(1)
    ml_conv(2, 4, whole(qm2))
    ml_conv(3, 5, whole(pair_cols("win", 11, 5, xH, xL, xt)))
    wout_t = []

    og_t = []

    def ml_fill():
        og_t.extend(keep_block(og, 2, (yield from blocks("win", 12, xH, xL, 2, xt)), ACT.Sigmoid))
        yield
        wout_t.extend((yield from rows("wout", (2, 3, 0, 1), eH, eL, e_t)))

    fill = ml_fill()
    next(fill)
    next(fill)
    for c in range(4):
        ml_silu(c)
    st_out(1)
    for u in range(12):
        if 2 <= u < 10:
            ml_turn(u - 2)
        if u < 8:
            ml_scores(u)
        if 3 <= u < 11:
            ml_out(u - 3)
        if u in (7, 11):
            ml_norm(u // 4 - 1)
        if u == 9:
            ml_join(0, 6)
        for _ in range((1, 1, 0, 1, 0, 1, 1, 1, 0, 1, 0, 1)[u]):
            next(fill)
        if u == 1:
            st_join(1)
        if u == 11:
            ml_join(1, 6)
    gain_used("heads", [mn_t["on", 0], mn_t["on", 1], sn_t[0], sn_t[1]])
    for _ in fill:
        pass

    o = [OW]
    xn = sb("xn", [P, 2, D], off=o)
    xq = sb("xq", [P, KT, S], off=o)
    aH = sb("aH", [P, KT, S], F32R, off=o)
    aL = sb("aL", [P, KT, S], F32R, off=o)
    pr = [sb(f"pr{i}", [P, 2, S], off=o) for i in range(2)]
    pT = [sb(f"pT{i}", [P, 2, S], off=o) for i in range(2)]
    px = [sb(f"px{i}", [P, 3, 2], off=o) for i in range(2)]

    r_t, n_t = add_rms(wout_t, xn, "xattn", wout_t)
    qx_t, xp_t, pp_t, pT_t, ox_t, a_t, xo_t = {}, {}, {}, {}, {}, {}, []

    def x_query(c):
        t = first_q if c == 0 else (yield from pair_cols("xq", c, c, xH, xL, xt))
        qx_t[c] = AC(lambda e: e.activation(xq[:, 2 * c:2 * c + 2, :].rearrange("p a t -> p (a t)"), ps[c][:, :], ACT.Copy, scale=1.0 / 16), t, wout_t)
        free[c] = [qx_t[c]]

    def x_scores(hd):
        b, i = 4 + hd % 2, hd % 2
        for j in range(2):
            for k in range(2):
                t = mm(ps[b][:, j * S:j * S + S], xq[:, 2 * hd + k, j * P:j * P + P], xk[:, 2 * hd + k, :], k == 0, k == 1,
                       qx_t[hd], kx_t[hd], free[b], sig=j == 1 and k == 1)
        m = px[i]
        sv = ps[b][:, :].rearrange("p (j s) -> p j s", j=2)
        t = DV(lambda e: e.tensor_reduce(m[:, 0, :], sv, AX, ALU.max, negate=True), t, xp_t.get(hd - 2))
        ex = [AC(lambda e, j=j: e.activation(pr[i][:, j, :], sv[:, j, :], ACT.Exp, bias=m[:, 0, j:j + 1], accum_out=m[:, 1, j:j + 1]),
                 t, pp_t.get(hd - 2)) for j in range(2)]
        free[b] = ex
        t = DV(lambda e: e.reciprocal(m[:, 2, :], m[:, 1, :]), ex)
        xp_t[hd] = [DV(lambda e, j=j: e.tensor_scalar(pr[i][:, j, :], pr[i][:, j, :], m[:, 2, j:j + 1], None, ALU.mult), t) for j in range(2)]

    def x_turn(hd):
        i = hd % 2
        for k in range(2):
            for j in range(2):
                t = transpose(ps[6][:, (2 * k + j) * P:(2 * k + j) * P + P], pr[i][:, j, k * P:k * P + P], xp_t[hd], free[6], sig=k == 1 and j == 1)
        pp_t[hd] = t
        pT_t[hd] = AC(lambda e: e.activation(pT[i][:, :, :].rearrange("p k t -> p (k t)"), ps[6][:, :], ACT.Copy), t, ox_t.get(hd - 2))
        free[6] = [pT_t[hd]]

    def x_out(hd):
        for q in range(2):
            for k in range(2):
                t = mm(ps[7][:, q * S:q * S + S], xv[:, k, (2 * hd + q) * P:(2 * hd + q) * P + P], pT[hd % 2][:, k, :], k == 0, k == 1,
                       pT_t[hd], v_t, free[7], sig=q == 1 and k == 1)
        ox_t[hd] = t
        a_t[hd] = part(aH[:, 2 * hd:2 * hd + 2, :], aL[:, 2 * hd:2 * hd + 2, :], ps[7][:, :].rearrange("p (k t) -> p k t", k=2), t)
        free[7] = [a_t[hd][1]]

    def x_fill():
        for c in (2, 3):
            yield from x_query(c)
            yield
        xo_t.extend((yield from rows("xo", range(4), aH, aL, a_t)))

    fill = x_fill()
    first_q, xt = turn_cols("xq", 0, xn, n_t, xH, xL)
    whole(x_query(0))
    whole(x_query(1))
    for hd in range(5):
        if hd < 4:
            x_scores(hd)
        if hd >= 1:
            x_turn(hd - 1)
        next(fill)
        if hd < 4:
            next(fill)
        if hd >= 1:
            x_out(hd - 1)
    warm(ACT.Sqrt)
    for _ in fill:
        pass
    o = [OW - 16384]
    pn = sb("pn", [P, 2, D], off=o)
    qH = sb("qH", [P, 16, S], F32R, off=o)
    qL = sb("qL", [P, 16, S], F32R, off=o)
    r_t, n_t = add_rms(xo_t, pn, "ffn", xo_t)
    q_t = []
    for c in range(8):
        b = 4 + c % 4
        if c == 0:
            t, xt = turn_cols("pq", b, pn, n_t, xH, xL)
        else:
            t = whole(pair_cols("pq", c, b, xH, xL, xt))
        r = part(qH[:, 2 * c:2 * c + 2, :].rearrange("p a t -> p (a t)"), qL[:, 2 * c:2 * c + 2, :].rearrange("p a t -> p (a t)"),
                 ps[b][:, :], t)
        free[b] = [r[1]]
        q_t += r

    o = [OX]
    uH = [sb(f"uH{i}", [P, UW], F32R, off=o) for i in range(US)]
    uL = [sb(f"uL{i}", [P, UW], F32R, off=o) for i in range(US)]
    OG = o[0]
    oB = [sb(f"oB{i}", [P, P, GB], BF16, off=o) for i in range(2)]
    oE = [sb(f"oE{i}", [P, P, GB], BF16, off=o) for i in range(2)]
    oA = [[sb(f"oA{n}{i}", [P, P, GB], BF16, off=o) for i in range(3)] for n in range(2)]
    i1T = sb("i1T", [P, S], BF16, off=o)
    i2T = sb("i2T", [P, S], BF16, off=o)
    gT = sb("gT", [P, S], off=o)
    gp = [sb(f"gp{i}", [P, S], BF16, off=o) for i in range(3)]
    assert o[0] >= OG + 8192
    st = [sb(f"st{i}", [P, S], off=o) for i in range(4)]
    iob = sb("iob", [P, P, GB], BF16, off=o)
    GO = o[0]
    G = sb("G", [P, 2, P, P], off=o)
    assert OW + 8192 >= GO + 65536
    o = [OW - 16384 + 8192 + 32768]
    sc = sb("sc", [P, 2, 16, P], off=o)
    wk = [sb(f"wk{i}", [P, S], off=o) for i in range(4)]
    ti = sb("ti", [P, 16, 16], U32, off=o)
    tf = sb("tf", [P, 16, 16], off=o)
    tv = sb("tv", [P, 16, 16], off=o)
    bv = sb("bv", [P, 8, 16], off=o)
    bp = sb("bp", [P, 8, 16], U32, off=o)
    bq = [sb(f"bq{i}", [P, 8, 16], U32, off=o) for i in range(2)]
    bf = [sb(f"bf{i}", [P, 8, 16], off=o) for i in range(2)]
    ei = [sb(f"ei{i}", [P, 8, 16], off=o) for i in range(2)]
    gs = sb("gs", [P, 8, 2], off=o)
    eq = sb("eq", [P, P, 16], off=o)
    cand = sb("cand", [P, 8, S], off=[OW + 8192])

    idx, wh, wl, wt = take("sk", 0)
    last_chunk = len(STREAM) - 1
    u_raw = [sem(f"s_u{i}") for i in range(UR)]
    ua, ub, udone, u_t = {}, {}, {}, {}

    def ufetch(n):
        if n >= 2 * P:
            return
        k = n % UR
        if n < UR:
            c = max(m for m in range(len(STREAM)) if m % NR == k // 2)
            dep = [split_a[c], split_v[c]]
        else:
            dep = [ua[n - UR], ub[n - UR]]
        src = a["eu"][n] if n < P else a["ev"][n - P]
        u_t[n] = SP.dma(lambda e: e.dma_start(raw[k // 2][:, (k % 2) * UW:(k % 2) * UW + UW], src), u_raw[k], 16 * (n // UR + 1), dep)

    def usplit(n):
        if n >= 2 * P:
            return
        k, s_ = n % UR, n % US
        src = raw[k // 2][:, (k % 2) * UW:(k % 2) * UW + UW]
        dep = udone[n - US] if n >= US else [split_a[last_chunk], split_v[last_chunk], done[last_chunk - 1], done[last_chunk - 2], n_t]
        ua[n] = AC(lambda e: e.activation(uH[s_][:, :], src, ACT.Copy), u_t[n], dep)
        lane = GP if n < P and n % 2 == 0 else DV
        ub[n] = lane(lambda e: e.tensor_tensor(uL[s_][:, :], src, uH[s_][:, :].bitcast(F32), ALU.subtract), ua[n], u_t[n], dep)
        ufetch(n + UR)

    for n in range(UR):
        ufetch(n)

    for n in range(US - 1):
        usplit(n)

    sc_t = {}

    def sub_scores(j, q):
        b = q
        for i in range(4):
            hp = 4 * q + i
            ov = ps[b][:, i * P:i * P + P]
            ts = slice(j * P, j * P + P)
            kc = slice(hp * P, hp * P + P)
            mm(ov, qH[:, hp, ts], wh[:, kc], True, False, wt, q_t, free[b])
            mm(ov, qH[:, hp, ts], wl[:, kc], False, False)
            t = mm(ov, qL[:, hp, ts], wh[:, kc], False, True, sig=i == 3)
        sc_t[j, q] = AC(lambda e: e.activation(sc[:, j, 4 * q:4 * q + 4, :].rearrange("p a b -> p (a b)"), ps[b][:, :], ACT.Copy), t)
        free[b] = [sc_t[j, q]]
        done[last_chunk] = t

    h_t = SP.dma(lambda e: e.dma_start(hs, h[:, :, :]), s_hs, 16, r_t)
    iob_t = GP(lambda e: e.iota(iob[:, :, :].rearrange("p i t -> p (i t)"), [[1, P], [0, GB]], base=0, channel_multiplier=0,
                                allow_small_or_imprecise_dtypes=True), done[last_chunk - 1], done[last_chunk - 2], n_t)

    sel_t, ev_t = [], []
    NEG = -3.0e38

    def top16(row, w_, vals, inds, dep):
        n = len(row)
        t = [DV(lambda e: e.max(vals[k][:, 0:8], row[k]), dep[k]) for k in range(n)]
        yield
        for k in range(n):
            DV(lambda e: e.max_index(inds[k][:, 0:8], vals[k][:, 0:8], row[k]), t[k])
        yield
        t = [DV(lambda e: e.match_replace(w_[k], vals[k][:, 0:8], row[k], NEG), t[k]) for k in range(n)]
        yield
        t = [DV(lambda e: e.max(vals[k][:, 8:16], w_[k]), t[k]) for k in range(n)]
        yield
        top_t[:] = [DV(lambda e: e.max_index(inds[k][:, 8:16], vals[k][:, 8:16], w_[k]), t[k]) for k in range(n)]
        yield

    top_t = []

    def pause(j):
        for _ in range(PAUSE[j]):
            yield

    def route():
        prev = None
        for j in range(2):
            tops = []
            for q in range(4):
                r = range(4 * q, 4 * q + 4)
                yield from top16([sc[:, j, x, :] for x in r], [wk[x % 4][:, 0:P] for x in r], [tv[:, x, :] for x in r],
                                 [ti[:, x, :] for x in r], [[sc_t[j, q], prev, ev_t]] * 4)
                tops += top_t
            tf_t = DV(lambda e: e.tensor_copy(tf[:, :, :], ti[:, :, :]), tops)
            s1 = tv[:, :, :].rearrange("p (h c) k -> p h c k", c=2)
            cv = cand[:, :, :].rearrange("p h (a b) -> p h a b", a=16)
            c_t = []
            for hd in range(8):
                c_t.append(DV(lambda e: e.tensor_tensor(cv[:, hd, :, :], s1[:, hd, 0, :].unsqueeze(2).broadcast_to([P, 16, 16]),
                                                        s1[:, hd, 1, :].unsqueeze(1).broadcast_to([P, 16, 16]), ALU.add), tops, sc_t[1, 3]))
                if hd % 2:
                    yield
            tops = []
            for q in range(2):
                r = range(4 * q, 4 * q + 4)
                yield from top16([cand[:, x, :] for x in r], [wk[x % 4][:, :] for x in r], [bv[:, x, :] for x in r],
                                 [bp[:, x, :] for x in r], [[c_t[x], prev] for x in r])
                tops += top_t
            t = DV(lambda e: e.tensor_tensor(ei[0][:, :, :], bv[:, :, :], bv[:, :, 0:1].broadcast_to([P, 8, 16]), ALU.subtract), tops)
            t = AC(lambda e: e.activation(ei[0][:, :, :], ei[0][:, :, :], ACT.Exp), t)
            t = DV(lambda e: e.reduce_sum(gs[:, :, 0], ei[0][:, :, :], AX), t)
            t = DV(lambda e: e.reciprocal(gs[:, :, 1], gs[:, :, 0]), t)
            g_t = DV(lambda e: e.tensor_tensor(bv[:, :, :], ei[0][:, :, :], gs[:, :, 1:2].broadcast_to([P, 8, 16]), ALU.mult), t)
            yield
            u0 = DV(lambda e: e.tensor_scalar(bq[0][:, :, :], bp[:, :, :], 4, None, ALU.logical_shift_right), tops)
            u1 = DV(lambda e: e.tensor_scalar(bq[1][:, :, :], bp[:, :, :], 15, None, ALU.bitwise_and), tops)
            f_t = [DV(lambda e: e.tensor_copy(bf[i][:, :, :], bq[i][:, :, :]), u0, u1) for i in range(2)]
            yield
            e_t = []
            tfv = tf[:, :, :].rearrange("p (h c) k -> p h c k", c=2)
            for i in range(2):
                t = DV(lambda e: e.tensor_tensor(eq[:, :, :], bf[i][:, :, :].rearrange("p a b -> p (a b)").unsqueeze(2).broadcast_to([P, P, 16]),
                                                 iota[:, 0:16].unsqueeze(1).broadcast_to([P, P, 16]), ALU.is_equal), f_t[i], e_t[-1:], iota_t)
                yield from pause(j)
                ev = eq[:, :, :].rearrange("p (h k) a -> p h k a", h=8)
                t = DV(lambda e: e.tensor_tensor(ev, ev, tfv[:, :, i, :].unsqueeze(2).broadcast_to([P, 8, 16, 16]), ALU.mult), t, tf_t)
                yield from pause(j)
                e_t.append(DV(lambda e: e.reduce_sum(ei[i][:, :, :].rearrange("p a b -> p (a b)"), eq[:, :, :], AX), t, g_t))
                yield from pause(j)
            prev = (yield (e_t[0], e_t[1], g_t))

    def picks_turn(j, toks):
        b = j
        for i, src in enumerate((ei[0], ei[1], bv)):
            t = transpose(ps[b][:, i * P:i * P + P], src[:, :, :].rearrange("p a b -> p (a b)"), toks[i], free[b], sig=i == 2)
        ev_t.append(t)
        return t

    def picks_keep(j, t):
        b = j
        tj = slice(j * P, j * P + P)
        c1 = DV(lambda e: e.tensor_copy(i1T[:, tj], ps[b][:, 0:P]), t, n_t)
        c2 = DV(lambda e: e.tensor_copy(i2T[:, tj], ps[b][:, P:2 * P]), t)
        g0 = DV(lambda e: e.tensor_copy(gT[:, tj], ps[b][:, 2 * P:3 * P]), t)
        free[b] = [g0]
        c = g0
        for i in range(3):
            c = DV(lambda e: e.tensor_copy(gp[i][:, tj], gT[:, tj]), c)
            if i < 2:
                c = DV(lambda e: e.tensor_tensor(gT[:, tj], gT[:, tj], gp[i][:, tj], ALU.subtract), c)
        sel_t.append([c1, c2, c])

    NB = S // GB
    hot_t, ab_t, G_t = {}, {}, []

    def hots(bt):
        sel_, n = sel_t[bt * GB // P], bt % 2
        tt = slice(GB * bt, GB * bt + GB)

        def wide(x):
            return x[:, tt].unsqueeze(1).broadcast_to([P, P, GB])

        te = DV(lambda e: e.tensor_tensor(oE[n][:, :, :], iob[:, :, :], wide(i1T), ALU.is_equal), sel_, iob_t, ab_t.get(bt - 2))
        tb = DV(lambda e: e.tensor_tensor(oB[n][:, :, :], iob[:, :, :], wide(i2T), ALU.is_equal), sel_)
        ta = [DV(lambda e: e.tensor_tensor(oA[n][i][:, :, :], oE[n][:, :, :], wide(gp[i]), ALU.mult), te) for i in range(3)]
        hot_t[bt] = [tb, ta]

    def gates(bt):
        n, b = bt % 2, 6 + bt % 2
        for m in range(GB):
            for i in range(3):
                t = mm(ps[b][:, m * P:m * P + P], oB[n][:, :, m], oA[n][i][:, :, m], i == 0, i == 2, hot_t[bt], free[b],
                       sig=i == 2 and m == GB - 1)
        ab_t[bt] = t
        j, t0 = divmod(bt * GB, P)
        G_t.append(AC(lambda e: e.activation(G[:, j, :, t0:t0 + GB], ps[b][:, 0:GB * P].rearrange("p (t i) -> p i t", t=GB), ACT.Copy),
                      t, sel_t, h_t, n_t))
        free[b] = [G_t[-1]]

    s_st = [sem(f"s_st{i}") for i in range(4)]
    st_t = {}

    def ex_in(i):
        b = 4 + i % 2
        ov = ps[b][:, 0:S]
        w_h, w_l, wt = uH[i % US], uL[i % US], [ua[i], ub[i]]
        for k in range(KT):
            kc = slice(k * P, k * P + P)
            mm(ov, w_h[:, kc], xH[:, k, :], k == 0, False, wt, free[b], xt)
            mm(ov, w_h[:, kc], xL[:, k, :], False, False)
            t = mm(ov, w_l[:, kc], xH[:, k, :], False, k == KT - 1, sig=k == KT - 1)
        udone[i] = t
        t = AC(lambda e: e.activation(st[i % 4][:, :], ov, ACT.Gelu), t, st_t.get(i - 4), n_t)
        free[b] = [t]
        st_t[i] = SP.dma(lambda e: e.dma_start(gel[i], st[i % 4][:, :]), s_st[i % 4], 16 * (i // 4 + 1), t)

    o = [OG]
    ga = [sb(f"ga{i}", [P, S], off=o) for i in range(NA)]
    gH = [sb(f"gH{i}", [P, S], F32R, off=o) for i in range(NA)]
    gL = [sb(f"gL{i}", [P, S], F32R, off=o) for i in range(NA)]
    assert o[0] <= OG + 10 * P * GB * 2
    s_rb = [sem(f"s_rb{i}") for i in range(4)]
    rb_t, m_t, act_t = {}, {}, {}

    def ex_load(i):
        if i < P:
            rb_t[i] = SP.dma(lambda e: e.dma_start(st[i % 4][:, :], gel[i]), s_rb[i % 4], 16 * (i // 4 + 1),
                             st_t[i], st_t[P - 4 + i % 4], m_t.get(i - 4))

    def ex_gate(i):
        if i >= P:
            return
        ab = list(ab_t.values()) if i < NA else None
        m_t[i] = GP(lambda e: e.tensor_tensor(ga[i % NA][:, :].rearrange("p (j t) -> p j t", j=2),
                                                  st[i % 4][:, :].rearrange("p (j t) -> p j t", j=2), G[:, :, i, :], ALU.mult), rb_t[i], G_t, act_t.get(i - NA), ab)
        ex_load(i + 4)

    def ex_act(i):
        if i >= P:
            return
        y3 = udone[P + i - NA] if i >= NA else list(ab_t.values())
        t1 = AC(lambda e: e.activation(gH[i % NA][:, :], ga[i % NA][:, :], ACT.Copy), m_t[i], y3)
        t2 = DV(lambda e: e.tensor_tensor(gL[i % NA][:, :], ga[i % NA][:, :], gH[i % NA][:, :].bitcast(F32), ALU.subtract), t1, m_t[i], y3)
        act_t[i] = [t1, t2]

    def ex_out(i):
        n = P + i
        w_h, w_l, wt = uH[n % US], uL[n % US], [ua[n], ub[n]]
        for t in range(2):
            ts = slice(t * P, t * P + P)
            for part_, (l, w) in enumerate(((gH, w_h), (gH, w_l), (gL, w_h))):
                for e2 in range(2):
                    b = 2 * t + e2
                    last = i == P - 1 and part_ == 2
                    tok = mm(ps[b][:, :], l[i % NA][:, ts], w[:, e2 * 512:e2 * 512 + 512], i == 0 and part_ == 0, last,
                             act_t[i], wt, free[b] if i == 0 else None, sig=last or (t == 1 and part_ == 2 and e2 == 1))
                    if last:
                        free[b] = [tok]
        udone[n] = tok

    work, found, turned_t, pend = route(), None, None, None
    nh = ng = 0
    waited = False
    for i in range(P):
        usplit(i + US - 1)
        if i < 8:
            sub_scores(i // 4, i % 4)
        if ng < nh - 1 or nh == NB > ng:
            gates(ng)
            ng += 1
        if i == P - 1:
            assert ng == NB
            ex_gate(0)
            ex_act(0)
        ex_in(i)
        if i >= P - 3:
            ex_load(i - P + 3)
        if turned_t is not None:
            picks_keep(len(sel_t), turned_t)
            turned_t = None
        if found is not None and waited:
            turned_t = pend = picks_turn(len(sel_t), found)
            found = None
        waited = found is not None
        for _ in range(1 if sel_t or i % 2 else 2):
            if work is not None and found is None:
                found = work.send(pend)
                pend = None
                if found is not None and len(sel_t) == 1:
                    work = None
        if nh < len(sel_t) * NB // 2 and (work is None or i % 2 == 0):
            hots(nh)
            nh += 1

    ex_load(3)
    ex_gate(1)
    ex_gate(2)
    ex_act(1)
    for i in range(P):
        usplit(P + i + US - 1)
        ex_act(i + 2)
        ex_out(i)
        ex_gate(i + 3)
        if i == 8:
            warm(ACT.Sqrt)

    o = [GO]
    hb = sb("hb", [P, 2, D], off=o)
    pn = sb("pnl", [P, 2, D], off=o)
    gl = sb("gl", [P, D], off=o)
    b_t = SP.dma(lambda e: e.dma_start(hb[:, :, :], hs), s_hs, 32, h_t, m_t[P - 1])
    gl_t = SP.dma(lambda e: e.dma_start(gl[:, :], a["gains"][len(GAINS):len(GAINS) + 1, :].broadcast_to([P, D])), s_gl, 16, m_t[P - 1])
    for j in range(2):
        t = []
        for e2 in range(2):
            k = 2 * j + e2
            hv = hb[:, j, e2 * 512:e2 * 512 + 512]
            t.append(DV(lambda e: e.tensor_tensor(hv, hv, ps[k][:, :], ALU.add), free[k], b_t))
        t = AC(lambda e: e.activation(pn[:, j, :], hb[:, j, :], ACT.Square, accum_out=rs[:, j, 0:1]), t, m_t[P - 1])
        t = root(rs[:, j, 1:2], rs[:, j, 0:1], 1.0 / D, 1, t)()
        t = DV(lambda e: e.scalar_tensor_tensor(pn[:, j, :], hb[:, j, :], rs[:, j, 1:2], gl[:, :], ALU.mult, ALU.mult), t, gl_t)
        SP.dma(lambda e: e.dma_start(out[j], pn[:, j, :]), s_out, 16 * (j + 1), t)
    SP.wait((s_out, 32))
    assert nuse[0] == len(STREAM)


def constants():
    c = np.zeros((P, CWID), np.float32)
    pos = np.arange(S, dtype=np.float32)
    inv = (np.float32(500000.0) ** (-np.arange(0, 16, 2, dtype=np.float32) / np.float32(16))).astype(np.float32)
    ang = pos[:, None] * inv[None, :]
    p, f = np.arange(P)[:, None], np.arange(S)[None, :]
    for j in range(2):
        for name, fn in (("cos", np.cos), ("sin", np.sin)):
            c0 = CC[name][0] + j * P
            c[:, c0:c0 + P] = np.tile(fn(ang[j * P:j * P + P]).astype(np.float32), (1, 16))
        c0 = CC["amask"][0] + j * S
        c[:, c0:c0 + S] = np.where(f // 64 <= (j * P + p) // 64, 0.0, -1e30)
        c0 = CC["cmask"][0] + j * S
        c[:, c0:c0 + S] = np.where(f <= j * P + p, 0.0, -1e30)
        g = np.arange(P)[None, :]
        c0 = CC["keep"][0] + j * P
        c[:, c0:c0 + P] = np.where(p < g, 1.0, 0.0)
        c0 = CC["sneg"][0] + j * P
        c[:, c0:c0 + P] = np.where(p < g, 0.0, -1e30)
    c0 = CC["tri"][0]
    c[:, c0:c0 + P] = np.where(p >= np.arange(P)[None, :], 1.0, 0.0)
    c0 = CC["ones"][0]
    c[:, c0:c0 + P] = 1.0
    sel = np.zeros((4, 4, P), np.float32)
    for k in range(4):
        sel[k, k, :] = 1.0
    return {"consts": c, "ident": np.eye(P, dtype=np.float32),
            "iota": np.tile(np.arange(P, dtype=np.float32)[None, :], (P, 1)), "sel": sel}


def layout(v):
    def side(w, n):
        e = w.shape[1] // n
        return w.reshape(KT, P, e, n).transpose(2, 1, 0, 3).reshape(e, P, KT * n)

    def deep(w, kk):
        c = w.shape[0] // (P * kk)
        return w.reshape(c, kk, P, w.shape[1]).transpose(0, 2, 1, 3).reshape(c, P, kk * w.shape[1])

    def block(w):
        b = w.shape[1] // 512
        return w.reshape(2, 4, P, b, 512).transpose(3, 0, 2, 1, 4).reshape(2 * b, P, CW)

    def pair(x, y):
        return np.stack([x.reshape(D, -1, P), y.reshape(D, -1, P)], 2).reshape(D, -1)

    def rows2(x):
        return x.reshape(2, P, D).transpose(1, 0, 2)

    out = constants()
    out["x"] = rows2(v["x"][0])
    out["mem"] = rows2(v["mem_2"][0])
    out["qkv"] = block(v["attn_w_qkv"][0])
    out["wo"] = deep(v["attn_w_o"][0], 2)
    for i in range(2):
        out[f"gu{i}"] = side(pair(v["ffn_w_gate"][i], v["ffn_w_up"][i]), 256)
        out[f"dn{i}"] = deep(v["ffn_w_down"][i], 2)
    ci = v["conv_w_in"][0]
    out["cin"] = np.concatenate([side(pair(ci[:, D:2 * D], ci[:, 2 * D:]), 256), side(ci[:, :D], 256)])
    out["cout"] = deep(v["conv_w_out"][0], 2)
    wi = v["w_in_2"][0]
    out["win"] = np.concatenate([side(wi[:, 2056:2568], 256), side(wi[:, 2568:3080], 256), block(wi[:, 3080:3592]),
                                 block(wi[:, 1024:1536]), side(pair(wi[:, :512], wi[:, 512:1024]), 256), block(wi[:, 1536:2048])])
    out["gatew"] = wi[:, 2048:2056].reshape(KT, P, 8).transpose(1, 0, 2)
    out["gateb"] = np.stack([v["igate_b_2"][0], v["fgate_b_2"][0]], 1)
    out["wout"] = deep(v["w_out_2"][0], 2)
    out["xk"] = side(v["xattn_wkv_2"][0][:, :D], 256)
    out["xv"] = side(v["xattn_wkv_2"][0][:, D:], 256)
    out["xq"] = side(v["xattn_wq_2"][0], 256)
    out["xo"] = deep(v["xattn_wo_2"][0], 2)
    out["pq"] = side(v["peer_wq_2"][0], 256)
    out["sk"] = v["peer_subkeys_2"][0].reshape(16, P, P).transpose(2, 0, 1).reshape(1, P, CW)
    u = v["peer_u_2"][0].reshape(P, P, KT, P).transpose(0, 3, 2, 1).reshape(P, P, D)
    out["eu"] = u
    out["ev"] = v["peer_v_2"][0].reshape(P, P, D)
    out["convw"] = v["conv_w"][0].reshape(3, KT, P).transpose(2, 1, 0)
    c4 = np.concatenate([v["conv_w_2"][0], v["conv_b_2"]], 0)
    out["conv4"] = c4.reshape(5, 8, P).transpose(2, 1, 0)
    out["lam"] = np.concatenate([v["attn_lambda_q1"], v["attn_lambda_q2"], v["attn_lambda_k1"], v["attn_lambda_k2"]], 1)
    out["subg"] = v["attn_subln_g"]
    rows = {"ln1g0": v["ln1_g"][0], "ln1b0": v["ln1_b"][0], "ln2g0": v["ln2_g"][0], "ln2b0": v["ln2_b"][0],
            "ln1g1": v["ln1_g"][1], "ln1b1": v["ln1_b"][1], "ln2g1": v["ln2_g"][1], "ln2b1": v["ln2_b"][1],
            "mem": v["mem_norm_g_2"][0], "mix": v["mix_norm_g_2"][0],
            "heads": np.concatenate([v["mlstm_norm_g_2"][0], v["sb_norm_g_2"][0]]),
            "xattn": v["xattn_norm_g_2"][0], "ffn": v["ffn_norm_g_2"][0], "final": v["final_norm_g_2"]}
    out["gains"] = np.stack([rows[n] for n in GAINS + ["final"]])
    return {k: np.ascontiguousarray(x) for k, x in out.items()}


def kernel(**inputs):
    from contextlib import ExitStack

    import concourse.bacc as bacc
    from concourse.bass_utils import run_bass_kernel_spmd

    nc = bacc.Bacc("TRN2", target_bir_lowering=False, num_devices=1)
    arrays = layout({k: np.asarray(x) for k, x in inputs.items()})
    aps = {k: nc.dram_tensor("in_" + k, list(x.shape), F32, kind="ExternalInput").ap() for k, x in arrays.items()}
    out = nc.dram_tensor("out_0", [2, P, D], F32, kind="ExternalOutput").ap()
    with ExitStack() as ctx:
        build(nc, aps, out, ctx)
    r = run_bass_kernel_spmd(nc, [{"in_" + k: x for k, x in arrays.items()}], core_ids=[0])
    return np.asarray(r.results[0]["out_0"]).reshape(1, S, D)
```
